# Optimizing a Trainium2 kernel written in Bass

```python
import math
import jax
import jax.numpy as jnp
from jax import lax
import numpy as np

D_MODEL = 1024
BATCH = 1
SEQ = 256
DEPTH = 2

N_EVEN = (DEPTH + 1) // 2
N_ODD = DEPTH // 2

D_HYENA = D_MODEL // 2
HYENA_ORDER = 2
SHORT_CONV = 3
FILTER_EMB = 33
FILTER_ORDER = 64
DECAY_FAST_PCT = 0.3
DECAY_SLOW_PCT = 1.5
DECAY_TARGET = 1e-2

HEAD_DIM = 64
N_Q_HEADS = (D_MODEL - D_HYENA) // HEAD_DIM
N_KV_HEADS = 2
WINDOW = 128
BLOCK = 128
D_IN0 = (HYENA_ORDER + 1) * D_HYENA + (N_Q_HEADS + 2 * N_KV_HEADS) * HEAD_DIM

RWKV_HEAD = 64
RWKV_HEADS = D_MODEL // RWKV_HEAD
LORA_W = 64
LORA_A = 64
LORA_G = 160
GN_EPS = 64e-5

D_FF = 2816
NORM_EPS = 1e-6

kernel_name = 'hybrid_hyena_swa_rwkv7_macaron_encoder'

def rms_norm(x, g, eps=NORM_EPS):
    xf = x.astype(jnp.float32)
    y = xf * lax.rsqrt(jnp.mean(xf * xf, axis=-1, keepdims=True) + eps)
    return (y * g.astype(jnp.float32)).astype(x.dtype)

def swiglu(x, w_gate, w_up, w_down):
    return (jax.nn.silu(x @ w_gate) * (x @ w_up)) @ w_down

def alibi_slopes(n_heads):
    return 2.0 ** (-8.0 * jnp.arange(1, n_heads + 1, dtype=jnp.float32) / n_heads)

def hyena_filter(L, f1_w, f1_b, f2_w, f2_b, f3_w, f3_b, f4_w, sin_freq):
    f32 = jnp.float32
    pos = jnp.arange(L, dtype=f32)
    t = pos / max(L - 1, 1)
    bands = (FILTER_EMB - 1) // 2
    freqs = jnp.linspace(1e-4, bands - 1, bands, dtype=f32)
    ang = (2.0 * math.pi / L) * pos[:, None] * freqs[None, :]
    z = jnp.concatenate([t[:, None], jnp.cos(ang), -jnp.sin(ang)], axis=-1)
    freq = sin_freq.astype(f32)
    hf = jnp.sin(freq * (z @ f1_w.astype(f32) + f1_b.astype(f32)))
    hf = jnp.sin(freq * (hf @ f2_w.astype(f32) + f2_b.astype(f32)))
    hf = jnp.sin(freq * (hf @ f3_w.astype(f32) + f3_b.astype(f32)))
    hf = hf @ f4_w.astype(f32)
    deltas = jnp.abs(jnp.linspace(math.log(DECAY_TARGET) / DECAY_SLOW_PCT,
                                  math.log(DECAY_TARGET) / DECAY_FAST_PCT, D_HYENA, dtype=f32))
    window = jnp.exp(-t[:, None] * deltas[None, :])
    h_f = hf[:, :D_HYENA] * window
    h_b = hf[:, D_HYENA:] * window
    filt = jnp.concatenate([h_f[:1] + h_b[:1], h_f[1:], jnp.zeros((1, D_HYENA), f32), h_b[:0:-1]], axis=0)
    return filt / jnp.sum(jnp.abs(filt), axis=0, keepdims=True)

def hyena_mixer(u, conv_w, conv_b, f1_w, f1_b, f2_w, f2_b, f3_w, f3_b, f4_w, sin_freq, hy_bias):
    B, L, _ = u.shape
    up = jnp.pad(u, ((0, 0), (1, 1), (0, 0)))
    uc = up[:, :-2] * conv_w[0] + up[:, 1:-1] * conv_w[1] + up[:, 2:] * conv_w[2] + conv_b
    x0, x1, v = jnp.split(uc, HYENA_ORDER + 1, axis=-1)
    z = (v * x1).astype(jnp.float32)
    filt = hyena_filter(L, f1_w, f1_b, f2_w, f2_b, f3_w, f3_b, f4_w, sin_freq)
    n = 2 * L
    conv = jnp.fft.irfft(jnp.fft.rfft(z, n=n, axis=1) * jnp.fft.rfft(filt, n=n, axis=0)[None], n=n, axis=1)[:, :L]
    y = conv + z * hy_bias.astype(jnp.float32)
    return y.astype(u.dtype) * x0

def windowed_gqa(q, k, v, q_gain, k_gain, sink):
    f32 = jnp.float32
    B, L, Hq, D = q.shape
    G = Hq // N_KV_HEADS
    nb = L // BLOCK
    q = rms_norm(q, q_gain)
    k = rms_norm(k, k_gain)
    qb = q.reshape(B, nb, BLOCK, N_KV_HEADS, G, D)

    def band(t):
        tp = jnp.pad(t, ((0, 0), (BLOCK, BLOCK), (0, 0), (0, 0))).reshape(B, nb + 2, BLOCK, N_KV_HEADS, D)
        return jnp.concatenate([tp[:, :-2], tp[:, 1:-1], tp[:, 2:]], axis=2)

    kb, vb = band(k), band(v)
    s = jnp.einsum('bnqhgd,bnshd->bnhgqs', qb, kb).astype(f32) * (D ** -0.5)
    kpos = jnp.arange(3 * BLOCK) - BLOCK
    dist = jnp.arange(BLOCK)[:, None] - kpos[None, :]
    key_abs = jnp.arange(nb)[:, None] * BLOCK + kpos[None, :]
    valid = (jnp.abs(dist) <= WINDOW)[None] & ((key_abs >= 0) & (key_abs < L))[:, None, :]
    slopes = alibi_slopes(Hq).reshape(N_KV_HEADS, G)
    s = s - slopes[:, :, None, None] * jnp.abs(dist).astype(f32)
    s = jnp.where(valid[None, :, None, None], s, -1e30)
    sink_l = sink.astype(f32).reshape(N_KV_HEADS, G)[None, None, :, :, None, None]
    m = jnp.maximum(jnp.max(s, axis=-1, keepdims=True), sink_l)
    p = jnp.exp(s - m)
    p = p / (jnp.sum(p, axis=-1, keepdims=True) + jnp.exp(sink_l - m))
    o = jnp.einsum('bnhgqs,bnshd->bnqhgd', p.astype(vb.dtype), vb)
    return o.reshape(B, L, Hq * D)

def hyena_attention_mixer(h, w_in, conv_w, conv_b, f1_w, f1_b, f2_w, f2_b, f3_w, f3_b, f4_w,
                          sin_freq, hy_bias, q_gain, k_gain, sink, w_out):
    B, L, _ = h.shape
    u = h @ w_in
    n_hy = (HYENA_ORDER + 1) * D_HYENA
    n_q = N_Q_HEADS * HEAD_DIM
    n_kv = N_KV_HEADS * HEAD_DIM
    u_hy, q, k, v = jnp.split(u, [n_hy, n_hy + n_q, n_hy + n_q + n_kv], axis=-1)
    y_hy = hyena_mixer(u_hy, conv_w, conv_b, f1_w, f1_b, f2_w, f2_b, f3_w, f3_b, f4_w, sin_freq, hy_bias)
    y_at = windowed_gqa(q.reshape(B, L, N_Q_HEADS, HEAD_DIM), k.reshape(B, L, N_KV_HEADS, HEAD_DIM),
                        v.reshape(B, L, N_KV_HEADS, HEAD_DIM), q_gain, k_gain, sink)
    return jnp.concatenate([y_hy, y_at], axis=-1) @ w_out

def rwkv7_bidir_mixer(h, mu, w_r, w_k, w_v, w_o, w0, w1, w2, a0, a1, a2, g1, g2,
                      k_k, k_a, r_k, ln_w, ln_b):
    f32 = jnp.float32
    B, L, C = h.shape
    H, N = RWKV_HEADS, RWKV_HEAD
    hp = jnp.pad(h, ((0, 0), (1, 1), (0, 0)))
    xx = 0.5 * (hp[:, :-2] + hp[:, 2:]) - h
    xr, xw, xk, xv, xa, xg = (h + xx * mu[i] for i in range(6))
    r = (xr @ w_r).astype(f32)
    k = (xk @ w_k).astype(f32)
    v = (xv @ w_v).astype(f32)
    g = jax.nn.sigmoid(xg @ g1) @ g2
    lw = jnp.einsum('zblr,zrc->zblc', jnp.tanh(jnp.einsum('blc,zcr->zblr', xw, w1)), w2).astype(f32)
    w_log = -jax.nn.softplus(-(w0.astype(f32)[:, None, None, :] + lw)) - 0.5
    decay = jnp.exp(-jnp.exp(w_log))
    la = jnp.einsum('zblr,zrc->zblc', jnp.einsum('blc,zcr->zblr', xa, a1), a2).astype(f32)
    a = jax.nn.sigmoid(a0.astype(f32)[:, None, None, :] + la)
    kk = (k * k_k.astype(f32)).reshape(B, L, H, N)
    kk = (kk / jnp.maximum(jnp.linalg.norm(kk, axis=-1, keepdims=True), 1e-12)).reshape(B, L, C)
    k_dir = k[None] * (1.0 + (a - 1.0) * k_a.astype(f32))
    b_dir = kk[None] * a

    def time_major(t2):
        t2 = jnp.stack([t2[0], t2[1][:, ::-1]])
        return t2.reshape(2, B, L, H, N).transpose(2, 0, 1, 3, 4)

    def shared(t):
        return time_major(jnp.stack([t, t]))

    def step(S, inp):
        r_t, w_t, k_t, v_t, a_t, b_t = inp
        sa = jnp.einsum('zbhvk,zbhk->zbhv', S, a_t)
        S = S * w_t[..., None, :] + sa[..., :, None] * b_t[..., None, :] + v_t[..., :, None] * k_t[..., None, :]
        return S, jnp.einsum('zbhvk,zbhk->zbhv', S, r_t)

    xs = (shared(r), time_major(decay), time_major(k_dir), shared(v), shared(-kk), time_major(b_dir))
    _, ys = lax.scan(step, jnp.zeros((2, B, H, N, N), f32), xs)
    ys = ys.transpose(1, 2, 0, 3, 4)
    y = ys[0] + ys[1][:, ::-1]
    mean = jnp.mean(y, axis=-1, keepdims=True)
    var = jnp.mean(jnp.square(y - mean), axis=-1, keepdims=True)
    y = ((y - mean) * lax.rsqrt(var + GN_EPS)).reshape(B, L, C) * ln_w.astype(f32) + ln_b.astype(f32)
    k_bonus = 0.5 * (k_dir[0] + k_dir[1])
    bonus = jnp.sum((r * k_bonus * r_k.astype(f32).reshape(C)).reshape(B, L, H, N), axis=-1, keepdims=True) * v.reshape(B, L, H, N)
    y = y + bonus.reshape(B, L, C)
    return (y.astype(h.dtype) * g) @ w_o

def setup_inputs(seed: int = 0) -> dict:
    key = jax.random.key(seed)
    ks = iter(jax.random.split(key, 64))
    f32 = jnp.float32
    C, F = D_MODEL, D_FF

    def nrm(shape, scale):
        return scale * jax.random.normal(next(ks), shape, f32)

    def gain(shape):
        return 1.0 + 0.02 * jax.random.normal(next(ks), shape, f32)

    def unif(shape, lo, hi):
        return jax.random.uniform(next(ks), shape, f32, lo, hi)

    n_hy = (HYENA_ORDER + 1) * D_HYENA
    inp = {}
    inp['x'] = nrm((BATCH, SEQ, C), 1.0)
    inp['ffn1_norm'] = gain((DEPTH, C))
    inp['ffn1_wg'] = nrm((DEPTH, C, F), C ** -0.5)
    inp['ffn1_wu'] = nrm((DEPTH, C, F), C ** -0.5)
    inp['ffn1_wd'] = nrm((DEPTH, F, C), F ** -0.5)
    inp['mix_norm'] = gain((DEPTH, C))
    inp['ffn2_norm'] = gain((DEPTH, C))
    inp['ffn2_wg'] = nrm((DEPTH, C, F), C ** -0.5)
    inp['ffn2_wu'] = nrm((DEPTH, C, F), C ** -0.5)
    inp['ffn2_wd'] = nrm((DEPTH, F, C), F ** -0.5)
    inp['ab_w_in'] = nrm((N_EVEN, C, D_IN0), C ** -0.5)
    inp['ab_conv_w'] = nrm((N_EVEN, SHORT_CONV, n_hy), SHORT_CONV ** -0.5)
    inp['ab_conv_b'] = nrm((N_EVEN, n_hy), 0.02)
    inp['hy_f1_w'] = nrm((N_EVEN, FILTER_EMB, FILTER_ORDER), FILTER_EMB ** -0.5)
    inp['hy_f1_b'] = nrm((N_EVEN, FILTER_ORDER), 0.1)
    inp['hy_f2_w'] = nrm((N_EVEN, FILTER_ORDER, FILTER_ORDER), FILTER_ORDER ** -0.5)
    inp['hy_f2_b'] = nrm((N_EVEN, FILTER_ORDER), 0.1)
    inp['hy_f3_w'] = nrm((N_EVEN, FILTER_ORDER, FILTER_ORDER), FILTER_ORDER ** -0.5)
    inp['hy_f3_b'] = nrm((N_EVEN, FILTER_ORDER), 0.1)
    inp['hy_f4_w'] = nrm((N_EVEN, FILTER_ORDER, 2 * D_HYENA), FILTER_ORDER ** -0.5)
    inp['hy_sin_freq'] = gain((N_EVEN, FILTER_ORDER))
    inp['hy_bias'] = nrm((N_EVEN, D_HYENA), 1.0)
    inp['attn_q_norm'] = gain((N_EVEN, HEAD_DIM))
    inp['attn_k_norm'] = gain((N_EVEN, HEAD_DIM))
    inp['attn_sink'] = nrm((N_EVEN, N_Q_HEADS), 0.5)
    inp['ab_w_out'] = nrm((N_EVEN, C, C), C ** -0.5)
    inp['rw_mu'] = unif((N_ODD, 6, C), 0.0, 1.0)
    inp['rw_w_r'] = nrm((N_ODD, C, C), C ** -0.5)
    inp['rw_w_k'] = nrm((N_ODD, C, C), C ** -0.5)
    inp['rw_w_v'] = nrm((N_ODD, C, C), C ** -0.5)
    inp['rw_w_o'] = nrm((N_ODD, C, C), C ** -0.5)
    inp['rw_w0'] = unif((N_ODD, 2, C), -6.5, -1.5)
    inp['rw_w1'] = nrm((N_ODD, 2, C, LORA_W), C ** -0.5)
    inp['rw_w2'] = nrm((N_ODD, 2, LORA_W, C), 0.1 * LORA_W ** -0.5)
    inp['rw_a0'] = nrm((N_ODD, 2, C), 0.1)
    inp['rw_a1'] = nrm((N_ODD, 2, C, LORA_A), C ** -0.5)
    inp['rw_a2'] = nrm((N_ODD, 2, LORA_A, C), 0.1 * LORA_A ** -0.5)
    inp['rw_g1'] = nrm((N_ODD, C, LORA_G), C ** -0.5)
    inp['rw_g2'] = nrm((N_ODD, LORA_G, C), LORA_G ** -0.5)
    inp['rw_k_k'] = 0.85 + nrm((N_ODD, C), 0.02)
    inp['rw_k_a'] = gain((N_ODD, C))
    inp['rw_r_k'] = nrm((N_ODD, RWKV_HEADS, RWKV_HEAD), 0.1)
    inp['rw_ln_w'] = gain((N_ODD, C))
    inp['rw_ln_b'] = nrm((N_ODD, C), 0.02)
    return inp

def reference(x, ffn1_norm, ffn1_wg, ffn1_wu, ffn1_wd, mix_norm, ffn2_norm, ffn2_wg, ffn2_wu, ffn2_wd,
              ab_w_in, ab_conv_w, ab_conv_b, hy_f1_w, hy_f1_b, hy_f2_w, hy_f2_b, hy_f3_w, hy_f3_b,
              hy_f4_w, hy_sin_freq, hy_bias, attn_q_norm, attn_k_norm, attn_sink, ab_w_out,
              rw_mu, rw_w_r, rw_w_k, rw_w_v, rw_w_o, rw_w0, rw_w1, rw_w2, rw_a0, rw_a1, rw_a2,
              rw_g1, rw_g2, rw_k_k, rw_k_a, rw_r_k, rw_ln_w, rw_ln_b):
    for layer in range(DEPTH):
        x = x + 0.5 * swiglu(rms_norm(x, ffn1_norm[layer]), ffn1_wg[layer], ffn1_wu[layer], ffn1_wd[layer])
        h = rms_norm(x, mix_norm[layer])
        j = layer // 2
        if layer % 2 == 0:
            x = x + hyena_attention_mixer(h, ab_w_in[j], ab_conv_w[j], ab_conv_b[j], hy_f1_w[j], hy_f1_b[j],
                                          hy_f2_w[j], hy_f2_b[j], hy_f3_w[j], hy_f3_b[j], hy_f4_w[j],
                                          hy_sin_freq[j], hy_bias[j], attn_q_norm[j], attn_k_norm[j],
                                          attn_sink[j], ab_w_out[j])
        else:
            x = x + rwkv7_bidir_mixer(h, rw_mu[j], rw_w_r[j], rw_w_k[j], rw_w_v[j], rw_w_o[j], rw_w0[j],
                                      rw_w1[j], rw_w2[j], rw_a0[j], rw_a1[j], rw_a2[j], rw_g1[j], rw_g2[j],
                                      rw_k_k[j], rw_k_a[j], rw_r_k[j], rw_ln_w[j], rw_ln_b[j])
        x = x + 0.5 * swiglu(rms_norm(x, ffn2_norm[layer]), ffn2_wg[layer], ffn2_wu[layer], ffn2_wd[layer])
    return x


_drawn_inputs = setup_inputs


def setup_inputs(seed=0):
    import zlib

    import numpy as np

    out = dict(_drawn_inputs(seed))
    spreads = {}
    factors = {'ffn1_norm': 3.711,
     'ffn2_norm': 5.498,
     'hy_f1_b': 4.045,
     'hy_f2_b': 3.692,
     'hy_f3_b': 2.864,
     'hy_sin_freq': 8.0,
     'attn_q_norm': 8.0,
     'attn_k_norm': 8.0,
     'attn_sink': 8.0,
     'rw_w1': 22.18,
     'rw_w2': 8.0,
     'rw_a0': 3.636,
     'rw_a1': 4.308,
     'rw_a2': 4.324,
     'rw_k_k': 58.552,
     'rw_k_a': 28.126,
     'rw_ln_w': 57.64,
     'rw_ln_b': 60.104,
     'ab_conv_b': 6.253}
    for name, (base, spread) in spreads.items():
        noise = np.random.default_rng([zlib.crc32(name.encode()), seed]).standard_normal(out[name].shape)
        drawn = base * np.exp(spread * noise) if base else spread * noise
        out[name] = jnp.asarray(drawn.astype(out[name].dtype))
    for name, factor in factors.items():
        out[name] = (out[name] * factor).astype(out[name].dtype)
    return out
```

```python
import math
from contextlib import ExitStack

import numpy as np
import concourse.bass as bass
from concourse import mybir

P = 128
C = 1024
L = 256
CT = C // P
F = 2816
FT = F // P
HT = 4
NQ, NKV, HD = 8, 2, 64
LORA_G = 160
CH = 64
NCH = L // CH
NU = 2 * NCH
BLK = CT * P
FILTER_EMB, FILTER_ORDER = 33, 64
DECAY = math.exp(-0.5)

FFN_STEPS = FT + 1
IN_STEPS, OUT_STEPS, RKV_STEPS, LORA_STEPS, O_STEPS = 6, 3, 8, 2, 4
SCAN_OWN = 59
S_FFN = [0, 0, 0, 0]
S_FFN[0] = 0
S_IN = FFN_STEPS
S_OUT = S_IN + IN_STEPS
S_FFN[1] = S_OUT + OUT_STEPS
S_FFN[2] = S_FFN[1] + FFN_STEPS
S_RKV = S_FFN[2] + FFN_STEPS
S_LORA = S_RKV + RKV_STEPS
S_O = S_LORA + LORA_STEPS
S_FFN[3] = S_O + O_STEPS
STEPS = S_FFN[3] + FFN_STEPS


def blocks_in(s):
    for s0 in S_FFN:
        if s == s0:
            return 2
        if s == s0 + FT:
            return 1
    return {S_OUT + 2: 2, S_O + 3: 1}.get(s, 3)


_names = [("ffn1_norm", 2 * CT), ("mix_norm", 2 * CT), ("ffn2_norm", 2 * CT), ("conv_w", 3 * 12), ("conv_b", 12),
          ("hy_bias", HT), ("mu", 6 * CT), ("w0", 2 * CT), ("a0", 2 * CT), ("k_k", CT), ("k_a", CT), ("r_k", CT),
          ("ln_w", CT), ("ln_b", CT), ("q_gain", 1), ("k_gain", 1), ("sink", NQ), ("f_b", 3), ("freq", 1)]
COL = {}
_at = 0
for _n, _w in _names:
    COL[_n] = _at
    _at += _w
NPAR = _at
LEVELS = [2, 4, 8, 16, 32]
ARENA = 17000

_cn = [("ident", P), ("istack", CH), ("blockones", P), ("ones", P), ("sel", CT * 16), ("selt", CT * P), ("perm", P), ("m1", 2 * CH), ("m1t", 2 * CH),
       ("strict", 2 * CH), ("incl", 2 * CH), ("level", len(LEVELS) * 2 * P), ("reset", L)]
CC = {}
_at = 0
for _n, _w in _cn:
    CC[_n] = _at
    _at += _w
NCONST = _at
_hn = [("cos", 2 * L), ("sin", 2 * L), ("icos", 2 * L), ("isin", 2 * L), ("window", 2 * 512), ("dist", 2 * L),
       ("feat", L)]
HC = {}
_at = 0
for _n, _w in _hn:
    HC[_n] = _at
    _at += _w
NHC = _at
NFW = 3 * FILTER_ORDER + 2 * 512


def build(nc, io):
    fp32 = mybir.dt.float32
    f32r = mybir.dt.float32r
    ALU = mybir.AluOpType
    ACT = mybir.ActivationFunctionType
    AX = mybir.AxisListType
    xT, stream, par_d, const_d, hconst_d, fw_d, out = io
    ctx = ExitStack()
    with ctx:
        def sb(name, shape, dt=fp32):
            return ctx.enter_context(nc.sbuf_tensor(name, shape, dt))

        def sem(name):
            return ctx.enter_context(nc.semaphore(name))

        X = sb("X", [P, CT, L])
        h_offset = nc.sbuf_base
        HH = sb("HH", [P, CT, L], f32r)
        HL = sb("HL", [P, CT, L], f32r)
        XSQ = sb("XSQ", [P, CT, L])
        raw = sb("raw", [P, 2, 3 * BLK])
        w_offset = nc.sbuf_base
        WH = sb("WH", [P, 2, 3 * BLK], f32r)
        WL = sb("WL", [P, 2, 3 * BLK], f32r)
        PH = sb("PH", [P, 2, L], f32r)
        PL = sb("PL", [P, 2, L], f32r)
        work = sb("work", [P, 4, 2, L])
        prod, gs, us, sg = (work[:, n, :, :] for n in range(4))
        std = sb("std", [P, L])
        rstd = sb("rstd", [P, L])
        par = sb("par", [P, NPAR])
        cst = sb("cst", [P, NCONST])

        scan = nc.alloc_sbuf_tensor_at("scan", [P, 4 * 3 * BLK], fp32, offset=w_offset)
        scan2 = nc.alloc_sbuf_tensor_at("scan2", [P, 2 * CT * L], fp32, offset=h_offset)

        bank = [ctx.enter_context(nc.psum_tensor(f"bank{i}", [P, 512], fp32)) for i in range(8)]
        GU = bank[0:2]
        ST = bank[2]
        DN = bank[4:8]

        def pcol(name, i=0):
            return par[:, COL[name] + i:COL[name] + i + 1]

        def ccols(name, n, off=0):
            return cst[:, CC[name] + off:CC[name] + off + n]

        ones = ccols("ones", P)

        raw_full = [sem("raw_full0"), sem("raw_full1")]
        hi_ready = sem("hi_ready")
        lo_ready = sem("lo_ready")
        blocks_done = sem("blocks_done")
        loaded = sem("loaded")
        hh_ready = sem("hh_ready")
        hl_ready = sem("hl_ready")
        sq_ready = sem("sq_ready")
        std_ready = sem("std_ready")
        rstd_ready = sem("rstd_ready")
        gs_ready = sem("gs_ready")
        sg_ready = sem("sg_ready")
        prod_ready = sem("prod_ready")
        ph_ready = sem("ph_ready")
        pl_ready = sem("pl_ready")
        x_ready = sem("x_ready")
        stored = sem("stored")
        block = ctx.enter_context(nc.Block())

        def split_hi(act, s, width=3 * BLK, slot=None, uses=None):
            slot = s % 2 if slot is None else slot
            act.wait_ge(raw_full[slot], 16 * (s // 2 + 1) if uses is None else uses)
            act.wait_ge(blocks_done, 3 * s - 3) if not (isinstance(s, int) and s < 2) else None
            nc.scalar.activation(WH[:, slot, :width], raw[:, slot, :width], ACT.Copy).then_inc(hi_ready, 1)

        def split_lo(dve, s, width=3 * BLK, slot=None):
            slot = s % 2 if slot is None else slot
            dve.wait_ge(hi_ready, s + 1)
            nc.vector.tensor_tensor(WL[:, slot, :width], raw[:, slot, :width],
                                    WH[:, slot, :width].bitcast(fp32), ALU.subtract).then_inc(lo_ready, 1)

        def next_hi(act, s):
            if s < STEPS:
                split_hi(act, s, blocks_in(s) * BLK)

        def next_lo(dve, s):
            if s < STEPS:
                split_lo(dve, s, blocks_in(s) * BLK)

        def three(out_ap, lo_off, slot, xh, xl, start, stop, rows=slice(0, P), m=P, **kw):
            wh = WH[rows, slot, lo_off:lo_off + m]
            wl = WL[rows, slot, lo_off:lo_off + m]
            nc.tensor.matmul(out_ap, wh, xh, start=start, stop=False, **kw)
            nc.tensor.matmul(out_ap, wh, xl, start=False, stop=False, **kw)
            return nc.tensor.matmul(out_ap, wl, xh, start=False, stop=stop, **kw)

        def project(out_ap, slot, b, inp=None, wait=None):
            xh, xl = inp if inp is not None else (HH, HL)
            for k in range(CT):
                if wait is not None:
                    wait(k)
                last = three(out_ap, b * BLK + k * P, slot, xh[:, k, :], xl[:, k, :], k == 0, k == CT - 1)
            return last

        def pe_down(pe, slot, b, par_, first, last=False):
            for m in range(CT):
                dst = DN[m // 2][:, (m % 2) * L:(m % 2) * L + L]
                w = b * BLK + m * P
                a, c_ = PH[:, par_, :], PL[:, par_, :]
                ins = three(dst, w, slot, a, c_, first and m % 2 == 0, last, skip_group_check=True)
                if last and m in (3, 5):
                    ins.then_inc(blocks_done, 1)
            ins.then_inc(blocks_done, 1)

        def pe_ffn(pe, n, s0, q0):
            p0 = s0 % 2
            h0 = NORM_TILES[n]
            pe.wait_ge(lo_ready, s0 + 1)

            def wait_h(k):
                pe.wait_ge(hl_ready, h0 + k + 1)
            project(GU[0][:, 0:L], p0, 0, wait=wait_h).then_inc(blocks_done, 1)
            project(GU[0][:, L:2 * L], p0, 1).then_inc(blocks_done, 1)
            pe_stats(pe, n).then_inc(blocks_done, 1)

            def step(s, f, slot, first=False):
                pe.wait_ge(lo_ready, s + 1)
                if not (isinstance(f, int) and f < 2):
                    pe.wait_ge(gs_ready, 2 * (q0 + f - 1))
                g = GU[(slot - p0) % 2]
                project(g[:, 0:L], slot, 0).then_inc(blocks_done, 1)
                project(g[:, L:2 * L], slot, 1).then_inc(blocks_done, 1)
                pe.wait_ge(pl_ready, q0 + f)
                pe_down(pe, slot, 2, (slot - p0 + 1) % 2, first)
            step(s0 + 1, 1, (p0 + 1) % 2, first=True)
            with pe.Fori(0, (FT - 2) // 2) as i:
                for u in range(2):
                    f = 2 * i + (2 + u)
                    step(s0 + f, f, (p0 + u) % 2)
            pe.wait_ge(lo_ready, s0 + FT + 1)
            pe.wait_ge(pl_ready, q0 + FT)
            pe_down(pe, (s0 + FT) % 2, 0, (FT - 1) % 2, False, last=True)

        def pe_stats(pe, n):
            for k in range(CT):
                if k % (CT // 2) == 0:
                    pe.wait_ge(sq_ready, 2 * n + 1 + k // (CT // 2))
                last = nc.tensor.matmul(ST[:, 0:L], ones, XSQ[:, k, :], start=k == 0, stop=k == CT - 1)
            return last

        def act_norm_in(act, n, gain):
            if n == 0:
                act.wait_ge(loaded, LOADS)
            elif n % 3 == 2:
                act.wait_ge(x_ready, 3 * n)
            for k in range(CT):
                if n % 3 != 2 and n and k in (0, 4, 6):
                    act.wait_ge(x_ready, 3 * n - 2 + (0, 4, 6).index(k))
                nc.scalar.activation(HH[:, k, :], X[:, k, :], ACT.Copy, scale=pcol(gain[0], gain[1] + k))\
                    .then_inc(hh_ready, 1)
            act_squares(act)

        def act_squares(act):
            for k in range(2):
                nc.scalar.activation(XSQ[:, 4 * k:4 * k + 4, :], X[:, 4 * k:4 * k + 4, :], ACT.Square)\
                    .then_inc(sq_ready, 1)

        def dve_norm_in(dve, n, gain):
            for k in range(CT):
                dve.wait_ge(hh_ready, NORM_TILES[n] + k + 1)
                nc.vector.scalar_tensor_tensor(out=HL[:, k, :], in0=X[:, k, :], scalar=pcol(gain[0], gain[1] + k),
                                               in1=HH[:, k, :].bitcast(fp32), op0=ALU.mult, op1=ALU.subtract)\
                    .then_inc(hl_ready, 1)

        def act_root(act, n, st_wait):
            act.wait_ge(*st_wait)
            if n == 0:
                act.wait_ge(eps_ready, 1)
            nc.scalar.activation(std[:, :], ST[:, 0:L], ACT.Sqrt, bias=eps6[:, 0:1], scale=1.0 / C).then_inc(std_ready, 1)

        def dve_root(dve, n):
            dve.wait_ge(std_ready, n + 1)
            nc.vector.reciprocal(rstd[:, :], std[:, :]).then_inc(rstd_ready, 1)

        def act_ffn(act, n, s0, q0):
            p0 = s0 % 2
            next_hi(act, s0 + 1)
            act_root(act, n, (blocks_done, 3 * s0 + 3))

            def glue(f, o):
                act.wait_ge(gs_ready, 2 * (q0 + f) + 1)
                nc.scalar.activation(sg[:, o, :], gs[:, o, :], ACT.Silu).then_inc(sg_ready, 1)
                act.wait_ge(prod_ready, q0 + f + 1)
                nc.scalar.activation(PH[:, o, :], prod[:, o, :], ACT.Copy).then_inc(ph_ready, 1)
            glue(0, 0)
            with act.Fori(0, (FT - 2) // 2) as i:
                for u in range(2):
                    s = s0 + 2 * i + (2 + u)
                    slot = (p0 + u) % 2
                    split_hi(act, s, slot=slot, uses=16 * i + 16 * ((s0 + 2 + u) // 2 + 1))
                    glue(2 * i + (1 + u), (1 + u) % 2)
            next_hi(act, s0 + FT)
            glue(FT - 1, (FT - 1) % 2)
            next_hi(act, s0 + FT + 1)

        def dve_ffn(dve, n, s0, q0):
            p0 = s0 % 2
            next_lo(dve, s0 + 1)
            dve_root(dve, n)

            def glue(f, o):
                dve.wait_ge(blocks_done, 3 * s0 + 3 * f + 2)
                if isinstance(f, int) and f == 0:
                    dve.wait_ge(rstd_ready, n + 1)
                nc.vector.tensor_tensor(gs[:, o, :], GU[o][:, 0:L], rstd[:, :], ALU.mult).then_inc(gs_ready, 1)
                nc.vector.tensor_tensor(us[:, o, :], GU[o][:, L:2 * L], rstd[:, :], ALU.mult).then_inc(gs_ready, 1)
                dve.wait_ge(sg_ready, q0 + f + 1)
                dve.wait_ge(gs_ready, 2 * (q0 + f + 1))
                nc.vector.tensor_tensor(prod[:, o, :], sg[:, o, :], us[:, o, :], ALU.mult).then_inc(prod_ready, 1)
                dve.wait_ge(ph_ready, q0 + f + 1)
                nc.vector.tensor_tensor(PL[:, o, :], prod[:, o, :], PH[:, o, :].bitcast(fp32), ALU.subtract)\
                    .then_inc(pl_ready, 1)
            glue(0, 0)
            with dve.Fori(0, (FT - 2) // 2) as i:
                for u in range(2):
                    split_lo(dve, s0 + 2 * i + (2 + u), slot=(p0 + u) % 2)
                    glue(2 * i + (1 + u), (1 + u) % 2)
            next_lo(dve, s0 + FT)
            glue(FT - 1, (FT - 1) % 2)
            next_lo(dve, s0 + FT + 1)

        def dve_residual(dve, s, scale):
            for part, js in enumerate(((0, 1), (2,), (3,))):
                dve.wait_ge(blocks_done, 3 * s + part + 1)
                for j in js:
                    last = nc.vector.scalar_tensor_tensor(
                        out=X[:, 2 * j:2 * j + 2, :], in0=DN[j][:, :].rearrange("p (a n) -> p a n", a=2), scalar=scale,
                        in1=X[:, 2 * j:2 * j + 2, :], op0=ALU.mult, op1=ALU.add)
                last.then_inc(x_ready, 1)

        eps6 = sb("eps6", [P, 4])
        NORM_TILES = [0, CT, 2 * CT, 3 * CT, None, 4 * CT]
        arena = sb("arena", [P, ARENA])
        at = [0]

        def place(n):
            at[0] += n
            assert at[0] <= ARENA
            return arena[:, at[0] - n:at[0]]
        hcst = place(NHC)
        fw = place(NFW)
        HRI = place(4 * 512).rearrange("p (i k c) -> p i k c", i=2, k=2)
        U3 = place(12 * (L + 2)).rearrange("p (m t) -> p m t", t=L + 2)
        UQ = place(6 * L).rearrange("p (m t) -> p m t", t=L)
        after_u = at[0]
        UC = place(12 * L).rearrange("p (m t) -> p m t", t=L)
        ZT = place(2 * 512).rearrange("p (a c) -> p a c", a=2)
        TM = XSQ[:, :, :].rearrange("p k t -> p (k t)").rearrange("p (i c) -> p i c", i=4)
        at[0] = NHC + NFW + 4 * 512
        YRI = place(4 * 512).rearrange("p (i k c) -> p i k c", i=2, k=2)
        at[0] = NHC + NFW + 4 * 512
        HFB = place(4 * 512).rearrange("p (i a c) -> p i a c", i=2, a=2)
        ABS = place(4 * 512).rearrange("p (i a c) -> p i a c", i=2, a=2)
        HSD = place(4 * 512).rearrange("p (i a c) -> p i a c", i=2, a=2)
        FARG = place(3 * L).rearrange("p (i t) -> p i t", i=3)
        FHID = place(3 * L).rearrange("p (i t) -> p i t", i=3)
        at[0] = after_u
        QN = place(4 * L).rearrange("p (m t) -> p m t", t=L)
        KN = place(2 * L).rearrange("p (m t) -> p m t", t=L)
        VT = place(2 * P).rearrange("p (a c) -> p a c", a=2)
        SC = place(2 * 512).rearrange("p (o a k) -> p o a k", o=2, a=2)
        EX = place(2 * 512).rearrange("p (o a k) -> p o a k", o=2, a=2)
        PT = place(2 * 512).rearrange("p (o b q) -> p o b q", o=2, b=2)
        RN = sg[0:16, :, :]
        small = sb("small", [P, 64])
        hy_rnorm = small[:, 0:4]
        amax, anegm, asum, aes, aden, arden = (small[:, 4 + 2 * k:6 + 2 * k] for k in range(6))
        ymix = prod
        sel = ccols("sel", CT * 16).rearrange("p (j h) -> p j h", h=16)
        selt = ccols("selt", CT * P)[0:16, :].rearrange("p (j c) -> p j c", c=P)
        ident = ccols("ident", P)

        def hc(name, n):
            return hcst[:, HC[name]:HC[name] + n]
        dft = [hc(n, 2 * L).rearrange("p (a k) -> p a k", a=2) for n in ("cos", "sin")]
        idft = [hc(n, 2 * L).rearrange("p (k t) -> p k t", k=2) for n in ("icos", "isin")]
        window = hc("window", 1024).rearrange("p (a c) -> p a c", a=2)
        dist = hc("dist", 2 * L).rearrange("p (a k) -> p a k", a=2)
        FO = FILTER_ORDER
        INV2PI = 1.0 / (2.0 * math.pi)
        ROUND = 1.5 * 2.0 ** 23
        PI2 = [6.28125, float(np.float32(2 * math.pi - 6.28125))]
        PI2.append(2 * math.pi - PI2[0] - PI2[1])
        SLOPES = [2.0 ** (-8.0 * (h + 1) / NQ) for h in range(NQ)]

        eps_ready = sem("eps_ready")
        dve_own = sem("dve_own")
        flt_mm = sem("flt_mm")
        flt_arg = sem("flt_arg")
        flt_sin = sem("flt_sin")
        flt_win = sem("flt_win")
        flt_abs = sem("flt_abs")
        flt_sum = sem("flt_sum")
        flt_h = sem("flt_h")
        u_ready = sem("u_ready")
        cv_ready = sem("cv_ready")
        qsq_ready = sem("qsq_ready")
        ss_done = sem("ss_done")
        root_ready = sem("root_ready")
        rec_ready = sem("rec_ready")
        bc_done = sem("bc_done")
        qn_ready = sem("qn_ready")
        z_ready = sem("z_ready")
        zt_done = sem("zt_done")
        zt_ready = sem("zt_ready")
        zf_done = sem("zf_done")
        y_spec = sem("y_spec")
        yi_done = sem("yi_done")
        ym_ready = sem("ym_ready")
        ks_done = sem("ks_done")
        ks_ready = sem("ks_ready")
        mix_hh = sem("mix_hh")
        mix_hl = sem("mix_hl")
        st_ready = sem("st_ready")
        sc_done = sem("sc_done")
        sc_ready = sem("sc_ready")
        ex_ready = sem("ex_ready")
        pr_ready = sem("pr_ready")
        pt_done = sem("pt_done")
        pt_ready = sem("pt_ready")
        pv_done = sem("pv_done")

        class Own:
            def __init__(self, eng, s, before=0):
                self.eng, self.s, self.before, self.n = eng, s, before, 0

            def __call__(self, ins):
                ins.then_inc(self.s, 1)
                self.n = self.n + 1

            def settle(self):
                self.eng.wait_ge(self.s, self.before + self.n)

        def pe_filter(pe):
            b3 = bank[3]
            nc.tensor.matmul(b3[0:FO, 0:L], fw[0:FILTER_EMB, 0:FO], hc("feat", L)[0:FILTER_EMB, :],
                             start=True, stop=True).then_inc(flt_mm, 1)
            for n in (1, 2):
                pe.wait_ge(flt_sin, n)
                nc.tensor.matmul(b3[0:FO, 0:L], fw[0:FO, n * FO:(n + 1) * FO], FHID[0:FO, n - 1, :],
                                 start=True, stop=True).then_inc(flt_mm, 1)
            pe.wait_ge(flt_sin, 3)
            for a in range(2):
                for i in range(2):
                    last = nc.tensor.matmul(DN[2 * a + i][:, :], FHID[0:FO, 2, a * P:(a + 1) * P],
                                            fw[0:FO, 3 * FO + 512 * i:3 * FO + 512 * (i + 1)], start=True, stop=True)
            last.then_inc(flt_mm, 1)
            pe.wait_ge(flt_abs, 1)
            for c in range(HT):
                for n in range(4):
                    last = nc.tensor.matmul(b3[:, c:c + 1], ABS[:, n // 2, n % 2, c * P:(c + 1) * P], ones[:, 0:1],
                                            start=n == 0, stop=n == 3)
            last.then_inc(flt_mm, 1)
            pe.wait_ge(flt_sum, 1)
            for i in range(2):
                for k in range(2):
                    for a in range(2):
                        last = nc.tensor.matmul(DN[2 * i + k][:, :], dft[i][:, a, k * P:(k + 1) * P], HSD[:, i, a, :],
                                                start=a == 0, stop=a == 1)
            last.then_inc(flt_mm, 1)

        def act_filter(act):
            for n in range(3):
                act.wait_ge(flt_arg, n + 1)
                nc.scalar.activation(FHID[0:FO, n, :], FARG[0:FO, 0, :], ACT.Sin).then_inc(flt_sin, 1)
            act.wait_ge(flt_win, 1)
            nc.scalar.activation(ABS[:, :, :, :], HFB[:, :, :, :], ACT.Abs).then_inc(flt_abs, 1)
            act.wait_ge(flt_mm, 6)
            for n in range(4):
                last = nc.scalar.activation(HRI[:, n // 2, n % 2, :], DN[n][:, :], ACT.Copy)
            last.then_inc(flt_h, 1)

        def dve_filter(dve, own):
            ts, stt = nc.vector.tensor_scalar, nc.vector.scalar_tensor_tensor
            x, k = FARG[0:FO, 0, :], FARG[0:FO, 1, :]
            for n in range(3):
                dve.wait_ge(flt_mm, n + 1)
                if n:
                    dve.wait_ge(flt_sin, n)
                own(ts(x, bank[3][0:FO, 0:L], pcol("f_b", n)[0:FO], pcol("freq")[0:FO], ALU.add, ALU.mult))
                own.settle()
                own(ts(k, x, INV2PI, ROUND, ALU.mult, ALU.add))
                own.settle()
                own(ts(k, k, -ROUND, None, ALU.add))
                for c in PI2:
                    own.settle()
                    own(stt(out=x, in0=k, scalar=-c, in1=x, op0=ALU.mult, op1=ALU.add))
                own.settle()
                ts(x, x, 3.1415925, -3.1415925, ALU.min, ALU.max).then_inc(flt_arg, 1)
            dve.wait_ge(flt_mm, 4)
            for a in range(2):
                for i in range(2):
                    own(nc.vector.tensor_tensor(HFB[:, i, a, :], DN[2 * a + i][:, :], window[:, a, :], ALU.mult))
            own.settle()
            own(nc.vector.tensor_tensor(HFB[0:1, 0, 0, :], HFB[0:1, 0, 0, :], HFB[0:1, 1, 0, :], ALU.add))
            own.settle()
            nc.vector.memset(HFB[0:1, 1, 0, :], 0.0).then_inc(flt_win, 1)
            dve.wait_ge(flt_win, 1)
            nc.vector.tensor_tensor(HSD[:, 0, :, :], HFB[:, 0, :, :], HFB[:, 1, :, :], ALU.add)
            nc.vector.tensor_tensor(HSD[:, 1, :, :], HFB[:, 0, :, :], HFB[:, 1, :, :], ALU.subtract).then_inc(flt_sum, 1)
            dve.wait_ge(flt_mm, 5)
            own(nc.vector.reciprocal(hy_rnorm, bank[3][:, 0:HT]))
            dve.wait_ge(flt_mm, 6)
            own(nc.vector.memset(U3[:, :, 0:1], 0.0))
            own(nc.vector.memset(U3[:, :, L + 1:L + 2], 0.0))

        UB = [GU[0], GU[1], bank[3]]

        def pe_mix0(pe):
            s0, n = S_IN, 1
            for m in range(18):
                s, b = s0 + m // 3, m % 3
                if b == 0:
                    pe.wait_ge(lo_ready, s + 1)
                if m >= 3:
                    pe.wait_ge(u_ready, m - 2)
                wait = (lambda k: pe.wait_ge(hl_ready, NORM_TILES[n] + k + 1)) if m == 0 else None
                project(UB[m % 3][:, 0:L], s % 2, b, wait=wait).then_inc(blocks_done, 1)
                if m == 0:
                    pe_stats(pe, n).then_inc(st_ready, 1)
            pe.wait_ge(qsq_ready, 5)
            pe.wait_ge(u_ready, 16)
            for j in range(5):
                last = nc.tensor.matmul(GU[0][0:16, 0:L], sel[:, j, :], XSQ[:, j, :], start=j == 0, stop=j == 4)
            last.then_inc(ss_done, 1)
            pe.wait_ge(z_ready, 1)
            for a in range(2):
                for c in range(HT):
                    last = nc.tensor.transpose(DN[a][:, c * P:(c + 1) * P], UC[:, 8 + c, a * P:(a + 1) * P], ident)
            last.then_inc(zt_done, 1)
            pe.wait_ge(u_ready, 18)
            pe.wait_ge(rec_ready, 1)
            for j in range(5):
                dst = (bank[3], GU[1], GU[0])[j // 2][:, (j % 2) * L:(j % 2) * L + L]
                last = nc.tensor.matmul(dst, selt[:, j, :], RN[:, 1, :], start=True, stop=True)
            last.then_inc(bc_done, 1)
            pe.wait_ge(zt_ready, 1)
            for i in range(2):
                for k in range(2):
                    for a in range(2):
                        last = nc.tensor.matmul(DN[2 * i + k][:, :], dft[i][:, a, k * P:(k + 1) * P], ZT[:, a, :],
                                                start=a == 0, stop=a == 1)
            last.then_inc(zf_done, 1)
            pe.wait_ge(y_spec, 1)
            for c in range(HT):
                for n in range(4):
                    last = nc.tensor.matmul(DN[c][:, 0:L], YRI[:, n // 2, n % 2, c * P:(c + 1) * P],
                                            idft[n // 2][:, n % 2, :], start=n == 0, stop=n == 3)
                last.then_inc(yi_done, 1)
            pe.wait_ge(qn_ready, 5)
            nc.tensor.matmul(GU[0][:, L:2 * L], ccols("perm", P), KN[:, 0, :], start=True, stop=True).then_inc(ks_done, 1)
            for a in range(2):
                last = nc.tensor.transpose(ST[:, a * P:(a + 1) * P], UQ[:, 5, a * P:(a + 1) * P], ident)
            last.then_inc(zt_done, 1)
            pe.wait_ge(ks_ready, 1)
            pe.wait_ge(zt_ready, 2)
            pe.wait_ge(ym_ready, HT)

            def scores(h):
                if h >= 2:
                    pe.wait_ge(sc_ready, h - 1)
                r = slice(HD * (h % 2), HD * (h % 2) + HD)
                kn = KN[r, 0 if h % 2 == h // 4 else 1, :]
                for a in range(2):
                    last = nc.tensor.matmul(DN[h % 2][:, a * L:(a + 1) * L], QN[r, h // 2, a * P:(a + 1) * P], kn,
                                            start=True, stop=True)
                last.then_inc(sc_done, 1)
            scores(0)
            for h in range(NQ):
                if h + 1 < NQ:
                    scores(h + 1)
                pe.wait_ge(pr_ready, h + 1)
                if h >= 2:
                    pe.wait_ge(pt_ready, h - 1)
                for b in range(2):
                    for a in range(2):
                        last = nc.tensor.transpose(DN[2 + h % 2][:, b * L + a * P:b * L + (a + 1) * P],
                                                   SC[:, h % 2, a, b * P:(b + 1) * P], ident)
                last.then_inc(pt_done, 1)
                pe.wait_ge(pt_ready, h + 1)
                if h >= 4 and h % 2 == 0:
                    pe.wait_ge(ym_ready, HT + (h - 4) // 2 + 1)
                kv, r = h // 4, slice(HD * (h % 2), HD * (h % 2) + HD)
                for b in range(2):
                    last = nc.tensor.matmul(GU[(h // 2) % 2][r, 0:L], VT[:, b, kv * HD:(kv + 1) * HD],
                                            PT[:, h % 2, b, :], start=b == 0, stop=b == 1)
                last.then_inc(pv_done, 1)
            pe_out(pe, S_OUT)

        def pe_out(pe, s0):
            for m in range(CT):
                s, b = s0 + m // 3, m % 3
                if b == 0:
                    pe.wait_ge(lo_ready, s + 1)
                dst = DN[m // 2][:, (m % 2) * L:(m % 2) * L + L]
                for k in range(CT):
                    if m == 0:
                        pe.wait_ge(mix_hl, (CT if s0 == S_O else 0) + k + 1)
                    last = three(dst, b * BLK + k * P, s % 2, HH[:, k, :], HL[:, k, :], k == 0, k == CT - 1)
                    if m == CT - 1 and k == 3:
                        last.then_inc(blocks_done, 1)
                last.then_inc(blocks_done, 1)

        def dve_out(dve, s0):
            for part, (js, done) in enumerate((((0, 1), 4), ((2,), 6), ((3,), 9))):
                dve.wait_ge(blocks_done, 3 * s0 + done)
                for j in js:
                    last = nc.vector.tensor_tensor(X[:, 2 * j:2 * j + 2, :], DN[j][:, :].rearrange("p (a n) -> p a n", a=2),
                                                   X[:, 2 * j:2 * j + 2, :], ALU.add)
                last.then_inc(x_ready, 1)

        def act_mix0(act):
            act_root(act, 1, (st_ready, 1))
            for m in range(18):
                if m % 3 == 0:
                    next_hi(act, S_IN + m // 3 + 1)
                act.wait_ge(u_ready, m + 1)
                if m < 12:
                    nc.scalar.activation(UC[:, m, :], U3[:, m, 1:L + 1], ACT.Identity, bias=pcol("conv_b", m),
                                         scale=pcol("conv_w", 12 + m)).then_inc(cv_ready, 1)
                elif m < 17:
                    nc.scalar.activation(XSQ[:, m - 12, :], UQ[:, m - 12, :], ACT.Square).then_inc(qsq_ready, 1)
            act.wait_ge(ss_done, 1)
            nc.scalar.activation(RN[:, 0, :], GU[0][0:16, 0:L], ACT.Sqrt, bias=eps6[0:16, 0:1], scale=1.0 / HD)\
                .then_inc(root_ready, 1)
            act.wait_ge(zt_done, 1)
            for a in range(2):
                last = nc.scalar.activation(ZT[:, a, :], DN[a][:, :], ACT.Copy)
            last.then_inc(zt_ready, 1)
            for c in range(HT):
                act_mixed(act, c)
            act.wait_ge(ks_done, 1)
            nc.scalar.activation(KN[:, 1, :], GU[0][:, L:2 * L], ACT.Copy).then_inc(ks_ready, 1)
            act.wait_ge(zt_done, 2)
            nc.scalar.activation(VT[:, :, :], ST[:, 0:2 * P].rearrange("p (a c) -> p a c", a=2), ACT.Copy)\
                .then_inc(zt_ready, 1)
            for h in range(NQ):
                act.wait_ge(sc_ready, h + 1)
                for a in range(2):
                    nc.scalar.activation(EX[:, h % 2, a, :], SC[:, h % 2, a, :], ACT.Exp, bias=anegm[:, a:a + 1],
                                         accum_out=asum[:, a:a + 1])
                nc.scalar.activation(aes, anegm, ACT.Exp, bias=pcol("sink", h)).then_inc(ex_ready, 1)
                act.wait_ge(pt_done, h + 1)
                nc.scalar.activation(PT[:, h % 2, :, :], DN[2 + h % 2][:, :].rearrange("p (b q) -> p b q", b=2), ACT.Copy)\
                    .then_inc(pt_ready, 1)
                if h % 2:
                    act_mixed(act, HT + h // 2)

        def act_mixed(act, t, base=0):
            act.wait_ge(ym_ready, base + t + 1)
            nc.scalar.activation(HH[:, t, :], ymix[:, t % 2, :], ACT.Copy).then_inc(mix_hh, 1)

        def dve_mixed(dve, t, base=0):
            dve.wait_ge(mix_hh, base + t + 1)
            nc.vector.tensor_tensor(HL[:, t, :], ymix[:, t % 2, :], HH[:, t, :].bitcast(fp32), ALU.subtract)\
                .then_inc(mix_hl, 1)

        def dve_mix0(dve, own):
            tt, stt = nc.vector.tensor_tensor, nc.vector.scalar_tensor_tensor
            dve_root(dve, 1)
            dve.wait_ge(rstd_ready, 2)
            own.settle()
            dve.wait_ge(flt_h, 1)

            def conv(m):
                dve.wait_ge(cv_ready, m + 1)
                own(stt(out=UC[:, m, :], in0=U3[:, m, 0:L], scalar=pcol("conv_w", m), in1=UC[:, m, :],
                        op0=ALU.mult, op1=ALU.add))
                own.settle()
                own(stt(out=UC[:, m, :], in0=U3[:, m, 2:L + 2], scalar=pcol("conv_w", 24 + m), in1=UC[:, m, :],
                        op0=ALU.mult, op1=ALU.add))
            for m in range(18):
                if m % 3 == 0:
                    next_lo(dve, S_IN + m // 3 + 1)
                dve.wait_ge(blocks_done, 3 * S_IN + m + 1)
                dst = U3[:, m, 1:L + 1] if m < 12 else UQ[:, m - 12, :]
                tt(dst, UB[m % 3][:, 0:L], rstd[:, :], ALU.mult).then_inc(u_ready, 1)
                if 1 <= m <= 12:
                    conv(m - 1)
                if m == 12:
                    own.settle()
                    tt(UC[:, 8:12, :], UC[:, 8:12, :], UC[:, 4:8, :], ALU.mult).then_inc(z_ready, 1)
            dve.wait_ge(root_ready, 1)
            nc.vector.reciprocal(RN[:, 1, :], RN[:, 0, :]).then_inc(rec_ready, 1)
            dve.wait_ge(zf_done, 1)
            for k in range(2):
                for n in range(4):
                    i, o = ((0, 0), (1, 1), (0, 1), (1, 0))[n]
                    own(tt(TM[:, n, :], HRI[:, i, k, :], DN[2 * o + k][:, :], ALU.mult))
                own.settle()
                own(tt(YRI[:, 0, k, :], TM[:, 0, :], TM[:, 1, :], ALU.subtract))
                ins = tt(YRI[:, 1, k, :], TM[:, 2, :], TM[:, 3, :], ALU.add)
                if k:
                    ins.then_inc(y_spec, 1)
                else:
                    own(ins)
                    own.settle()
            for c in range(HT):
                if c >= 2:
                    dve.wait_ge(mix_hh, c - 1)
                y = ymix[:, c % 2, :]
                own(nc.vector.tensor_scalar(y, UC[:, 8 + c, :], pcol("hy_bias", c), None, ALU.mult))
                own.settle()
                dve.wait_ge(yi_done, c + 1)
                own(stt(out=y, in0=DN[c][:, 0:L], scalar=hy_rnorm[:, c:c + 1], in1=y, op0=ALU.mult, op1=ALU.add))
                own.settle()
                tt(y, y, UC[:, c, :], ALU.mult).then_inc(ym_ready, 1)
                dve_mixed(dve, c)
            dve.wait_ge(bc_done, 1)
            dve.wait_ge(zt_ready, 1)
            dve.wait_ge(ym_ready, HT)
            for j in range(5):
                src = (bank[3], GU[1], GU[0])[j // 2][:, (j % 2) * L:(j % 2) * L + L]
                if j < 4:
                    stt(out=QN[:, j, :], in0=UQ[:, j, :], scalar=pcol("q_gain"), in1=src, op0=ALU.mult, op1=ALU.mult)\
                        .then_inc(qn_ready, 1)
                else:
                    own(nc.vector.tensor_scalar(UQ[:, j, :], UQ[:, j, :], pcol("k_gain"), HD ** -0.5, ALU.mult, ALU.mult))
                    own.settle()
                    tt(KN[:, 0, :], UQ[:, j, :], src, ALU.mult).then_inc(qn_ready, 1)
            for h in range(NQ):
                o = h % 2
                dve.wait_ge(sc_done, h + 1)
                if h >= 2:
                    dve.wait_ge(pt_done, h - 1)
                own(stt(out=SC[:, o, :, :], in0=dist[:, :, :], scalar=-SLOPES[h],
                        in1=DN[o][:, :].rearrange("p (a k) -> p a k", a=2), op0=ALU.mult, op1=ALU.add))
                own.settle()
                if h:
                    dve.wait_ge(ex_ready, h)
                own(nc.vector.tensor_reduce(amax, SC[:, o, :, :], AX.X, ALU.max))
                own.settle()
                nc.vector.tensor_scalar(anegm, amax, pcol("sink", h), -1.0, ALU.max, ALU.mult).then_inc(sc_ready, 1)
                dve.wait_ge(ex_ready, h + 1)
                own(tt(aden, asum, aes, ALU.add))
                own.settle()
                own(nc.vector.reciprocal(arden, aden))
                own.settle()
                for a in range(2):
                    last = nc.vector.tensor_scalar(SC[:, o, a, :], EX[:, o, a, :], arden[:, a:a + 1], None, ALU.mult)
                last.then_inc(pr_ready, 1)
                if o:
                    t = HT + h // 2
                    dve.wait_ge(pv_done, h + 1)
                    dve.wait_ge(mix_hh, t - 1)
                    nc.vector.tensor_copy(ymix[:, t % 2, :], GU[(h // 2) % 2][:, 0:L]).then_inc(ym_ready, 1)
                    dve_mixed(dve, t)
        LOADS = 80

        at[0] = 0
        R, K, V = (place(CT * L) for _ in range(3))
        LW = place(2 * CT * L)
        AG = place(2 * CT * L)
        h_at = at[0]
        H = place(CT * (L + 2)).rearrange("p (k t) -> p k t", t=L + 2)
        XX = XSQ
        XI = work[:, :, :, :].rearrange("p i o t -> p (i o) t")
        at[0] = h_at
        KK = place(CT * L + 16)[:, 0:CT * L]
        CI = place(2 * L)
        HID = CI.rearrange("p (i t) -> p i t", i=2)
        s2 = [0]

        def place2(n):
            s2[0] += n
            assert s2[0] <= 2 * CT * L
            return scan2[:, s2[0] - n:s2[0]]
        CE, E1, E2, KAT = (place2(2 * L) for _ in range(4))
        OPS = work[:, :, :, :].rearrange("p i o t -> p (i o t)")
        AR = OPS[:, 0:1024].rearrange("p (u i t) -> p u i t", i=2, t=CH)
        BE = OPS[:, 1024:1536]
        KD = OPS[:, 1536:2048]
        E3 = XSQ[:, 0:2, :].rearrange("p k t -> p (k t)")
        BB = XSQ[:, 2:4, :].rearrange("p k t -> p (k t)")
        RB = XSQ[:, 4, :]
        TMPK = XSQ[:, 5, :]
        sat = [0]

        def splace(n):
            sat[0] += n
            assert sat[0] <= 6 * BLK * 2
            return scan[:, sat[0] - n:sat[0]]

        def bd(n=NU):
            return splace(n * P).rearrange("p (u h s) -> p u h s", h=2, s=CH)

        def cf(n=NU):
            return splace(n * CH).rearrange("p (u s) -> p u s", s=CH)
        ALB, BEB, KAB, VB = bd(), bd(), bd(), bd(NCH)
        ABD, TBD, ZBD, BTB = bd(), bd(), bd(), bd()
        XLV, QBD = KAB, BEB
        TC, QC, ZC, AQ, BQ = cf(), cf(), cf(), cf(), cf()
        xsq_rest = XSQ[:, 6:8, :].rearrange("p k t -> p (k t)")
        tok_at = place2(1792)
        BTK = tok_at[:, 0:1024].rearrange("p (u c) -> p u c", c=P)
        KTK = splace(1024).rearrange("p (u c) -> p u c", c=P)
        VTK = splace(512).rearrange("p (u c) -> p u c", c=P)
        RC, UC1, SC1 = (xsq_rest[:, n * P:(n + 1) * P].rearrange("p (z v) -> p z v", z=2) for n in range(3))
        VC = tok_at[:, 1024:1280].rearrange("p (c v) -> p c v", v=CH)
        UBD = tok_at[:, 1280:1536].rearrange("p (z h v) -> p z h v", z=2, h=2)
        SBD = tok_at[:, 1536:1792].rearrange("p (z h v) -> p z h v", z=2, h=2)
        etot = small[:, 16:16 + NU]
        omk = small[:, 24:24 + CT]
        GH, GL = sb("GH", [P, 2, L], f32r), sb("GL", [P, 2, L], f32r)
        blockones, istack = ccols("blockones", P), ccols("istack", CH)
        BANKS = bank

        def mask(name, z):
            return ccols(name, CH, z * CH)

        scan_own = sem("scan_own")
        mx_hh, mx_hl = sem("mx_hh"), sem("mx_hl")
        xi_ready = sem("xi_ready")
        rkv_ready = sem("rkv_ready")
        lr_done = sem("lr_done")
        lr_ready = sem("lr_ready")
        lr_hi, lr_lo = sem("lr_hi"), sem("lr_lo")
        kk_sq, kk_ss, kk_max, kk_root, kk_rec, kk_bc, kk_ready = (sem(f"kk_{n}") for n in
                                                                "sq ss max root rec bc ready".split())
        ka_ready, c_ready, e_ready = sem("ka_ready"), sem("c_ready"), sem("e_ready")
        rb_ready, bo_done = sem("rb_ready"), sem("bo_done")
        opc_ready, bd_ready = sem("opc_ready"), sem("bd_ready")
        tr_done, tr_ready, a_done, a_ready = sem("tr_done"), sem("tr_ready"), sem("a_done"), sem("a_ready")
        xl_ready, z_done, zc_ready, zb_ready, d_done, t_ready = (sem(n) for n in
                                                               "xl_ready z_done zc_ready zb_ready d_done t_ready".split())
        r_done, r_ready, uu_done, uu_ready, y_done, s_done, s_ready, sb_ready = (
            sem(n) for n in "r_done r_ready uu_done uu_ready y_done s_done s_ready sb_ready".split())
        yt_ready = sem("yt_ready")
        gn_mean, gn_sq, gn_ss, gn_root, gn_rec, gn_bc, gn_af, gn_c = (sem(f"gn_{n}") for n in
                                                                      "mean sq ss root rec bc af c".split())
        g_done, gn_n = sem("g_done"), sem("gn_n")
        MIXES = [0, 2, 3, 1, 4, 5]

        def pe_mix1(pe):
            s0, n = S_RKV, 4
            pe_stats(pe, n).then_inc(st_ready, 1)
            q = 0
            for i in range(6):
                for m in (range(CT) if i < 3 else range(1 if i < 5 else 2)):
                    g = CT * i + m if i < 3 else 24 + i - 3 + m
                    s, b = s0 + g // 3, g % 3
                    if b == 0:
                        pe.wait_ge(lo_ready, s + 1)
                    if g >= 3:
                        pe.wait_ge(rkv_ready, g - 2)
                    wait = (lambda k: pe.wait_ge(mx_hl, CT * i + k + 1)) if m == 0 else None
                    project(UB[g % 3][:, 0:L], s % 2, b, wait=wait).then_inc(blocks_done, 1)
            for i in range(2):
                pe.wait_ge(lr_lo, i + 1)
                s, b = S_LORA + 1, 1 + i
                for m in range(CT):
                    for z in range(2):
                        if q >= 3:
                            pe.wait_ge(lr_ready, q - 2)
                        else:
                            pe.wait_ge(rkv_ready, 28)
                        r = slice(64 * z, 64 * z + 64)
                        ins = three(UB[q % 3][:, 0:L], b * BLK + m * P, s % 2, PH[r, i, :], PL[r, i, :], True, True,
                                    rows=r)
                        if m == CT - 1 and z == 1:
                            ins.then_inc(blocks_done, 1)
                        else:
                            ins.then_inc(lr_done, 1)
                        q += 1
            pe.wait_ge(kk_sq, CT)
            pe.wait_ge(lr_lo, 4)
            for j in range(CT):
                last = nc.tensor.matmul(ST[0:16, 0:L], sel[:, j, :], XSQ[:, j, :], start=j == 0, stop=j == CT - 1)
            last.then_inc(kk_ss, 1)
            pe.wait_ge(kk_rec, 1)
            for j in range(CT):
                last = nc.tensor.matmul(DN[j // 2][:, (j % 2) * L:(j % 2) * L + L], selt[:, j, :], RN[:, 1, :],
                                        start=True, stop=True)
            last.then_inc(kk_bc, 1)
            pe.wait_ge(kk_ready, 1)
            with pe.Fori(0, CT) as j:
                pe_scan(pe, j)
            pe_groupnorm(pe)

        def pe_scan(pe, j):
            mm, tr, B = nc.tensor.matmul, nc.tensor.transpose, BANKS

            def flat(a):
                return a.rearrange("p h s -> p (h s)")
            pe.wait_ge(bd_ready, 3 * j + 3)
            pe.wait_ge(opc_ready, 4 * j + 4)
            for c in range(NCH):
                tr(B[5][:, c * P:(c + 1) * P], flat(VB[:, c, :, :]), ident)
            for u in range(NU):
                last = tr(B[6 + u // NCH][:, (u % NCH) * P:(u % NCH + 1) * P], flat(KAB[:, u, :, :]), ident)
            last.then_inc(tr_done, 1)
            for u in range(NU):
                last = mm(B[0][:, u * CH:(u + 1) * CH], flat(ALB[:, u, :, :]), BE[:, u * CH:(u + 1) * CH], start=True, stop=True)
            last.then_inc(a_done, 1)
            for lhs, b0 in ((BEB, 1), (KAB, 3)):
                for u in range(NU):
                    last = mm(B[b0 + u // NCH][:, (u % NCH) * P:(u % NCH + 1) * P], flat(lhs[:, u, :, :]),
                              AR[:, u, :, :].rearrange("p i t -> p (i t)"), start=True, stop=True)
                last.then_inc(a_done, 1)
            pe.wait_ge(tr_ready, 2 * j + 1)
            for u in range(NU):
                last = tr(B[6 + u // NCH][:, (u % NCH) * P:(u % NCH + 1) * P], flat(BEB[:, u, :, :]), ident)
            last.then_inc(tr_done, 1)
            pe.wait_ge(rb_ready, j + 1)
            mm(B[5][:, 0:L], blockones, RB, start=True, stop=True).then_inc(bo_done, 1)
            for n in range(len(LEVELS)):
                for z in range(2):
                    pe.wait_ge(xl_ready, 10 * j + 2 * n + z + 1)
                    pe.wait_ge(t_ready, 12 * j + 2 * n + z + 1)
                    if n == 0:
                        pe.wait_ge(a_ready, 1 * j + 1)
                    for c in range(NCH):
                        u = z * NCH + c
                        last = mm(B[z][:, c * CH:(c + 1) * CH], flat(XLV[:, u, :, :]), QC[:, u, :], start=True, stop=True)
                    last.then_inc(z_done, 1)
                for z in range(2):
                    pe.wait_ge(zc_ready, 10 * j + 2 * n + z + 1)
                    for c in range(NCH):
                        u = z * NCH + c
                        last = mm(B[2 + z][:, c * CH:(c + 1) * CH], flat(TBD[:, u, :, :]), ZC[:, u, :], start=True, stop=True)
                    if n < len(LEVELS) - 1:
                        pe.wait_ge(zb_ready, 8 * j + 2 * n + z + 1)
                        for c in range(NCH):
                            u = z * NCH + c
                            last = mm(B[2 + z][:, L + c * CH:L + (c + 1) * CH], flat(ZBD[:, u, :, :]), TC[:, u, :],
                                      start=True, stop=True)
                    last.then_inc(d_done, 1)
            for i in range(NCH):
                us_ = (i, 2 * NCH - 1 - i)
                for z, u in enumerate(us_):
                    c = u % NCH
                    if i:
                        pe.wait_ge(s_ready, 6 * j + 2 * i)
                        mm(B[4][:, z * CH:(z + 1) * CH], flat(ALB[:, u, :, :]), SC1[:, z, :], start=True, stop=False)
                    elif z == 0:
                        pe.wait_ge(tr_ready, 2 * j + 2)
                        pe.wait_ge(t_ready, 12 * j + 12)
                        pe.wait_ge(bd_ready, 3 * j + 3)
                    last = mm(B[4][:, z * CH:(z + 1) * CH], flat(BTB[:, u, :, :]), VC[:, c, :], start=i == 0, stop=True)
                last.then_inc(r_done, 1)
                for z, u in enumerate(us_):
                    pe.wait_ge(r_ready, 4 * j + i + 1)
                    last = mm(B[5][:, z * CH:(z + 1) * CH], flat(QBD[:, u, :, :]), RC[:, z, :], start=True, stop=True)
                last.then_inc(uu_done, 1)
                if i < NCH - 1:
                    for z, u in enumerate(us_):
                        c = u % NCH
                        if i:
                            mm(B[6][:, z * CH:(z + 1) * CH], ident, SC1[:, z, :], start=True, stop=False)
                        mm(B[6][:, z * CH:(z + 1) * CH], KTK[:, u, :], VC[:, c, :], start=i == 0, stop=False)
                        pe.wait_ge(uu_ready, 12 * j + 3 * i + 1)
                        last = mm(B[6][:, z * CH:(z + 1) * CH], BTK[:, u, :], UC1[:, z, :], start=False, stop=True)
                    last.then_inc(s_done, 1)
                for z, u in enumerate(us_):
                    c = u % NCH
                    dst = B[z][:, c * CH:(c + 1) * CH]
                    mm(dst, VTK[:, c, :], BQ[:, u, :], start=True, stop=False)
                    if i:
                        pe.wait_ge(sb_ready, 3 * j + i)
                        mm(dst, flat(SBD[:, z, :, :]), AR[:, u, 1, :], start=False, stop=False)
                    pe.wait_ge(uu_ready, 12 * j + 3 * i + 3)
                    last = mm(dst, flat(UBD[:, z, :, :]), AQ[:, u, :], start=False, stop=True)
                last.then_inc(y_done, 1)

        def halves(fn):
            for h in range(2):
                last = fn(slice(HD * h, HD * h + HD), h)
            return last

        def tile_of(a, j, z=0, n=1):
            return a[:, bass.ds(z * CT * L + j * L, L)]

        def act_scan(act, j):
            A, cp, B = nc.scalar.activation, ACT.Copy, BANKS
            act.wait_ge(yt_ready, j + 1)
            for z in range(2):
                last = A(KAT[:, z * L:(z + 1) * L], tile_of(AG, j, z), ACT.Identity,
                         bias=small[:, bass.ds(24 + j, 1)], scale=par[:, bass.ds(COL["k_a"] + j, 1)])
            last.then_inc(ka_ready, 1)
            halves(lambda r, h: A(VB[r, :, h, :], V[r, bass.ds(j * L, L)].rearrange("p (c s) -> p c s", c=NCH), cp))\
                .then_inc(bd_ready, 1)
            act.wait_ge(c_ready, j + 1)
            ci = CI[:, :].rearrange("p (z c t) -> p z c t", z=2, c=NCH)
            for z in range(2):
                A(etot[:, z * NCH:(z + 1) * NCH], ci[:, z, :, (CH - 1) if z == 0 else 0], ACT.Exp, scale=-DECAY)
            A(E1[:, :], CE[:, :], ACT.Exp, scale=-DECAY).then_inc(e_ready, 1)
            A(E2[:, :], CI[:, :], ACT.Exp, scale=-DECAY).then_inc(e_ready, 1)
            A(E3, CI[:, :], ACT.Exp, scale=DECAY).then_inc(e_ready, 1)
            act.wait_ge(opc_ready, 4 * j + 1)
            halves(lambda r, h: A(ALB[r, :, h, :], AR[r, :, 0, :], cp)).then_inc(bd_ready, 1)
            act.wait_ge(opc_ready, 4 * j + 3)
            halves(lambda r, h: A(BEB[r, :, h, :], BE[r, :].rearrange("p (u t) -> p u t", u=NU), cp)).then_inc(bd_ready, 1)
            act.wait_ge(tr_done, 2 * j + 1)
            A(VTK[:, :, :], B[5][:, :].rearrange("p (c s) -> p c s", c=NCH), cp)
            halves(lambda r, h: A(VC[r, :, :], B[5][r, :].rearrange("p (c h s) -> p c h s", c=NCH, h=2)[:, :, h, :], cp))
            for z in range(2):
                last = A(KTK[:, z * NCH:(z + 1) * NCH, :], B[6 + z][:, :].rearrange("p (c s) -> p c s", c=NCH), cp)
            last.then_inc(tr_ready, 1)
            act.wait_ge(tr_done, 2 * j + 2)
            for z in range(2):
                last = A(BTK[:, z * NCH:(z + 1) * NCH, :], B[6 + z][:, :].rearrange("p (c s) -> p c s", c=NCH), cp)
            last.then_inc(tr_ready, 1)
            for n in range(len(LEVELS)):
                for z in range(2):
                    act.wait_ge(z_done, 10 * j + 2 * n + z + 1)
                    src = B[z][:, 0:L].rearrange("p (c s) -> p c s", c=NCH)
                    A(ZC[:, z * NCH:(z + 1) * NCH, :], src, cp).then_inc(zc_ready, 1)
                    if n < len(LEVELS) - 1:
                        halves(lambda r, h: A(ZBD[r, z * NCH:(z + 1) * NCH, h, :], src[r], cp)).then_inc(zb_ready, 1)
            act.wait_ge(e_ready, 3 * j + 1)
            for i in range(NCH):
                act.wait_ge(uu_done, 4 * j + i + 1)
                src = B[5][:, 0:P].rearrange("p (z v) -> p z v", z=2)
                act.wait_ge(uu_ready, 12 * j + 3 * i + 1)
                r0 = slice(0, HD)
                A(UBD[r0, :, 0, :], src[r0], cp).then_inc(uu_ready, 1)
                if i < NCH - 1:
                    act.wait_ge(s_done, 3 * j + i + 1)
                    for z, u in enumerate((i, 2 * NCH - 1 - i)):
                        A(SC1[:, z, :], B[6][:, z * CH:(z + 1) * CH], cp, scale=etot[:, u:u + 1]).then_inc(s_ready, 1)

        def dve_scan(dve, j, own):
            V_, B = nc.vector, BANKS
            tt, ts, stt = V_.tensor_tensor, V_.tensor_scalar, V_.scalar_tensor_tensor
            z2 = lambda a: a.rearrange("p (z t) -> p z t", z=2)
            zc = lambda a: a.rearrange("p (z c t) -> p z c t", z=2, c=NCH)
            Kj, Rj, Vj, KKj = (tile_of(a, j) for a in (K, R, V, KK))
            reset = ccols("reset", L)
            for z in range(2):
                own(V_.tensor_tensor_scan(out=(CI if z == 0 else CE)[:, z * L:(z + 1) * L], data0=reset,
                                          data1=tile_of(LW, j, z), initial=0.0, op0=ALU.mult, op1=ALU.add))
            own.settle()
            own(tt(CE[:, 0:L], CI[:, 0:L], tile_of(LW, j, 0), ALU.subtract))
            p1 = zc(CE)[:, 1]
            own(V_.tensor_copy(small[:, 32:36], p1[:, :, CH - 1]))
            own.settle()
            own(tt(p1, small[:, 32:36].rearrange("p (c o) -> p c o", o=1).broadcast_to([P, NCH, CH]), p1, ALU.subtract))
            own.settle()
            tt(CI[:, L:2 * L], CE[:, L:2 * L], tile_of(LW, j, 1), ALU.add).then_inc(c_ready, 1)
            dve.wait_ge(ka_ready, j + 1)
            for z in range(2):
                own(tt(KD[:, z * L:(z + 1) * L], KAT[:, z * L:(z + 1) * L], Kj, ALU.mult))
                own(tt(BB[:, z * L:(z + 1) * L], tile_of(AG, j, z), KKj, ALU.mult))
            own.settle()
            own(tt(TMPK, KD[:, 0:L], KD[:, L:2 * L], ALU.add))
            own.settle()
            stt(out=RB, in0=Rj, scalar=par[:, bass.ds(COL["r_k"] + j, 1)], in1=TMPK, op0=ALU.mult, op1=ALU.mult)\
                .then_inc(rb_ready, 1)
            dve.wait_ge(e_ready, 3 * j + 1)
            arz = AR.rearrange("p (z c) i t -> p z c i t", z=2)
            c4 = lambda a: a.rearrange("p (c t) -> p c t", c=NCH)
            for z in range(2):
                ins = stt(out=AR[:, z * NCH:(z + 1) * NCH, 0, :], in0=c4(KKj), scalar=-1.0, in1=c4(E1[:, z * L:(z + 1) * L]),
                          op0=ALU.mult, op1=ALU.mult)
            ins.then_inc(opc_ready, 1)
            dve.wait_ge(e_ready, 3 * j + 2)
            for z in range(2):
                ins = tt(AR[:, z * NCH:(z + 1) * NCH, 1, :], c4(Rj), c4(E2[:, z * L:(z + 1) * L]), ALU.mult)
            ins.then_inc(opc_ready, 1)
            dve.wait_ge(e_ready, 3 * j + 3)
            tt(BE, BB, E3, ALU.mult).then_inc(opc_ready, 1)
            u8 = lambda a: a.rearrange("p (u t) -> p u t", u=NU)
            halves(lambda r, h: tt(KAB[r, :, h, :], u8(KD)[r], u8(E3)[r], ALU.mult)).then_inc(opc_ready, 1)
            dve.wait_ge(a_done, 3 * j + 1)
            a_src = B[0][:, :].rearrange("p (u s) -> p u s", u=NU)
            halves(lambda r, h: own(V_.tensor_copy(ABD[r, :, h, :], a_src[r])))

            def spread(m, n=NCH):
                return m.rearrange("p (o s) -> p o s", o=1).broadcast_to([P, n, CH])
            for z in range(2):
                us_ = slice(z * NCH, (z + 1) * NCH)
                own(tt(TC[:, us_, :], a_src[:, us_, :], spread(mask("m1", z)), ALU.mult))
            own.settle()
            own(tt(TC[:, :, :], TC[:, :, :], spread(istack, NU), ALU.add))
            dve.wait_ge(a_done, 3 * j + 2)
            for z in range(2):
                us_ = slice(z * NCH, (z + 1) * NCH)
                src = B[1 + z][:, :].rearrange("p (c i s) -> p c i s", c=NCH, i=2)
                own(tt(QC[:, us_, :], src[:, :, 0, :], spread(mask("m1t", z)), ALU.mult))
                own(tt(AQ[:, us_, :], src[:, :, 1, :], spread(mask("incl", z)), ALU.mult))
            own.settle()
            for z in range(2):
                us_ = slice(z * NCH, (z + 1) * NCH)
                halves(lambda r, h: own(V_.tensor_copy(TBD[r, us_, h, :], TC[r, us_, :])))
                tt(QC[:, us_, :], QC[:, us_, :], spread(istack), ALU.add).then_inc(t_ready, 1)
            dve.wait_ge(a_done, 3 * j + 3)
            for z in range(2):
                us_ = slice(z * NCH, (z + 1) * NCH)
                src = B[3 + z][:, :].rearrange("p (c i s) -> p c i s", c=NCH, i=2)
                halves(lambda r, h: own(tt(BTB[r, us_, h, :], src[r, :, 0, :], spread(mask("strict", z))[r], ALU.mult)))
                ins = tt(BQ[:, us_, :], src[:, :, 1, :], spread(mask("incl", z)), ALU.mult)
                if z == 0:
                    own(ins)
            ins.then_inc(a_ready, 1)
            dve.wait_ge(bo_done, j + 1)
            own(stt(out=Kj, in0=B[5][:, 0:L], scalar=0.5, in1=Vj, op0=ALU.mult, op1=ALU.mult))
            for n in range(len(LEVELS)):
                for z in range(2):
                    us_ = slice(z * NCH, (z + 1) * NCH)
                    dve.wait_ge(d_done, 10 * j + 2 * n + z + 1)
                    dq = B[2 + z][:, 0:L].rearrange("p (c s) -> p c s", c=NCH)
                    dt = B[2 + z][:, L:2 * L].rearrange("p (c s) -> p c s", c=NCH)
                    dve.wait_ge(t_ready, 12 * j + 2 * n + z + 1)
                    if n < len(LEVELS) - 1:
                        own(tt(TC[:, us_, :], TC[:, us_, :], dt, ALU.add))
                        own.settle()
                        halves(lambda r, h: own(V_.tensor_copy(TBD[r, us_, h, :], TC[r, us_, :])))
                        tt(QC[:, us_, :], QC[:, us_, :], dq, ALU.add).then_inc(t_ready, 1)
                    else:
                        r0, r1 = slice(0, HD), slice(HD, P)
                        own(tt(QBD[r0, us_, 0, :], QC[r0, us_, :], dq[r0], ALU.add))
                        tt(QBD[r1, us_, 1, :], QC[r1, us_, :], dq[r1], ALU.add).then_inc(t_ready, 1)
            for i in range(NCH):
                dve.wait_ge(r_done, 4 * j + i + 1)
                V_.tensor_copy(RC[:, :, :], B[4][:, 0:P].rearrange("p (z v) -> p z v", z=2)).then_inc(r_ready, 1)
                dve.wait_ge(uu_done, 4 * j + i + 1)
                src = B[5][:, 0:P].rearrange("p (z v) -> p z v", z=2)
                V_.tensor_copy(UC1[:, :, :], src).then_inc(uu_ready, 1)
                r1 = slice(HD, P)
                dve.wait_ge(uu_ready, 12 * j + 3 * i + 2)
                V_.tensor_copy(UBD[r1, :, 1, :], src[r1]).then_inc(uu_ready, 1)
                if i < NCH - 1:
                    dve.wait_ge(s_ready, 6 * j + 2 * i + 2)
                    dve.wait_ge(y_done, 4 * j + i + 1)
                    own(V_.tensor_copy(SBD[0:HD, :, 0, :], SC1[0:HD, :, :]))
                    V_.tensor_copy(SBD[HD:P, :, 1, :], SC1[HD:P, :, :]).then_inc(sb_ready, 1)
            dve.wait_ge(y_done, 4 * j + 4)
            own(V_.tensor_copy(TMPK, B[0][:, 0:L]))
            own.settle()
            tt(Rj, TMPK, B[1][:, 0:L], ALU.add).then_inc(yt_ready, 1)

        def pool_scan(pool, j):
            for n in range(len(LEVELS)):
                for z in range(2):
                    us_ = slice(z * NCH, (z + 1) * NCH)
                    if n:
                        pool.wait_ge(z_done, 10 * j + 2 * (n - 1) + z + 1)
                    elif z == 0:
                        pool.wait_ge(a_ready, j + 1)
                        pool.wait_ge(tr_ready, 2 * j + 2)
                    lv = ccols("level", P, (z * len(LEVELS) + n) * P)
                    nc.gpsimd.tensor_tensor(XLV[:, us_, :, :].rearrange("p u h s -> p u (h s)"),
                                            ABD[:, us_, :, :].rearrange("p u h s -> p u (h s)"),
                                            lv.rearrange("p (o s) -> p o s", o=1).broadcast_to([P, NCH, P]), ALU.mult)\
                        .then_inc(xl_ready, 1)

        def act_mix1(act):
            s0 = S_RKV
            A = nc.scalar.activation
            act_root(act, 4, (st_ready, 2))
            for i in range(6):
                for k in range(CT):
                    act.wait_ge(xi_ready, CT * i + k + 1)
                    if i and k == 0:
                        act.wait_ge(blocks_done, 3 * s0 + (CT * i if i < 4 else 24 + i - 3))
                    A(HH[:, k, :], XI[:, k, :], ACT.Copy).then_inc(mx_hh, 1)
                for m in (range(CT) if i < 3 else range(1 if i < 5 else 2)):
                    g = CT * i + m if i < 3 else 24 + i - 3 + m
                    if g % 3 == 0 and s0 + g // 3 + 1 < S_O:
                        next_hi(act, s0 + g // 3 + 1)
                    act.wait_ge(blocks_done, 3 * s0 + g + 1)
                    src = UB[g % 3][:, 0:L]
                    if i < 3:
                        A((R, K, V)[i][:, m * L:(m + 1) * L], src, ACT.Copy).then_inc(rkv_ready, 1)
                    elif i == 3:
                        A(HID[:, 0, :], src, ACT.Tanh).then_inc(rkv_ready, 1)
                        act.wait_ge(rkv_ready, g + 1)
                        A(PH[:, 0, :], HID[:, 0, :], ACT.Copy).then_inc(lr_hi, 1)
                    elif i == 4:
                        A(HID[:, 1, :], src, ACT.Copy).then_inc(rkv_ready, 1)
                        act.wait_ge(rkv_ready, g + 1)
                        A(PH[:, 1, :], HID[:, 1, :], ACT.Copy).then_inc(lr_hi, 1)
                    else:
                        act.wait_ge(lr_lo, m + 1)
                        A(HID[:, m, :], src, ACT.Sigmoid).then_inc(rkv_ready, 1)
                        act.wait_ge(rkv_ready, g + 1)
                        A(GH[:, m, :], HID[:, m, :], ACT.Copy).then_inc(lr_hi, 1)
            q = 0
            for i, dst in enumerate((LW, AG)):
                for m in range(CT):
                    for z in range(2):
                        if m == CT - 1 and z == 1:
                            act.wait_ge(blocks_done, 3 * (S_LORA + 1) + 2 + i)
                        else:
                            act.wait_ge(lr_done, q + 1 - i)
                        A(dst[:, (z * CT + m) * L:(z * CT + m + 1) * L], UB[q % 3][:, 0:L], ACT.Sigmoid,
                          bias=pcol(("w0", "a0")[i], z * CT + m)).then_inc(lr_ready, 1)
                        q += 1
            for j in range(CT):
                A(XSQ[:, j, :], K[:, j * L:(j + 1) * L], ACT.Square, scale=pcol("k_k", j)).then_inc(kk_sq, 1)
            act.wait_ge(kk_max, 1)
            A(RN[:, 0, :], HID[0:16, 0, :], ACT.Sqrt).then_inc(kk_root, 1)
            act.wait_ge(kk_ready, 1)
            with act.Fori(0, CT) as j:
                act_scan(act, j)
            act.wait_ge(yt_ready, CT + 1)
            next_hi(act, S_O)
            next_hi(act, S_O + 1)
            act_groupnorm(act)

        def dve_mix1(dve, own):
            V_ = nc.vector
            tt, ts, stt = V_.tensor_tensor, V_.tensor_scalar, V_.scalar_tensor_tensor
            dve_root(dve, 4)
            own(V_.memset(H[:, :, 0:1], 0.0))
            own(V_.memset(H[:, :, L + 1:L + 2], 0.0))
            dve.wait_ge(rstd_ready, 5)
            for k in range(CT):
                own(stt(out=H[:, k, 1:L + 1], in0=X[:, k, :], scalar=pcol("mix_norm", CT + k), in1=rstd[:, :],
                        op0=ALU.mult, op1=ALU.mult))
            own.settle()
            own(tt(XX[:, :, :], H[:, :, 0:L], H[:, :, 2:L + 2], ALU.add))
            own.settle()
            own(stt(out=XX[:, :, :], in0=XX[:, :, :], scalar=0.5, in1=H[:, :, 1:L + 1], op0=ALU.mult, op1=ALU.subtract))
            own.settle()

            def mix(i):
                if i:
                    dve.wait_ge(mx_hl, CT * i)
                for k in range(CT):
                    stt(out=XI[:, k, :], in0=XX[:, k, :], scalar=pcol("mu", MIXES[i] * CT + k), in1=H[:, k, 1:L + 1],
                        op0=ALU.mult, op1=ALU.add).then_inc(xi_ready, 1)
            mix(0)
            for i in range(6):
                for k in range(CT):
                    dve.wait_ge(mx_hh, CT * i + k + 1)
                    tt(HL[:, k, :], XI[:, k, :], HH[:, k, :].bitcast(fp32), ALU.subtract).then_inc(mx_hl, 1)
                if i < 5:
                    mix(i + 1)
                for m in (range(CT) if i < 3 else range(1 if i < 5 else 2)):
                    g = CT * i + m if i < 3 else 24 + i - 3 + m
                    if g % 3 == 0 and S_RKV + g // 3 + 1 < S_O:
                        next_lo(dve, S_RKV + g // 3 + 1)
                    if i >= 3:
                        dve.wait_ge(lr_hi, g - 23)
                        hi, lo, o = (PH, PL, i - 3) if i < 5 else (GH, GL, m)
                        tt(lo[:, o, :], HID[:, o, :], hi[:, o, :].bitcast(fp32), ALU.subtract).then_inc(lr_lo, 1)
            dve.wait_ge(kk_ss, 1)
            ts(HID[0:16, 0, :], ST[0:16, 0:L], 1e-24, None, ALU.max).then_inc(kk_max, 1)
            dve.wait_ge(kk_root, 1)
            V_.reciprocal(RN[:, 1, :], RN[:, 0, :]).then_inc(kk_rec, 1)
            own(ts(omk, par[:, COL["k_a"]:COL["k_a"] + CT], -1.0, 1.0, ALU.mult, ALU.add))
            for a in (ALB, BEB, KAB, ABD, TBD, ZBD, BTB):
                own(V_.memset(a[:, :, :, :], 0.0))
            own(V_.memset(VB[:, :, :, :], 0.0))
            own(V_.memset(UBD[:, :, :, :], 0.0))
            own(V_.memset(SBD[:, :, :, :], 0.0))
            dve.wait_ge(kk_bc, 1)
            for j in range(CT):
                own(stt(out=KK[:, j * L:(j + 1) * L], in0=K[:, j * L:(j + 1) * L], scalar=pcol("k_k", j),
                        in1=DN[j // 2][:, (j % 2) * L:(j % 2) * L + L], op0=ALU.mult, op1=ALU.mult))
            own.settle()
            V_.memset(small[:, 36:37], 0.0).then_inc(yt_ready, 1)
            V_.memset(small[:, 37:38], 0.0).then_inc(kk_ready, 1)
            with dve.Fori(0, CT) as j:
                body = Own(dve, scan_own, j * SCAN_OWN)
                dve_scan(dve, j, body)
                assert body.n == SCAN_OWN, body.n
            next_lo(dve, S_O)
            next_lo(dve, S_O + 1)
            dve_groupnorm(dve, own)

        def ytile(j):
            return R[:, j * L:(j + 1) * L]

        def half_bank(bs, j):
            return bs[j // 2][:, (j % 2) * L:(j % 2) * L + L]
        MB = [bank[0], bank[1], bank[2], bank[3]]

        def pe_groupnorm(pe):
            for j in range(CT):
                pe.wait_ge(yt_ready, CT + 1)
                nc.tensor.matmul(half_bank(MB, j), blockones, ytile(j), start=True, stop=True).then_inc(gn_mean, 1)
            for j in range(CT):
                pe.wait_ge(lo_ready, S_O + 1)
                for i in range(2):
                    last = three(half_bank(DN, j), i * BLK + j * P, S_O % 2, GH[:, i, :], GL[:, i, :], i == 0, i == 1)
                    if j == CT - 1:
                        last.then_inc(blocks_done, 1)
            for j in range(CT):
                pe.wait_ge(gn_sq, max(j + 1, 2))
                last = nc.tensor.matmul(bank[0][0:16, 0:L], sel[:, j, :], XSQ[:, j, :], start=j == 0, stop=j == CT - 1)
            last.then_inc(gn_ss, 1)
            pe.wait_ge(gn_rec, 1)
            for j in range(CT):
                if j >= 2:
                    pe.wait_ge(gn_n, j - 1)
                nc.tensor.matmul(bank[j % 2][:, L:2 * L], selt[:, j, :], RN[:, 1, :], start=True, stop=True).then_inc(gn_bc, 1)
            for m in range(CT):
                g = m + 2
                s, b = S_O + g // 3, g % 3
                if b == 0:
                    pe.wait_ge(lo_ready, s + 1)
                if m == 0:
                    pe.wait_ge(gn_n, CT)
                for k in range(CT):
                    if m == 0:
                        pe.wait_ge(mix_hl, CT + k + 1)
                    last = three(half_bank(MB, m), b * BLK + k * P, s % 2, HH[:, k, :], HL[:, k, :], k == 0, k == CT - 1)
                    if m == CT - 1 and k in (2, 5):
                        last.then_inc(blocks_done, 1)
                last.then_inc(blocks_done, 1)

        def act_groupnorm(act):
            A = nc.scalar.activation
            for j in range(CT):
                act.wait_ge(gn_c, j + 1)
                A(XSQ[:, j, :], ytile(j), ACT.Square).then_inc(gn_sq, 1)
            act.wait_ge(gn_ss, 1)
            A(RN[:, 0, :], bank[0][0:16, 0:L], ACT.Sqrt, bias=eps6[0:16, 1:2], scale=1.0 / HD).then_inc(gn_root, 1)
            for j in range(CT):
                act.wait_ge(gn_n, j + 1)
                A(ytile(j), ytile(j), ACT.Identity, bias=pcol("ln_b", j), scale=pcol("ln_w", j)).then_inc(gn_af, 1)
                act_mixed(act, j, CT)
            for s in (2, 3, 4):
                next_hi(act, S_O + s)

        def dve_groupnorm(dve, own):
            tt, stt = nc.vector.tensor_tensor, nc.vector.scalar_tensor_tensor
            for j in range(CT):
                dve.wait_ge(gn_mean, 2 * (j // 2) + 2)
                stt(out=ytile(j), in0=half_bank(MB, j), scalar=-1.0 / HD, in1=ytile(j), op0=ALU.mult, op1=ALU.add)\
                    .then_inc(gn_c, 1)
            dve.wait_ge(gn_root, 1)
            nc.vector.reciprocal(RN[:, 1, :], RN[:, 0, :]).then_inc(gn_rec, 1)
            dve.wait_ge(blocks_done, 3 * S_O + 2)
            for j in range(CT):
                dve.wait_ge(gn_bc, j + 1)
                tt(ytile(j), ytile(j), bank[j % 2][:, L:2 * L], ALU.mult).then_inc(gn_n, 1)
                dve.wait_ge(gn_af, j + 1)
                own(tt(ytile(j), ytile(j), K[:, j * L:(j + 1) * L], ALU.add))
                own.settle()
                if j >= 2:
                    dve.wait_ge(mix_hh, CT + j - 1)
                tt(ymix[:, j % 2, :], ytile(j), half_bank(DN, j), ALU.mult).then_inc(ym_ready, 1)
                dve_mixed(dve, j, CT)
            for s in (2, 3, 4):
                next_lo(dve, S_O + s)
            for part, (js, done) in enumerate((((0, 1), 6), ((2,), 8), ((3,), 12))):
                dve.wait_ge(blocks_done, 3 * S_O + done)
                for j in js:
                    last = tt(X[:, 2 * j:2 * j + 2, :], MB[j][:, :].rearrange("p (a n) -> p a n", a=2),
                              X[:, 2 * j:2 * j + 2, :], ALU.add)
                last.then_inc(x_ready, 1)
        @block.sync
        def _(sp):
            for dst, src in ((hcst, hconst_d), (fw, fw_d), (par[:, :], par_d), (cst[:, :], const_d), (X[:, :, :], xT)):
                sp.dma_start(dst, src).then_inc(loaded, 16)
            for s in range(2):
                sp.dma_start(raw[:, s, :], stream[s]).then_inc(raw_full[s], 16)
            n = (STEPS - 2) // 2
            if n:
                with sp.Fori(0, n) as i:
                    for u in range(2):
                        sp.wait_ge(lo_ready, 2 * i + (u + 1))
                        sp.dma_start(raw[:, u, :], stream[2 * i + (2 + u)]).then_inc(raw_full[u], 16)
            for s in range(2 + 2 * n, STEPS):
                sp.wait_ge(lo_ready, s - 1)
                sp.dma_start(raw[:, s % 2, :], stream[s]).then_inc(raw_full[s % 2], 16)
            sp.wait_ge(x_ready, 3 * len(NORM_TILES))
            sp.dma_start(out, X[:, :, :]).then_inc(stored, 16)
            sp.wait_ge(stored, 16)

        @block.tensor
        def _(pe):
            pe.wait_ge(loaded, LOADS)
            pe_filter(pe)
            pe_ffn(pe, 0, S_FFN[0], 0)
            pe_mix0(pe)
            pe_ffn(pe, 2, S_FFN[1], FT)
            pe_ffn(pe, 3, S_FFN[2], 2 * FT)
            pe_mix1(pe)
            pe_ffn(pe, 5, S_FFN[3], 3 * FT)

        @block.scalar
        def _(act):
            act.wait_ge(loaded, LOADS)
            act_filter(act)
            next_hi(act, 0)
            act_norm_in(act, 0, ("ffn1_norm", 0))
            act_ffn(act, 0, S_FFN[0], 0)
            act_norm_in(act, 1, ("mix_norm", 0))
            act_mix0(act)
            for s in (1, 2, 3):
                next_hi(act, S_OUT + s)
            act_norm_in(act, 2, ("ffn2_norm", 0))
            act_ffn(act, 2, S_FFN[1], FT)
            act_norm_in(act, 3, ("ffn1_norm", CT))
            act_ffn(act, 3, S_FFN[2], 2 * FT)
            act.wait_ge(x_ready, 12)
            act_squares(act)
            act_mix1(act)
            act_norm_in(act, 5, ("ffn2_norm", CT))
            act_ffn(act, 5, S_FFN[3], 3 * FT)

        @block.gpsimd
        def _(pool):
            pool.wait_ge(kk_ready, 1)
            with pool.Fori(0, CT) as j:
                pool_scan(pool, j)

        @block.vector
        def _(dve):
            own = Own(dve, dve_own)
            nc.vector.memset(eps6[:, 0:1], 1e-6)
            nc.vector.memset(eps6[:, 1:2], 64e-5).then_inc(eps_ready, 1)
            dve.wait_ge(loaded, LOADS)
            dve_filter(dve, own)
            next_lo(dve, 0)
            dve_norm_in(dve, 0, ("ffn1_norm", 0))
            dve_ffn(dve, 0, S_FFN[0], 0)
            dve_residual(dve, S_FFN[0] + FT, 0.5)
            dve_norm_in(dve, 1, ("mix_norm", 0))
            dve_mix0(dve, own)
            for s in (1, 2, 3):
                next_lo(dve, S_OUT + s)
            dve_out(dve, S_OUT)
            dve_norm_in(dve, 2, ("ffn2_norm", 0))
            dve_ffn(dve, 2, S_FFN[1], FT)
            dve_residual(dve, S_FFN[1] + FT, 0.5)
            dve_norm_in(dve, 3, ("ffn1_norm", CT))
            dve_ffn(dve, 3, S_FFN[2], 2 * FT)
            dve_residual(dve, S_FFN[2] + FT, 0.5)
            dve_mix1(dve, own)
            dve_norm_in(dve, 5, ("ffn2_norm", CT))
            dve_ffn(dve, 5, S_FFN[3], 3 * FT)
            dve_residual(dve, S_FFN[3] + FT, 0.5)


def _consts():
    c = np.zeros((P, NCONST), np.float32)

    def put(name, a, off=0):
        c[:, CC[name] + off:CC[name] + off + a.shape[1]] = a
    r = np.arange(P)
    put("ident", np.eye(P))
    put("istack", np.tile(np.eye(CH), (2, 1)))
    put("blockones", (r[:, None] // HD == r[None, :] // HD) * 1.0)
    put("ones", np.ones((P, P)))
    for j in range(CT):
        put("sel", (np.arange(16)[None, :] == 2 * j + r[:, None] // HD) * 1.0, 16 * j)
        put("selt", (r[:, None] == 2 * j + r[None, :] // HD) * 1.0, P * j)
    put("perm", (r[:, None] == (r[None, :] + HD) % P) * 1.0)
    t, s = np.arange(CH)[:, None], np.arange(CH)[None, :]
    for z in range(2):
        pair = (t // 2 == s // 2) & ((t > s) if z == 0 else (t < s))
        before = (s < t) if z == 0 else (s > t)
        put("m1", np.tile(pair * 1.0, (2, 1)), z * CH)
        put("m1t", np.tile(pair.T * 1.0, (2, 1)), z * CH)
        put("strict", np.tile(before.T * 1.0, (2, 1)), z * CH)
        put("incl", np.tile((before | (s == t)).T * 1.0, (2, 1)), z * CH)
        for n, b in enumerate(LEVELS):
            m = (t // (2 * b) == s // (2 * b)) & ((t // b > s // b) if z == 0 else (t // b < s // b))
            put("level", np.kron(np.eye(2), m * 1.0), (z * len(LEVELS) + n) * P)
    put("reset", np.tile((np.arange(L) % CH != 0) * 1.0, (P, 1)))
    return c


def _hconsts():
    c = np.zeros((P, NHC), np.float32)

    def put(name, a):
        c[:, HC[name]:HC[name] + 2 * a.shape[1]] = a.reshape(2, P, -1).transpose(1, 0, 2).reshape(P, -1)
    t = np.arange(L, dtype=np.float64)
    theta = 2 * np.pi * (t + 0.5) / (2 * L)
    put("cos", np.cos(t[:, None] * theta[None, :]))
    put("sin", np.sin(t[:, None] * theta[None, :]))
    put("icos", np.cos(theta[:, None] * t[None, :]) / L)
    put("isin", np.sin(theta[:, None] * t[None, :]) / L)
    f32 = np.float32
    tt = (t.astype(f32) / f32(L - 1)).astype(f32)
    deltas = np.abs(np.linspace(math.log(1e-2) / 1.5, math.log(1e-2) / 0.3, 512).astype(f32))
    put("window", np.exp((-tt[:, None] * deltas[None, :]).astype(np.float64)))
    d = np.abs(t[:, None] - t[None, :])
    put("dist", np.where(d <= 128, d, 1e30))
    bands = (FILTER_EMB - 1) // 2
    freqs = np.linspace(1e-4, bands - 1, bands).astype(f32)
    ang = (f32(2.0 * math.pi / L) * t.astype(f32)[:, None] * freqs[None, :]).astype(np.float64)
    feat = np.concatenate([tt[:, None], np.cos(ang), -np.sin(ang)], axis=1)
    c[:FILTER_EMB, HC["feat"]:HC["feat"] + L] = feat.T
    return c


def _blocks(i):
    st = np.zeros((STEPS, P, 3, BLK), np.float32)

    def col(w, m, width=P):
        b = np.zeros((P, CT, P), np.float32)
        b[:, :, :width] = w[:, m * P:m * P + width].reshape(CT, P, width).transpose(1, 0, 2)
        return b.reshape(P, BLK)
    for n, (name, layer) in enumerate((("ffn1", 0), ("ffn2", 0), ("ffn1", 1), ("ffn2", 1))):
        g, u, d = (i[f"{name}_{k}"][layer] for k in ("wg", "wu", "wd"))
        for f in range(FT):
            st[S_FFN[n] + f, :, 0] = col(g, f)
            st[S_FFN[n] + f, :, 1] = col(u, f)
            st[S_FFN[n] + f + 1, :, 2 if f < FT - 1 else 0] = d[f * P:(f + 1) * P]

    def lay(s0, blocks):
        for k, b in enumerate(blocks):
            st[s0 + k // 3, :, k % 3] = b
    lay(S_IN, [col(i["ab_w_in"][0], m) for m in range(18)])
    lay(S_OUT, [col(i["ab_w_out"][0], m) for m in range(CT)])
    lay(S_RKV, [col(i[f"rw_w_{k}"][0], m) for k in "rkv" for m in range(CT)])
    both = lambda w: np.concatenate([w[0], w[1]], axis=-1)
    g1, g2 = i["rw_g1"][0], i["rw_g2"][0]
    g2b = np.zeros((P, C), np.float32)
    g2b[:LORA_G - P] = g2[P:]
    lay(S_LORA, [col(both(i["rw_w1"][0]), 0), col(both(i["rw_a1"][0]), 0), col(g1, 0),
                 col(g1, 1, LORA_G - P), i["rw_w2"][0].reshape(P, C), i["rw_a2"][0].reshape(P, C)])
    lay(S_O, [g2[:P], g2b] + [col(i["rw_w_o"][0], m) for m in range(CT)])
    return st.reshape(STEPS, P, 3 * BLK)


def _params(i):
    c = np.zeros((P, NPAR), np.float32)

    def put(name, a, off=0):
        a = a.reshape(-1, P).T
        c[:, COL[name] + off:COL[name] + off + a.shape[1]] = a
    for n in ("ffn1_norm", "mix_norm", "ffn2_norm"):
        put(n, i[n])
    put("conv_w", i["ab_conv_w"][0])
    put("conv_b", i["ab_conv_b"][0])
    put("hy_bias", i["hy_bias"][0])
    for n in ("mu", "w0", "a0", "k_k", "k_a", "r_k", "ln_w", "ln_b"):
        put(n, i["rw_" + n][0])
    c[:, COL["q_gain"]] = np.tile(i["attn_q_norm"][0], 2)
    c[:, COL["k_gain"]] = np.tile(i["attn_k_norm"][0], 2)
    c[:, COL["sink"]:COL["sink"] + NQ] = np.broadcast_to(i["attn_sink"][0], (P, NQ))
    for n in range(3):
        c[:FILTER_ORDER, COL["f_b"] + n] = i[f"hy_f{n + 1}_b"][0]
    c[:FILTER_ORDER, COL["freq"]] = i["hy_sin_freq"][0]
    return c


def _filter_weights(i):
    w = np.zeros((P, NFW), np.float32)
    w[:FILTER_EMB, :FILTER_ORDER] = i["hy_f1_w"][0]
    w[:FILTER_ORDER, FILTER_ORDER:2 * FILTER_ORDER] = i["hy_f2_w"][0]
    w[:FILTER_ORDER, 2 * FILTER_ORDER:3 * FILTER_ORDER] = i["hy_f3_w"][0]
    w[:FILTER_ORDER, 3 * FILTER_ORDER:] = i["hy_f4_w"][0]
    return w


def _channel_major(x):
    return np.ascontiguousarray(x.reshape(L, CT, P).transpose(2, 1, 0))


def _arrays(inputs):
    i = {k: np.asarray(v) for k, v in inputs.items()}
    return {"xT_in": _channel_major(i["x"][0]), "stream_in": _blocks(i), "par_in": _params(i), "const_in": _consts(),
            "hconst_in": _hconsts(), "fw_in": _filter_weights(i)}


def kernel(**inputs):
    import concourse.bacc as bacc
    from concourse.bass_utils import run_bass_kernel_spmd

    nc = bacc.Bacc("TRN2", target_bir_lowering=False, num_devices=1)
    arrays = _arrays(inputs)
    io = [nc.dram_tensor(n, a.shape, mybir.dt.float32, kind="ExternalInput").ap() for n, a in arrays.items()]
    io.append(nc.dram_tensor("out", (P, CT, L), mybir.dt.float32, kind="ExternalOutput").ap())
    build(nc, io)
    r = run_bass_kernel_spmd(nc, [arrays], core_ids=[0])
    y = np.asarray(r.results[0]["out"])
    return np.ascontiguousarray(y.transpose(2, 1, 0)).reshape(1, L, C)
```

```python
import math
from contextlib import ExitStack

import numpy as np
import concourse.bass as bass
from concourse import mybir

P = 128
C = 1024
L = 256
CT = C // P
F = 2816
FT = F // P
HT = 4
NQ, NKV, HD = 8, 2, 64
LORA_G = 160
CH = 64
NCH = L // CH
NU = 2 * NCH
BLK = CT * P
FILTER_EMB, FILTER_ORDER = 33, 64
DECAY = math.exp(-0.5)

FFN_STEPS = FT + 1
IN_STEPS, OUT_STEPS, RKV_STEPS, LORA_STEPS, O_STEPS = 6, 3, 8, 2, 4
SCAN_OWN = 48
S_FFN = [0, 0, 0, 0]
S_FFN[0] = 0
S_IN = FFN_STEPS
S_OUT = S_IN + IN_STEPS
S_FFN[1] = S_OUT + OUT_STEPS
S_FFN[2] = S_FFN[1] + FFN_STEPS
S_RKV = S_FFN[2] + FFN_STEPS
S_LORA = S_RKV + RKV_STEPS
S_O = S_LORA + LORA_STEPS
S_FFN[3] = S_O + O_STEPS
STEPS = S_FFN[3] + FFN_STEPS


def blocks_in(s):
    for s0 in S_FFN:
        if s == s0:
            return 2
        if s == s0 + FT:
            return 1
    return {S_OUT + 2: 2, S_O + 3: 1}.get(s, 3)


_names = [("ffn1_norm", 2 * CT), ("mix_norm", 2 * CT), ("ffn2_norm", 2 * CT), ("conv_w", 3 * 12), ("conv_b", 12),
          ("hy_bias", HT), ("mu", 6 * CT), ("w0", 2 * CT), ("a0", 2 * CT), ("k_k", CT), ("k_a", CT), ("r_k", CT),
          ("ln_w", CT), ("ln_b", CT), ("q_gain", 1), ("k_gain", 1), ("sink", NQ), ("f_b", 3), ("freq", 1)]
COL = {}
_at = 0
for _n, _w in _names:
    COL[_n] = _at
    _at += _w
NPAR = _at
LEVELS = [2, 4, 8, 16, 32]
ARENA = 18390

_cn = [("ident", P), ("istack", CH), ("blockones", P), ("ones", P), ("sel", CT * 16), ("selt", CT * P), ("perm", P),
       ("first", 2 * CH), ("first_incl", 2 * P), ("strict_incl", 2 * P), ("level", len(LEVELS) * 2 * CH), ("reset", L)]
CC = {}
_at = 0
for _n, _w in _cn:
    CC[_n] = _at
    _at += _w
NCONST = _at
_hn = [("cos", 2 * L), ("sin", 2 * L), ("icos", 2 * L), ("isin", 2 * L), ("window", 2 * 512), ("dist", 2 * L),
       ("feat", L)]
HC = {}
_at = 0
for _n, _w in _hn:
    HC[_n] = _at
    _at += _w
NHC = _at
NFW = 3 * FILTER_ORDER + 2 * 512


def build(nc, io):
    fp32 = mybir.dt.float32
    f32r = mybir.dt.float32r
    ALU = mybir.AluOpType
    ACT = mybir.ActivationFunctionType
    AX = mybir.AxisListType
    xT, stream, par_d, const_d, hconst_d, fw_d, out = io
    ctx = ExitStack()
    with ctx:
        def sb(name, shape, dt=fp32):
            return ctx.enter_context(nc.sbuf_tensor(name, shape, dt))

        def sem(name):
            return ctx.enter_context(nc.semaphore(name))

        X = sb("X", [P, CT, L])
        h_offset = nc.sbuf_base
        HH = sb("HH", [P, CT, L], f32r)
        HL = sb("HL", [P, CT, L], f32r)
        XSQ = sb("XSQ", [P, CT, L])
        raw = sb("raw", [P, 2, 3 * BLK])
        w_offset = nc.sbuf_base
        WH = sb("WH", [P, 2, 3 * BLK], f32r)
        WL = sb("WL", [P, 2, 3 * BLK], f32r)
        PH = sb("PH", [P, 2, L], f32r)
        PL = sb("PL", [P, 2, L], f32r)
        work = sb("work", [P, 4, 2, L])
        prod, gs, us, sg = (work[:, n, :, :] for n in range(4))
        std = sb("std", [P, L])
        rstd = sb("rstd", [P, L])
        par = sb("par", [P, NPAR])
        cst = sb("cst", [P, NCONST])

        scan = nc.alloc_sbuf_tensor_at("scan", [P, 4 * 3 * BLK], fp32, offset=w_offset)
        scan2 = nc.alloc_sbuf_tensor_at("scan2", [P, 2 * CT * L], fp32, offset=h_offset)

        bank = [ctx.enter_context(nc.psum_tensor(f"bank{i}", [P, 512], fp32)) for i in range(8)]
        GU = bank[0:2]
        ST = bank[2]
        DN = bank[4:8]

        def pcol(name, i=0):
            return par[:, COL[name] + i:COL[name] + i + 1]

        def ccols(name, n, off=0):
            return cst[:, CC[name] + off:CC[name] + off + n]

        ones = ccols("ones", P)

        raw_full = [sem("raw_full0"), sem("raw_full1")]
        hi_ready = sem("hi_ready")
        lo_ready = sem("lo_ready")
        blocks_done = sem("blocks_done")
        loaded = sem("loaded")
        hh_ready = sem("hh_ready")
        hl_ready = sem("hl_ready")
        sq_ready = sem("sq_ready")
        std_ready = sem("std_ready")
        rstd_ready = sem("rstd_ready")
        gs_ready = sem("gs_ready")
        sg_ready = sem("sg_ready")
        prod_ready = sem("prod_ready")
        ph_ready = sem("ph_ready")
        pl_ready = sem("pl_ready")
        x_ready = sem("x_ready")
        stored = sem("stored")
        block = ctx.enter_context(nc.Block())

        def split_hi(act, s, width=3 * BLK, slot=None, uses=None):
            slot = s % 2 if slot is None else slot
            act.wait_ge(raw_full[slot], 16 * (s // 2 + 1) if uses is None else uses)
            act.wait_ge(blocks_done, 3 * s - 3) if not (isinstance(s, int) and s < 2) else None
            nc.scalar.activation(WH[:, slot, :width], raw[:, slot, :width], ACT.Copy).then_inc(hi_ready, 1)

        def split_lo(dve, s, width=3 * BLK, slot=None):
            slot = s % 2 if slot is None else slot
            dve.wait_ge(hi_ready, s + 1)
            nc.vector.tensor_tensor(WL[:, slot, :width], raw[:, slot, :width],
                                    WH[:, slot, :width].bitcast(fp32), ALU.subtract).then_inc(lo_ready, 1)

        def next_hi(act, s):
            if s < STEPS:
                split_hi(act, s, blocks_in(s) * BLK)

        def next_lo(dve, s):
            if s < STEPS:
                split_lo(dve, s, blocks_in(s) * BLK)

        def three(out_ap, lo_off, slot, xh, xl, start, stop, rows=slice(0, P), m=P, **kw):
            wh = WH[rows, slot, lo_off:lo_off + m]
            wl = WL[rows, slot, lo_off:lo_off + m]
            nc.tensor.matmul(out_ap, wh, xh, start=start, stop=False, **kw)
            nc.tensor.matmul(out_ap, wh, xl, start=False, stop=False, **kw)
            return nc.tensor.matmul(out_ap, wl, xh, start=False, stop=stop, **kw)

        def project(out_ap, slot, b, inp=None, wait=None):
            xh, xl = inp if inp is not None else (HH, HL)
            for k in range(CT):
                if wait is not None:
                    wait(k)
                last = three(out_ap, b * BLK + k * P, slot, xh[:, k, :], xl[:, k, :], k == 0, k == CT - 1)
            return last

        def pe_down(pe, slot, b, par_, first, last=False):
            for m in range(CT):
                dst = DN[m // 2][:, (m % 2) * L:(m % 2) * L + L]
                w = b * BLK + m * P
                a, c_ = PH[:, par_, :], PL[:, par_, :]
                ins = three(dst, w, slot, a, c_, first and m % 2 == 0, last, skip_group_check=True)
                if last and m in (3, 5):
                    ins.then_inc(blocks_done, 1)
            ins.then_inc(blocks_done, 1)

        def pe_ffn(pe, n, s0, q0):
            p0 = s0 % 2
            h0 = NORM_TILES[n]
            pe.wait_ge(lo_ready, s0 + 1)

            def wait_h(k):
                pe.wait_ge(hl_ready, h0 + k + 1)
            project(GU[0][:, 0:L], p0, 0, wait=wait_h).then_inc(blocks_done, 1)
            project(GU[0][:, L:2 * L], p0, 1).then_inc(blocks_done, 1)
            pe_stats(pe, n).then_inc(blocks_done, 1)

            def step(s, f, slot, first=False):
                pe.wait_ge(lo_ready, s + 1)
                if not (isinstance(f, int) and f < 2):
                    pe.wait_ge(gs_ready, 2 * (q0 + f - 1))
                g = GU[(slot - p0) % 2]
                project(g[:, 0:L], slot, 0).then_inc(blocks_done, 1)
                project(g[:, L:2 * L], slot, 1).then_inc(blocks_done, 1)
                pe.wait_ge(pl_ready, q0 + f)
                pe_down(pe, slot, 2, (slot - p0 + 1) % 2, first)
            step(s0 + 1, 1, (p0 + 1) % 2, first=True)
            with pe.Fori(0, (FT - 2) // 2) as i:
                for u in range(2):
                    f = 2 * i + (2 + u)
                    step(s0 + f, f, (p0 + u) % 2)
            pe.wait_ge(lo_ready, s0 + FT + 1)
            pe.wait_ge(pl_ready, q0 + FT)
            pe_down(pe, (s0 + FT) % 2, 0, (FT - 1) % 2, False, last=True)

        def pe_stats(pe, n):
            for k in range(CT):
                if k % (CT // 2) == 0:
                    pe.wait_ge(sq_ready, 2 * n + 1 + k // (CT // 2))
                last = nc.tensor.matmul(ST[:, 0:L], ones, XSQ[:, k, :], start=k == 0, stop=k == CT - 1)
            return last

        def act_norm_in(act, n, gain):
            if n == 0:
                act.wait_ge(loaded, LOADS)
            elif n % 3 == 2:
                act.wait_ge(x_ready, 3 * n)
            for k in range(CT):
                if n % 3 != 2 and n and k in (0, 4, 6):
                    act.wait_ge(x_ready, 3 * n - 2 + (0, 4, 6).index(k))
                nc.scalar.activation(HH[:, k, :], X[:, k, :], ACT.Copy, scale=pcol(gain[0], gain[1] + k))\
                    .then_inc(hh_ready, 1)
            act_squares(act)

        def act_squares(act):
            for k in range(2):
                nc.scalar.activation(XSQ[:, 4 * k:4 * k + 4, :], X[:, 4 * k:4 * k + 4, :], ACT.Square)\
                    .then_inc(sq_ready, 1)

        def dve_norm_in(dve, n, gain):
            for k in range(CT):
                dve.wait_ge(hh_ready, NORM_TILES[n] + k + 1)
                nc.vector.scalar_tensor_tensor(out=HL[:, k, :], in0=X[:, k, :], scalar=pcol(gain[0], gain[1] + k),
                                               in1=HH[:, k, :].bitcast(fp32), op0=ALU.mult, op1=ALU.subtract)\
                    .then_inc(hl_ready, 1)

        def act_root(act, n, st_wait):
            act.wait_ge(*st_wait)
            if n == 0:
                act.wait_ge(eps_ready, 1)
            nc.scalar.activation(std[:, :], ST[:, 0:L], ACT.Sqrt, bias=eps6[:, 0:1], scale=1.0 / C).then_inc(std_ready, 1)

        def dve_root(dve, n):
            dve.wait_ge(std_ready, n + 1)
            nc.vector.reciprocal(rstd[:, :], std[:, :]).then_inc(rstd_ready, 1)

        def act_ffn(act, n, s0, q0):
            p0 = s0 % 2
            next_hi(act, s0 + 1)
            act_root(act, n, (blocks_done, 3 * s0 + 3))

            def glue(f, o):
                act.wait_ge(gs_ready, 2 * (q0 + f) + 1)
                nc.scalar.activation(sg[:, o, :], gs[:, o, :], ACT.Silu).then_inc(sg_ready, 1)
                act.wait_ge(prod_ready, q0 + f + 1)
                nc.scalar.activation(PH[:, o, :], prod[:, o, :], ACT.Copy).then_inc(ph_ready, 1)
            glue(0, 0)
            with act.Fori(0, (FT - 2) // 2) as i:
                for u in range(2):
                    s = s0 + 2 * i + (2 + u)
                    slot = (p0 + u) % 2
                    split_hi(act, s, slot=slot, uses=16 * i + 16 * ((s0 + 2 + u) // 2 + 1))
                    glue(2 * i + (1 + u), (1 + u) % 2)
            next_hi(act, s0 + FT)
            glue(FT - 1, (FT - 1) % 2)
            next_hi(act, s0 + FT + 1)

        def dve_ffn(dve, n, s0, q0):
            p0 = s0 % 2
            next_lo(dve, s0 + 1)
            dve_root(dve, n)

            def glue(f, o):
                dve.wait_ge(blocks_done, 3 * s0 + 3 * f + 2)
                if isinstance(f, int) and f == 0:
                    dve.wait_ge(rstd_ready, n + 1)
                nc.vector.tensor_tensor(gs[:, o, :], GU[o][:, 0:L], rstd[:, :], ALU.mult).then_inc(gs_ready, 1)
                nc.vector.tensor_tensor(us[:, o, :], GU[o][:, L:2 * L], rstd[:, :], ALU.mult).then_inc(gs_ready, 1)
                dve.wait_ge(sg_ready, q0 + f + 1)
                dve.wait_ge(gs_ready, 2 * (q0 + f + 1))
                nc.vector.tensor_tensor(prod[:, o, :], sg[:, o, :], us[:, o, :], ALU.mult).then_inc(prod_ready, 1)
                dve.wait_ge(ph_ready, q0 + f + 1)
                nc.vector.tensor_tensor(PL[:, o, :], prod[:, o, :], PH[:, o, :].bitcast(fp32), ALU.subtract)\
                    .then_inc(pl_ready, 1)
            glue(0, 0)
            with dve.Fori(0, (FT - 2) // 2) as i:
                for u in range(2):
                    split_lo(dve, s0 + 2 * i + (2 + u), slot=(p0 + u) % 2)
                    glue(2 * i + (1 + u), (1 + u) % 2)
            next_lo(dve, s0 + FT)
            glue(FT - 1, (FT - 1) % 2)
            next_lo(dve, s0 + FT + 1)

        def dve_residual(dve, s, scale):
            for part, js in enumerate(((0, 1), (2,), (3,))):
                dve.wait_ge(blocks_done, 3 * s + part + 1)
                for j in js:
                    last = nc.vector.scalar_tensor_tensor(
                        out=X[:, 2 * j:2 * j + 2, :], in0=DN[j][:, :].rearrange("p (a n) -> p a n", a=2), scalar=scale,
                        in1=X[:, 2 * j:2 * j + 2, :], op0=ALU.mult, op1=ALU.add)
                last.then_inc(x_ready, 1)

        eps6 = sb("eps6", [P, 4])
        NORM_TILES = [0, CT, 2 * CT, 3 * CT, None, 4 * CT]
        arena = sb("arena", [P, ARENA])
        at = [0]

        def place(n):
            at[0] += n
            assert at[0] <= ARENA
            return arena[:, at[0] - n:at[0]]
        hcst = place(NHC)
        fw = place(NFW)
        HRI = place(4 * 512).rearrange("p (i k c) -> p i k c", i=2, k=2)
        U3 = place(12 * (L + 2)).rearrange("p (m t) -> p m t", t=L + 2)
        UQ = place(6 * L).rearrange("p (m t) -> p m t", t=L)
        after_u = at[0]
        UC = place(12 * L).rearrange("p (m t) -> p m t", t=L)
        ZT = place(2 * 512).rearrange("p (a c) -> p a c", a=2)
        TM = XSQ[:, :, :].rearrange("p k t -> p (k t)").rearrange("p (i c) -> p i c", i=4)
        at[0] = NHC + NFW + 4 * 512
        YRI = place(4 * 512).rearrange("p (i k c) -> p i k c", i=2, k=2)
        at[0] = NHC + NFW + 4 * 512
        HFB = place(4 * 512).rearrange("p (i a c) -> p i a c", i=2, a=2)
        ABS = place(4 * 512).rearrange("p (i a c) -> p i a c", i=2, a=2)
        HSD = place(4 * 512).rearrange("p (i a c) -> p i a c", i=2, a=2)
        FARG = place(3 * L).rearrange("p (i t) -> p i t", i=3)
        FHID = place(3 * L).rearrange("p (i t) -> p i t", i=3)
        at[0] = after_u
        QN = place(4 * L).rearrange("p (m t) -> p m t", t=L)
        KN = place(2 * L).rearrange("p (m t) -> p m t", t=L)
        VT = place(2 * P).rearrange("p (a c) -> p a c", a=2)
        SC = place(2 * 512).rearrange("p (o a k) -> p o a k", o=2, a=2)
        EX = place(2 * 512).rearrange("p (o a k) -> p o a k", o=2, a=2)
        PT = place(2 * 512).rearrange("p (o b q) -> p o b q", o=2, b=2)
        RN = sg[0:16, :, :]
        small = sb("small", [P, 64])
        hy_rnorm = small[:, 0:4]
        amax, anegm, asum, aes, aden, arden = (small[:, 4 + 2 * k:6 + 2 * k] for k in range(6))
        ymix = prod
        sel = ccols("sel", CT * 16).rearrange("p (j h) -> p j h", h=16)
        selt = ccols("selt", CT * P)[0:16, :].rearrange("p (j c) -> p j c", c=P)
        ident = ccols("ident", P)

        def hc(name, n):
            return hcst[:, HC[name]:HC[name] + n]
        dft = [hc(n, 2 * L).rearrange("p (a k) -> p a k", a=2) for n in ("cos", "sin")]
        idft = [hc(n, 2 * L).rearrange("p (k t) -> p k t", k=2) for n in ("icos", "isin")]
        window = hc("window", 1024).rearrange("p (a c) -> p a c", a=2)
        dist = hc("dist", 2 * L).rearrange("p (a k) -> p a k", a=2)
        FO = FILTER_ORDER
        INV2PI = 1.0 / (2.0 * math.pi)
        ROUND = 1.5 * 2.0 ** 23
        PI2 = [6.28125, float(np.float32(2 * math.pi - 6.28125))]
        PI2.append(2 * math.pi - PI2[0] - PI2[1])
        SLOPES = [2.0 ** (-8.0 * (h + 1) / NQ) for h in range(NQ)]

        eps_ready = sem("eps_ready")
        dve_own = sem("dve_own")
        flt_mm = sem("flt_mm")
        flt_arg = sem("flt_arg")
        flt_sin = sem("flt_sin")
        flt_win = sem("flt_win")
        flt_abs = sem("flt_abs")
        flt_sum = sem("flt_sum")
        flt_h = sem("flt_h")
        u_ready = sem("u_ready")
        cv_ready = sem("cv_ready")
        qsq_ready = sem("qsq_ready")
        ss_done = sem("ss_done")
        root_ready = sem("root_ready")
        rec_ready = sem("rec_ready")
        bc_done = sem("bc_done")
        qn_ready = sem("qn_ready")
        z_ready = sem("z_ready")
        zt_done = sem("zt_done")
        zt_ready = sem("zt_ready")
        zf_done = sem("zf_done")
        y_spec = sem("y_spec")
        yi_done = sem("yi_done")
        ym_ready = sem("ym_ready")
        ks_done = sem("ks_done")
        ks_ready = sem("ks_ready")
        mix_hh = sem("mix_hh")
        mix_hl = sem("mix_hl")
        st_ready = sem("st_ready")
        sc_done = sem("sc_done")
        sc_ready = sem("sc_ready")
        ex_ready = sem("ex_ready")
        pr_ready = sem("pr_ready")
        pt_done = sem("pt_done")
        pt_ready = sem("pt_ready")
        pv_done = sem("pv_done")

        class Own:
            def __init__(self, eng, s, before=0):
                self.eng, self.s, self.before, self.n = eng, s, before, 0

            def __call__(self, ins):
                ins.then_inc(self.s, 1)
                self.n = self.n + 1

            def settle(self):
                self.eng.wait_ge(self.s, self.before + self.n)

            def enter(self, per):
                self.start, self.per = self.n, per

            def at(self, i):
                self.before, self.n = self.start + i * self.per, 0

            def leave(self, times):
                assert self.n == self.per, self.n
                self.before, self.n = 0, self.start + times * self.per

        def pe_filter(pe):
            b3 = bank[3]
            nc.tensor.matmul(b3[0:FO, 0:L], fw[0:FILTER_EMB, 0:FO], hc("feat", L)[0:FILTER_EMB, :],
                             start=True, stop=True).then_inc(flt_mm, 1)
            for n in (1, 2):
                pe.wait_ge(flt_sin, n)
                nc.tensor.matmul(b3[0:FO, 0:L], fw[0:FO, n * FO:(n + 1) * FO], FHID[0:FO, n - 1, :],
                                 start=True, stop=True).then_inc(flt_mm, 1)
            pe.wait_ge(flt_sin, 3)
            for a in range(2):
                for i in range(2):
                    last = nc.tensor.matmul(DN[2 * a + i][:, :], FHID[0:FO, 2, a * P:(a + 1) * P],
                                            fw[0:FO, 3 * FO + 512 * i:3 * FO + 512 * (i + 1)], start=True, stop=True)
            last.then_inc(flt_mm, 1)
            pe.wait_ge(flt_abs, 1)
            for c in range(HT):
                for n in range(4):
                    last = nc.tensor.matmul(b3[:, c:c + 1], ABS[:, n // 2, n % 2, c * P:(c + 1) * P], ones[:, 0:1],
                                            start=n == 0, stop=n == 3)
            last.then_inc(flt_mm, 1)
            pe.wait_ge(flt_sum, 1)
            for i in range(2):
                for k in range(2):
                    for a in range(2):
                        last = nc.tensor.matmul(DN[2 * i + k][:, :], dft[i][:, a, k * P:(k + 1) * P], HSD[:, i, a, :],
                                                start=a == 0, stop=a == 1)
            last.then_inc(flt_mm, 1)

        def act_filter(act):
            for n in range(3):
                act.wait_ge(flt_arg, n + 1)
                nc.scalar.activation(FHID[0:FO, n, :], FARG[0:FO, 0, :], ACT.Sin).then_inc(flt_sin, 1)
            act.wait_ge(flt_win, 1)
            nc.scalar.activation(ABS[:, :, :, :], HFB[:, :, :, :], ACT.Abs).then_inc(flt_abs, 1)
            act.wait_ge(flt_mm, 6)
            for n in range(4):
                last = nc.scalar.activation(HRI[:, n // 2, n % 2, :], DN[n][:, :], ACT.Copy)
            last.then_inc(flt_h, 1)

        def dve_filter(dve, own):
            ts, stt = nc.vector.tensor_scalar, nc.vector.scalar_tensor_tensor
            x, k = FARG[0:FO, 0, :], FARG[0:FO, 1, :]
            for n in range(3):
                dve.wait_ge(flt_mm, n + 1)
                if n:
                    dve.wait_ge(flt_sin, n)
                own(ts(x, bank[3][0:FO, 0:L], pcol("f_b", n)[0:FO], pcol("freq")[0:FO], ALU.add, ALU.mult))
                own.settle()
                own(ts(k, x, INV2PI, ROUND, ALU.mult, ALU.add))
                own.settle()
                own(ts(k, k, -ROUND, None, ALU.add))
                for c in PI2:
                    own.settle()
                    own(stt(out=x, in0=k, scalar=-c, in1=x, op0=ALU.mult, op1=ALU.add))
                own.settle()
                ts(x, x, 3.1415925, -3.1415925, ALU.min, ALU.max).then_inc(flt_arg, 1)
            dve.wait_ge(flt_mm, 4)
            for a in range(2):
                for i in range(2):
                    own(nc.vector.tensor_tensor(HFB[:, i, a, :], DN[2 * a + i][:, :], window[:, a, :], ALU.mult))
            own.settle()
            own(nc.vector.tensor_tensor(HFB[0:1, 0, 0, :], HFB[0:1, 0, 0, :], HFB[0:1, 1, 0, :], ALU.add))
            own.settle()
            nc.vector.memset(HFB[0:1, 1, 0, :], 0.0).then_inc(flt_win, 1)
            dve.wait_ge(flt_win, 1)
            nc.vector.tensor_tensor(HSD[:, 0, :, :], HFB[:, 0, :, :], HFB[:, 1, :, :], ALU.add)
            nc.vector.tensor_tensor(HSD[:, 1, :, :], HFB[:, 0, :, :], HFB[:, 1, :, :], ALU.subtract).then_inc(flt_sum, 1)
            dve.wait_ge(flt_mm, 5)
            own(nc.vector.reciprocal(hy_rnorm, bank[3][:, 0:HT]))
            dve.wait_ge(flt_mm, 6)
            own(nc.vector.memset(U3[:, :, 0:1], 0.0))
            own(nc.vector.memset(U3[:, :, L + 1:L + 2], 0.0))

        UB = [GU[0], GU[1], bank[3]]

        def pe_mix0(pe):
            s0, n = S_IN, 1
            for m in range(18):
                s, b = s0 + m // 3, m % 3
                if b == 0:
                    pe.wait_ge(lo_ready, s + 1)
                if m >= 3:
                    pe.wait_ge(u_ready, m - 2)
                wait = (lambda k: pe.wait_ge(hl_ready, NORM_TILES[n] + k + 1)) if m == 0 else None
                project(UB[m % 3][:, 0:L], s % 2, b, wait=wait).then_inc(blocks_done, 1)
                if m == 0:
                    pe_stats(pe, n).then_inc(st_ready, 1)
            pe.wait_ge(qsq_ready, 5)
            pe.wait_ge(u_ready, 16)
            for j in range(5):
                last = nc.tensor.matmul(GU[0][0:16, 0:L], sel[:, j, :], XSQ[:, j, :], start=j == 0, stop=j == 4)
            last.then_inc(ss_done, 1)
            pe.wait_ge(z_ready, 1)
            for a in range(2):
                for c in range(HT):
                    last = nc.tensor.transpose(DN[a][:, c * P:(c + 1) * P], UC[:, 8 + c, a * P:(a + 1) * P], ident)
            last.then_inc(zt_done, 1)
            pe.wait_ge(u_ready, 18)
            pe.wait_ge(rec_ready, 1)
            for j in range(5):
                dst = (bank[3], GU[1], GU[0])[j // 2][:, (j % 2) * L:(j % 2) * L + L]
                last = nc.tensor.matmul(dst, selt[:, j, :], RN[:, 1, :], start=True, stop=True)
            last.then_inc(bc_done, 1)
            pe.wait_ge(zt_ready, 1)
            for i in range(2):
                for k in range(2):
                    for a in range(2):
                        last = nc.tensor.matmul(DN[2 * i + k][:, :], dft[i][:, a, k * P:(k + 1) * P], ZT[:, a, :],
                                                start=a == 0, stop=a == 1)
            last.then_inc(zf_done, 1)
            pe.wait_ge(y_spec, 1)
            for c in range(HT):
                for n in range(4):
                    last = nc.tensor.matmul(DN[c][:, 0:L], YRI[:, n // 2, n % 2, c * P:(c + 1) * P],
                                            idft[n // 2][:, n % 2, :], start=n == 0, stop=n == 3)
                last.then_inc(yi_done, 1)
            pe.wait_ge(qn_ready, 5)
            nc.tensor.matmul(GU[0][:, L:2 * L], ccols("perm", P), KN[:, 0, :], start=True, stop=True).then_inc(ks_done, 1)
            for a in range(2):
                last = nc.tensor.transpose(ST[:, a * P:(a + 1) * P], UQ[:, 5, a * P:(a + 1) * P], ident)
            last.then_inc(zt_done, 1)
            pe.wait_ge(ks_ready, 1)
            pe.wait_ge(zt_ready, 2)
            pe.wait_ge(ym_ready, HT)

            def scores(h):
                if h >= 2:
                    pe.wait_ge(sc_ready, h - 1)
                r = slice(HD * (h % 2), HD * (h % 2) + HD)
                kn = KN[r, 0 if h % 2 == h // 4 else 1, :]
                for a in range(2):
                    last = nc.tensor.matmul(DN[h % 2][:, a * L:(a + 1) * L], QN[r, h // 2, a * P:(a + 1) * P], kn,
                                            start=True, stop=True)
                last.then_inc(sc_done, 1)
            scores(0)
            for h in range(NQ):
                if h + 1 < NQ:
                    scores(h + 1)
                pe.wait_ge(pr_ready, h + 1)
                if h >= 2:
                    pe.wait_ge(pt_ready, h - 1)
                for b in range(2):
                    for a in range(2):
                        last = nc.tensor.transpose(DN[2 + h % 2][:, b * L + a * P:b * L + (a + 1) * P],
                                                   SC[:, h % 2, a, b * P:(b + 1) * P], ident)
                last.then_inc(pt_done, 1)
                pe.wait_ge(pt_ready, h + 1)
                if h >= 4 and h % 2 == 0:
                    pe.wait_ge(ym_ready, HT + (h - 4) // 2 + 1)
                kv, r = h // 4, slice(HD * (h % 2), HD * (h % 2) + HD)
                for b in range(2):
                    last = nc.tensor.matmul(GU[(h // 2) % 2][r, 0:L], VT[:, b, kv * HD:(kv + 1) * HD],
                                            PT[:, h % 2, b, :], start=b == 0, stop=b == 1)
                last.then_inc(pv_done, 1)
            pe_out(pe, S_OUT)

        def pe_out(pe, s0):
            for m in range(CT):
                s, b = s0 + m // 3, m % 3
                if b == 0:
                    pe.wait_ge(lo_ready, s + 1)
                dst = DN[m // 2][:, (m % 2) * L:(m % 2) * L + L]
                for k in range(CT):
                    if m == 0:
                        pe.wait_ge(mix_hl, (CT if s0 == S_O else 0) + k + 1)
                    last = three(dst, b * BLK + k * P, s % 2, HH[:, k, :], HL[:, k, :], k == 0, k == CT - 1)
                    if m == CT - 1 and k == 3:
                        last.then_inc(blocks_done, 1)
                last.then_inc(blocks_done, 1)

        def dve_out(dve, s0):
            for part, (js, done) in enumerate((((0, 1), 4), ((2,), 6), ((3,), 9))):
                dve.wait_ge(blocks_done, 3 * s0 + done)
                for j in js:
                    last = nc.vector.tensor_tensor(X[:, 2 * j:2 * j + 2, :], DN[j][:, :].rearrange("p (a n) -> p a n", a=2),
                                                   X[:, 2 * j:2 * j + 2, :], ALU.add)
                last.then_inc(x_ready, 1)

        def act_mix0(act):
            act_root(act, 1, (st_ready, 1))
            for m in range(18):
                if m % 3 == 0:
                    next_hi(act, S_IN + m // 3 + 1)
                act.wait_ge(u_ready, m + 1)
                if m < 12:
                    nc.scalar.activation(UC[:, m, :], U3[:, m, 1:L + 1], ACT.Identity, bias=pcol("conv_b", m),
                                         scale=pcol("conv_w", 12 + m)).then_inc(cv_ready, 1)
                elif m < 17:
                    nc.scalar.activation(XSQ[:, m - 12, :], UQ[:, m - 12, :], ACT.Square).then_inc(qsq_ready, 1)
            act.wait_ge(ss_done, 1)
            nc.scalar.activation(RN[:, 0, :], GU[0][0:16, 0:L], ACT.Sqrt, bias=eps6[0:16, 0:1], scale=1.0 / HD)\
                .then_inc(root_ready, 1)
            act.wait_ge(zt_done, 1)
            for a in range(2):
                last = nc.scalar.activation(ZT[:, a, :], DN[a][:, :], ACT.Copy)
            last.then_inc(zt_ready, 1)
            for c in range(HT):
                act_mixed(act, c)
            act.wait_ge(ks_done, 1)
            nc.scalar.activation(KN[:, 1, :], GU[0][:, L:2 * L], ACT.Copy).then_inc(ks_ready, 1)
            act.wait_ge(zt_done, 2)
            nc.scalar.activation(VT[:, :, :], ST[:, 0:2 * P].rearrange("p (a c) -> p a c", a=2), ACT.Copy)\
                .then_inc(zt_ready, 1)
            for h in range(NQ):
                act.wait_ge(sc_ready, h + 1)
                for a in range(2):
                    nc.scalar.activation(EX[:, h % 2, a, :], SC[:, h % 2, a, :], ACT.Exp, bias=anegm[:, a:a + 1],
                                         accum_out=asum[:, a:a + 1])
                nc.scalar.activation(aes, anegm, ACT.Exp, bias=pcol("sink", h)).then_inc(ex_ready, 1)
                act.wait_ge(pt_done, h + 1)
                nc.scalar.activation(PT[:, h % 2, :, :], DN[2 + h % 2][:, :].rearrange("p (b q) -> p b q", b=2), ACT.Copy)\
                    .then_inc(pt_ready, 1)
                if h % 2:
                    act_mixed(act, HT + h // 2)

        def act_mixed(act, t, base=0):
            act.wait_ge(ym_ready, base + t + 1)
            nc.scalar.activation(HH[:, t, :], ymix[:, t % 2, :], ACT.Copy).then_inc(mix_hh, 1)

        def dve_mixed(dve, t, base=0):
            dve.wait_ge(mix_hh, base + t + 1)
            nc.vector.tensor_tensor(HL[:, t, :], ymix[:, t % 2, :], HH[:, t, :].bitcast(fp32), ALU.subtract)\
                .then_inc(mix_hl, 1)

        def dve_mix0(dve, own):
            tt, stt = nc.vector.tensor_tensor, nc.vector.scalar_tensor_tensor
            dve_root(dve, 1)
            dve.wait_ge(rstd_ready, 2)
            own.settle()
            dve.wait_ge(flt_h, 1)

            def conv(m):
                dve.wait_ge(cv_ready, m + 1)
                own(stt(out=UC[:, m, :], in0=U3[:, m, 0:L], scalar=pcol("conv_w", m), in1=UC[:, m, :],
                        op0=ALU.mult, op1=ALU.add))
                own.settle()
                own(stt(out=UC[:, m, :], in0=U3[:, m, 2:L + 2], scalar=pcol("conv_w", 24 + m), in1=UC[:, m, :],
                        op0=ALU.mult, op1=ALU.add))
            for m in range(18):
                if m % 3 == 0:
                    next_lo(dve, S_IN + m // 3 + 1)
                dve.wait_ge(blocks_done, 3 * S_IN + m + 1)
                dst = U3[:, m, 1:L + 1] if m < 12 else UQ[:, m - 12, :]
                tt(dst, UB[m % 3][:, 0:L], rstd[:, :], ALU.mult).then_inc(u_ready, 1)
                if 1 <= m <= 12:
                    conv(m - 1)
                if m == 12:
                    own.settle()
                    tt(UC[:, 8:12, :], UC[:, 8:12, :], UC[:, 4:8, :], ALU.mult).then_inc(z_ready, 1)
            dve.wait_ge(root_ready, 1)
            nc.vector.reciprocal(RN[:, 1, :], RN[:, 0, :]).then_inc(rec_ready, 1)
            dve.wait_ge(zf_done, 1)
            for k in range(2):
                for n in range(4):
                    i, o = ((0, 0), (1, 1), (0, 1), (1, 0))[n]
                    own(tt(TM[:, n, :], HRI[:, i, k, :], DN[2 * o + k][:, :], ALU.mult))
                own.settle()
                own(tt(YRI[:, 0, k, :], TM[:, 0, :], TM[:, 1, :], ALU.subtract))
                ins = tt(YRI[:, 1, k, :], TM[:, 2, :], TM[:, 3, :], ALU.add)
                if k:
                    ins.then_inc(y_spec, 1)
                else:
                    own(ins)
                    own.settle()
            for c in range(HT):
                if c >= 2:
                    dve.wait_ge(mix_hh, c - 1)
                y = ymix[:, c % 2, :]
                own(nc.vector.tensor_scalar(y, UC[:, 8 + c, :], pcol("hy_bias", c), None, ALU.mult))
                own.settle()
                dve.wait_ge(yi_done, c + 1)
                own(stt(out=y, in0=DN[c][:, 0:L], scalar=hy_rnorm[:, c:c + 1], in1=y, op0=ALU.mult, op1=ALU.add))
                own.settle()
                tt(y, y, UC[:, c, :], ALU.mult).then_inc(ym_ready, 1)
                dve_mixed(dve, c)
            dve.wait_ge(bc_done, 1)
            dve.wait_ge(zt_ready, 1)
            dve.wait_ge(ym_ready, HT)
            for j in range(5):
                src = (bank[3], GU[1], GU[0])[j // 2][:, (j % 2) * L:(j % 2) * L + L]
                if j < 4:
                    stt(out=QN[:, j, :], in0=UQ[:, j, :], scalar=pcol("q_gain"), in1=src, op0=ALU.mult, op1=ALU.mult)\
                        .then_inc(qn_ready, 1)
                else:
                    own(nc.vector.tensor_scalar(UQ[:, j, :], UQ[:, j, :], pcol("k_gain"), HD ** -0.5, ALU.mult, ALU.mult))
                    own.settle()
                    tt(KN[:, 0, :], UQ[:, j, :], src, ALU.mult).then_inc(qn_ready, 1)
            for h in range(NQ):
                o = h % 2
                dve.wait_ge(sc_done, h + 1)
                if h >= 2:
                    dve.wait_ge(pt_done, h - 1)
                own(stt(out=SC[:, o, :, :], in0=dist[:, :, :], scalar=-SLOPES[h],
                        in1=DN[o][:, :].rearrange("p (a k) -> p a k", a=2), op0=ALU.mult, op1=ALU.add))
                own.settle()
                if h:
                    dve.wait_ge(ex_ready, h)
                own(nc.vector.tensor_reduce(amax, SC[:, o, :, :], AX.X, ALU.max))
                own.settle()
                nc.vector.tensor_scalar(anegm, amax, pcol("sink", h), -1.0, ALU.max, ALU.mult).then_inc(sc_ready, 1)
                dve.wait_ge(ex_ready, h + 1)
                own(tt(aden, asum, aes, ALU.add))
                own.settle()
                own(nc.vector.reciprocal(arden, aden))
                own.settle()
                for a in range(2):
                    last = nc.vector.tensor_scalar(SC[:, o, a, :], EX[:, o, a, :], arden[:, a:a + 1], None, ALU.mult)
                last.then_inc(pr_ready, 1)
                if o:
                    t = HT + h // 2
                    dve.wait_ge(pv_done, h + 1)
                    dve.wait_ge(mix_hh, t - 1)
                    nc.vector.tensor_copy(ymix[:, t % 2, :], GU[(h // 2) % 2][:, 0:L]).then_inc(ym_ready, 1)
                    dve_mixed(dve, t)
        LOADS = 80

        at[0] = 0
        R, K, V = (place(CT * L) for _ in range(3))
        LW = place(2 * CT * L)
        AG = place(2 * CT * L)
        h_at = at[0]
        H = place(CT * (L + 2)).rearrange("p (k t) -> p k t", t=L + 2)
        XX = XSQ
        XI = work[:, :, :, :].rearrange("p i o t -> p (i o) t")
        at[0] = h_at
        KK = place(CT * L + 16)[:, 0:CT * L]
        CI = place(2 * L)
        HID = CI.rearrange("p (i t) -> p i t", i=2)
        pools = [[scan, 4 * 3 * BLK, 0], [scan2, 2 * CT * L, 0], [raw[:, :, :].rearrange("p s n -> p (s n)"), 6 * BLK, 0],
                 [work[:, :, :, :].rearrange("p i o t -> p (i o t)"), 8 * L, 0],
                 [XSQ[:, :, :].rearrange("p k t -> p (k t)"), CT * L, 0], [arena, ARENA, at[0]]]

        def splace(n):
            for pool in pools:
                if pool[2] + n <= pool[1]:
                    pool[2] += n
                    return pool[0][:, pool[2] - n:pool[2]]
            raise ValueError((n, [p[1] - p[2] for p in pools]))

        def bd(n=NU):
            return splace(n * P).rearrange("p (u h s) -> p u h s", h=2, s=CH)

        def full(n=NU):
            return splace(n * P).rearrange("p (u c) -> p u c", c=P)
        ALB, BTB, KTK, BTK, VTK = ([f(n) for _ in range(2)] for f, n in
                                   ((bd, NU), (bd, NU), (full, NU), (full, NU), (full, NCH)))
        AR = [splace(1024).rearrange("p (u i t) -> p u i t", i=2, t=CH) for _ in range(2)]
        AQ, BQ = ([full() for _ in range(2)] for _ in range(2))
        BEB, KAB, QBD = (bd() for _ in range(3))
        ABD, TBD, ZBD, XLV, QF = (full() for _ in range(5))
        VB = bd(NCH)
        CE, E2, E3, KD, BB = (splace(2 * L) for _ in range(5))
        E1, KAT, BE = CE, E2, BB
        TMPK = splace(L)
        RB = TMPK
        RCH, UCH, SCH0 = (full(2) for _ in range(3))
        SCH = (SCH0, std[:, :].rearrange("p (z v) -> p z v", z=2))
        etot = [small[:, 40:48], small[:, 48:56]]
        omk = small[:, 24:24 + CT]
        GH, GL = sb("GH", [P, 2, L], f32r), sb("GL", [P, 2, L], f32r)
        blockones, istack = ccols("blockones", P), ccols("istack", CH)

        def mask64(name, z):
            return ccols(name, CH, z * CH).rearrange("p (o s) -> p o s", o=1).broadcast_to([P, 2 * NCH, CH])

        def blocks(a, z):
            return a[:, z * NCH:(z + 1) * NCH, :].rearrange("p c (h s) -> p (c h) s", h=2)

        def mask(name, z):
            return ccols(name, P, z * P).rearrange("p (o s) -> p o s", o=1).broadcast_to([P, NCH, P])

        mx_hh, mx_hl = sem("mx_hh"), sem("mx_hl")
        xi_ready = sem("xi_ready")
        rkv_ready = sem("rkv_ready")
        lr_done = sem("lr_done")
        lr_ready = sem("lr_ready")
        lr_hi, lr_lo = sem("lr_hi"), sem("lr_lo")
        kk_sq, kk_ss, kk_max, kk_root, kk_rec, kk_bc, kk_ready = (sem(f"kk_{n}") for n in
                                                                "sq ss max root rec bc ready".split())
        ka_ready, c_ready, e_ready = sem("ka_ready"), sem("c_ready"), sem("e_ready")
        tm_ready, rb_ready, bo_done, bo_read = sem("tm_ready"), sem("rb_ready"), sem("bo_done"), sem("bo_read")
        kd_ready, al_ready, be_ready, bd_ready = sem("kd_ready"), sem("al_ready"), sem("be_ready"), sem("bd_ready")
        tr_done, tr_ready, a_done, a_ready = sem("tr_done"), sem("tr_ready"), sem("a_done"), sem("a_ready")
        abd_ready, bt_ready, kab_ready = sem("abd_ready"), sem("bt_ready"), sem("kab_ready")
        xl_ready, z_done, zb_ready, d_done, t_ready = (sem(n) for n in "xl_ready z_done zb_ready d_done t_ready".split())
        r_done, r_ready, uu_done, uu_ready, y_done, s_done, s_ready = (
            sem(n) for n in "r_done r_ready uu_done uu_ready y_done s_done s_ready".split())
        yt_ready = sem("yt_ready")
        gn_mean, gn_sq, gn_ss, gn_root, gn_rec, gn_bc, gn_af, gn_c = (sem(f"gn_{n}") for n in
                                                                      "mean sq ss root rec bc af c".split())
        g_done, gn_n = sem("g_done"), sem("gn_n")
        MIXES = [0, 2, 3, 1, 4, 5]

        def pe_mix1(pe):
            s0, n = S_RKV, 4
            pe_stats(pe, n).then_inc(st_ready, 1)
            q = 0
            for i in range(6):
                for m in (range(CT) if i < 3 else range(1 if i < 5 else 2)):
                    g = CT * i + m if i < 3 else 24 + i - 3 + m
                    s, b = s0 + g // 3, g % 3
                    if b == 0:
                        pe.wait_ge(lo_ready, s + 1)
                    if g >= 3:
                        pe.wait_ge(rkv_ready, g - 2)
                    wait = (lambda k: pe.wait_ge(mx_hl, CT * i + k + 1)) if m == 0 else None
                    project(UB[g % 3][:, 0:L], s % 2, b, wait=wait).then_inc(blocks_done, 1)
            for i in range(2):
                pe.wait_ge(lr_lo, i + 1)
                s, b = S_LORA + 1, 1 + i
                for m in range(CT):
                    for z in range(2):
                        if q >= 3:
                            pe.wait_ge(lr_ready, q - 2)
                        else:
                            pe.wait_ge(rkv_ready, 28)
                        r = slice(64 * z, 64 * z + 64)
                        ins = three(UB[q % 3][:, 0:L], b * BLK + m * P, s % 2, PH[r, i, :], PL[r, i, :], True, True,
                                    rows=r)
                        if m == CT - 1 and z == 1:
                            ins.then_inc(blocks_done, 1)
                        else:
                            ins.then_inc(lr_done, 1)
                        q += 1
            pe.wait_ge(kk_sq, CT)
            pe.wait_ge(lr_lo, 4)
            for j in range(CT):
                last = nc.tensor.matmul(ST[0:16, 0:L], sel[:, j, :], XSQ[:, j, :], start=j == 0, stop=j == CT - 1)
            last.then_inc(kk_ss, 1)
            pe.wait_ge(kk_rec, 1)
            for j in range(CT):
                last = nc.tensor.matmul(DN[j // 2][:, (j % 2) * L:(j % 2) * L + L], selt[:, j, :], RN[:, 1, :],
                                        start=True, stop=True)
            last.then_inc(kk_bc, 1)
            pe.wait_ge(kk_ready, 1)
            pe_bonus(pe, 0)
            tiles(pe, lambda t, p, c, a: pe_tile(pe, t, p, c, a))
            for i in range(NCH):
                pe_r(pe, CT - 1, 1, i)
                pe_u(pe, CT - 1, i)
                pe_s(pe, CT - 1, 1, i)
                pe_y(pe, CT - 1, 1, i)
            pe_groupnorm(pe)

        def tiles(eng, body, own=None):
            body(0, 0, False, True)
            if own:
                own.enter(SCAN_OWN)
            with eng.Fori(0, (CT - 2) // 2) as i:
                if own:
                    own.at(i)
                for o in range(2):
                    body(2 * i + (1 + o), (1 + o) % 2, True, True)
            if own:
                own.leave((CT - 2) // 2)
            body(CT - 1, (CT - 1) % 2, True, False)

        def flat(a):
            return a.rearrange("p h s -> p (h s)")

        def units(i):
            return (i, 2 * NCH - 1 - i)

        def pe_bonus(pe, t):
            pe.wait_ge(rb_ready, t + 1)
            nc.tensor.matmul(bank[7][:, 0:L], blockones, RB, start=True, stop=True).then_inc(bo_done, 1)

        def pe_tr(pe, t, n):
            if n:
                pe.wait_ge(tr_ready, 5 * t + n)
            else:
                pe.wait_ge(a_ready, t + 1)
            for c in range(NCH):
                src = VB[:, c] if n == 0 else (KAB, BEB)[(n - 1) // 2][:, (n - 1) % 2 * NCH + c]
                last = nc.tensor.transpose(bank[7][:, c * P:(c + 1) * P], flat(src), ident)
            last.then_inc(tr_done, 1)

        def pe_r(pe, t, p, i):
            for z, u in enumerate(units(i)):
                dst = bank[4][:, z * P:(z + 1) * P]
                if i:
                    pe.wait_ge(s_ready, 6 * t + 2 * i)
                    pe.wait_ge(uu_ready, 4 * t + i)
                    nc.tensor.matmul(dst, flat(ALB[p][:, u]), SCH[i % 2][:, z, :], start=True, stop=False)
                elif z == 0:
                    pe.wait_ge(tr_ready, 5 * t + 5)
                    pe.wait_ge(t_ready, 12 * t + 12)
                    pe.wait_ge(bt_ready, t + 1)
                last = nc.tensor.matmul(dst, flat(BTB[p][:, u]), VTK[p][:, u % NCH, :], start=i == 0, stop=True)
            last.then_inc(r_done, 1)

        def pe_u(pe, t, i):
            pe.wait_ge(r_ready, 4 * t + i + 1)
            for z, u in enumerate(units(i)):
                last = nc.tensor.matmul(bank[4][:, z * P:(z + 1) * P], QF[:, u, :], RCH[:, z, :], start=True, stop=True)
            last.then_inc(uu_done, 1)

        def pe_s(pe, t, p, i):
            if i == NCH - 1:
                return
            pe.wait_ge(uu_ready, 4 * t + i + 1)
            for z, u in enumerate(units(i)):
                dst = bank[5][:, z * P:(z + 1) * P]
                if i:
                    nc.tensor.matmul(dst, ident, SCH[i % 2][:, z, :], start=True, stop=False)
                nc.tensor.matmul(dst, KTK[p][:, u, :], VTK[p][:, u % NCH, :], start=i == 0, stop=False)
                last = nc.tensor.matmul(dst, BTK[p][:, u, :], UCH[:, z, :], start=False, stop=True)
            last.then_inc(s_done, 1)

        def pe_y(pe, t, p, i):
            if i == 0:
                pe.wait_ge(yt_ready, t + 1)
            pe.wait_ge(uu_ready, 4 * t + i + 1)
            for z, u in enumerate(units(i)):
                c = u % NCH
                dst = bank[6][:, c * P:(c + 1) * P]
                nc.tensor.matmul(dst, VTK[p][:, c, :], BQ[p][:, u, :], start=i == 0 and z == 0, stop=False)
                if i:
                    nc.tensor.matmul(dst, SCH[i % 2][:, z, :], flat(AR[p][:, u]), start=False, stop=False)
                last = nc.tensor.matmul(dst, UCH[:, z, :], AQ[p][:, u, :], start=False, stop=i == NCH - 1 and z == 1)
            last.then_inc(y_done, 1)

        def pe_tile(pe, t, p, chunks, ahead):
            mm, B, q = nc.tensor.matmul, bank, 1 - p
            pe.wait_ge(al_ready, 2 * t + 2)
            pe.wait_ge(bd_ready, 3 * t + 3)
            pe.wait_ge(kab_ready, t + 1)
            pe.wait_ge(bo_read, t + 1)
            for u in range(NU):
                last = mm(B[u // NCH][:, (u % NCH) * P:(u % NCH + 1) * P], flat(ALB[p][:, u]), flat(BEB[:, u]),
                          start=True, stop=True)
            last.then_inc(a_done, 1)
            for lhs, bs in ((BEB, (2, 3)), (KAB, (7, 1))):
                for u in range(NU):
                    if bs[u // NCH] == 1:
                        pe.wait_ge(abd_ready, 2 * t + 2)
                    last = mm(B[bs[u // NCH]][:, (u % NCH) * P:(u % NCH + 1) * P], flat(lhs[:, u]), flat(AR[p][:, u]),
                              start=True, stop=True)
                last.then_inc(a_done, 1)
            for n in range(len(LEVELS)):
                step = chunks and n < NCH
                if step:
                    pe_r(pe, t - 1, q, n)
                for z in range(2):
                    pe.wait_ge(xl_ready, 10 * t + 2 * n + z + 1)
                    pe.wait_ge(t_ready, 12 * t + 2 * n + z + 1)
                    if n == 0 and z == 1:
                        pe.wait_ge(a_ready, t + 1)
                    for c in range(NCH):
                        u = z * NCH + c
                        last = mm(B[z][:, c * P:(c + 1) * P], XLV[:, u, :], flat(QBD[:, u]), start=True, stop=True)
                    last.then_inc(z_done, 1)
                if n < 3:
                    pe_tr(pe, t, 2 * n)
                if step:
                    pe_u(pe, t - 1, n)
                for z in range(2):
                    pe.wait_ge(zb_ready, 10 * t + 2 * n + z + 1)
                    for c in range(NCH):
                        u = z * NCH + c
                        last = mm(B[2 + z][:, c * P:(c + 1) * P], TBD[:, u, :], ZBD[:, u, :], start=True, stop=True)
                    if n < len(LEVELS) - 1:
                        for c in range(NCH):
                            u = z * NCH + c
                            last = mm(B[z][:, c * P:(c + 1) * P], ZBD[:, u, :], TBD[:, u, :], start=True, stop=True)
                    last.then_inc(d_done, 1)
                    if z == 0:
                        if step:
                            pe_s(pe, t - 1, q, n)
                        if n == 3 and ahead:
                            pe.wait_ge(tr_ready, 5 * t + 5)
                            pe_bonus(pe, t + 1)
                if step:
                    pe_y(pe, t - 1, q, n)
                if n < 2:
                    pe_tr(pe, t, 2 * n + 1)

        def halves(fn):
            for h in range(2):
                last = fn(slice(HD * h, HD * h + HD), h)
            return last

        def tile_of(a, j, z=0, n=1):
            return a[:, bass.ds(z * CT * L + j * L, L)]

        def act_operands(act, t, part):
            A, cp, p = nc.scalar.activation, ACT.Copy, None
            if part == 0:
                if not (isinstance(t, int) and t == 0):
                    act.wait_ge(al_ready, 2 * t)
                for z in range(2):
                    last = A(KAT[:, z * L:(z + 1) * L], tile_of(AG, t, z), ACT.Identity,
                             bias=small[:, bass.ds(24 + t, 1)], scale=par[:, bass.ds(COL["k_a"] + t, 1)])
                last.then_inc(ka_ready, 1)
            elif part == 1:
                if not (isinstance(t, int) and t == 0):
                    act.wait_ge(tr_done, 5 * t - 4)
                halves(lambda r, h: A(VB[r, :, h, :], V[r, bass.ds(t * L, L)].rearrange("p (c s) -> p c s", c=NCH), cp))\
                    .then_inc(bd_ready, 1)
                act.wait_ge(c_ready, t + 1)
                if not (isinstance(t, int) and t == 0):
                    act.wait_ge(be_ready, 2 * t)
                A(E1[:, :], CE[:, :], ACT.Exp, scale=-DECAY).then_inc(e_ready, 1)
                A(E3[:, :], CI[:, :], ACT.Exp, scale=DECAY).then_inc(e_ready, 1)
            elif part == 2:
                act.wait_ge(kd_ready, t + 1)
                A(E2[:, :], CI[:, :], ACT.Exp, scale=-DECAY).then_inc(e_ready, 1)

        def act_operands_late(act, t, p):
            A, cp = nc.scalar.activation, ACT.Copy
            ci = CI[:, :].rearrange("p (z c t) -> p z c t", z=2, c=NCH)
            for z in range(2):
                last = A(etot[p][:, z * NCH:(z + 1) * NCH], ci[:, z, :, (CH - 1) if z == 0 else 0], ACT.Exp, scale=-DECAY)
            last.then_inc(e_ready, 1)
            act.wait_ge(be_ready, 2 * t + 1)
            if not (isinstance(t, int) and t == 0):
                act.wait_ge(tr_done, 5 * t)
            halves(lambda r, h: A(BEB[r, :, h, :], BE[r, :].rearrange("p (u t) -> p u t", u=NU), cp)).then_inc(bd_ready, 1)
            act.wait_ge(al_ready, 2 * t + 1)
            halves(lambda r, h: A(ALB[p][r, :, h, :], AR[p][r, :, 0, :], cp)).then_inc(bd_ready, 1)

        def act_tr(act, t, p, n):
            A, cp = nc.scalar.activation, ACT.Copy
            act.wait_ge(tr_done, 5 * t + n + 1)
            src = bank[7][:, :].rearrange("p (c s) -> p c s", c=NCH)
            dst = VTK[p][:, :, :] if n == 0 else (KTK, BTK)[(n - 1) // 2][p][:, (n - 1) % 2 * NCH:(n - 1) % 2 * NCH + NCH, :]
            A(dst, src, cp).then_inc(tr_ready, 1)

        def act_s(act, t, p, i):
            if i == NCH - 1:
                return
            act.wait_ge(s_done, 3 * t + i + 1)
            for z, u in enumerate(units(i)):
                nc.scalar.activation(SCH[(i + 1) % 2][:, z, :], bank[5][:, z * P:(z + 1) * P], ACT.Copy,
                                     scale=etot[p][:, u:u + 1])\
                    .then_inc(s_ready, 1)

        def act_tile(act, t, p, chunks, ahead):
            A, cp, B, q = nc.scalar.activation, ACT.Copy, bank, 1 - p
            act.wait_ge(a_done, 3 * t + 1)
            for z in range(2):
                A(ABD[:, z * NCH:(z + 1) * NCH, :], bank_of(z), cp).then_inc(abd_ready, 1)
            if ahead:
                act_operands(act, t + 1, 0)
            if chunks:
                act.wait_ge(e_ready, 4 * t)
            for n in range(len(LEVELS)):
                step = chunks and n < NCH
                for z in range(2):
                    act.wait_ge(z_done, 10 * t + 2 * n + z + 1)
                    A(ZBD[:, z * NCH:(z + 1) * NCH, :], bank_of(z), cp).then_inc(zb_ready, 1)
                if n < 3:
                    act_tr(act, t, p, 2 * n)
                if n == 0:
                    act.wait_ge(a_ready, t + 1)
                    halves(lambda r, h: A(BTB[p][r, :, h, :], BQ[p][r, :, 0:CH], cp)).then_inc(bt_ready, 1)
                if step:
                    act_s(act, t - 1, q, n)
                if n < 2:
                    act_tr(act, t, p, 2 * n + 1)
                if ahead and n in (1, 2):
                    act_operands(act, t + 1, n)
            if ahead:
                act_operands_late(act, t + 1, q)

        def dve_prefix(dve, own, t):
            tt, z2 = nc.vector.tensor_tensor, slice(L, 2 * L)
            if not (isinstance(t, int) and t == 0):
                dve.wait_ge(e_ready, 4 * t)
                dve.wait_ge(al_ready, 2 * t)
            for z in range(2):
                own(nc.vector.tensor_tensor_scan(out=(CI if z == 0 else CE)[:, z * L:(z + 1) * L], data0=ccols("reset", L),
                                                 data1=tile_of(LW, t, z), initial=0.0, op0=ALU.mult, op1=ALU.add))
            own.settle()
            own(tt(CE[:, 0:L], CI[:, 0:L], tile_of(LW, t, 0), ALU.subtract))
            p1 = CE[:, z2].rearrange("p (c t) -> p c t", c=NCH)
            own(nc.vector.tensor_copy(small[:, 32:36], p1[:, :, CH - 1]))
            own.settle()
            own(tt(p1, small[:, 32:36].rearrange("p (c o) -> p c o", o=1).broadcast_to([P, NCH, CH]), p1, ALU.subtract))
            own.settle()
            tt(CI[:, z2], CE[:, z2], tile_of(LW, t, 1), ALU.add).then_inc(c_ready, 1)

        def dve_kb(dve, own, t):
            tt = nc.vector.tensor_tensor
            dve.wait_ge(ka_ready, t + 1)
            if not (isinstance(t, int) and t == 0):
                dve.wait_ge(kab_ready, t)
            for z in range(2):
                own(tt(BB[:, z * L:(z + 1) * L], tile_of(AG, t, z), tile_of(KK, t), ALU.mult))
                ins = tt(KD[:, z * L:(z + 1) * L], KAT[:, z * L:(z + 1) * L], tile_of(K, t), ALU.mult)
                if z == 0:
                    own(ins)
            ins.then_inc(kd_ready, 1)

        def dve_rb(dve, t):
            dve.wait_ge(tm_ready, t + 1)
            nc.vector.scalar_tensor_tensor(out=RB, in0=tile_of(R, t), scalar=par[:, bass.ds(COL["r_k"] + t, 1)], in1=TMPK,
                                           op0=ALU.mult, op1=ALU.mult).then_inc(rb_ready, 1)

        def dve_bonus(dve, t):
            dve.wait_ge(bo_done, t + 1)
            dve.wait_ge(kd_ready, t + 1)
            nc.vector.scalar_tensor_tensor(out=tile_of(K, t), in0=bank[7][:, 0:L], scalar=0.5, in1=tile_of(V, t),
                                           op0=ALU.mult, op1=ALU.mult).then_inc(bo_read, 1)

        def dve_alpha(dve, t, p):
            c4 = lambda a: a.rearrange("p (c t) -> p c t", c=NCH)
            dve.wait_ge(e_ready, 4 * t + 1)
            for z in range(2):
                ins = nc.vector.scalar_tensor_tensor(out=AR[p][:, z * NCH:(z + 1) * NCH, 0, :], in0=c4(tile_of(KK, t)),
                                                     scalar=-1.0, in1=c4(E1[:, z * L:(z + 1) * L]), op0=ALU.mult, op1=ALU.mult)
            ins.then_inc(al_ready, 1)
            dve.wait_ge(e_ready, 4 * t + 3)
            for z in range(2):
                ins = nc.vector.tensor_tensor(AR[p][:, z * NCH:(z + 1) * NCH, 1, :], c4(tile_of(R, t)),
                                              c4(E2[:, z * L:(z + 1) * L]), ALU.mult)
            ins.then_inc(al_ready, 1)

        def dve_kappa(dve, own, t):
            dve.wait_ge(be_ready, 2 * t + 2)
            if not (isinstance(t, int) and t == 0):
                dve.wait_ge(tr_done, 5 * t)
            kd = KD.rearrange("p (u t) -> p u t", u=NU)
            own(nc.vector.tensor_copy(KAB[0:HD, :, 0, :], kd[0:HD]))
            nc.vector.tensor_copy(KAB[HD:P, :, 1, :], kd[HD:P]).then_inc(kab_ready, 1)

        def dve_rc(dve, t, i):
            dve.wait_ge(r_done, 4 * t + i + 1)
            nc.vector.tensor_copy(RCH[:, :, :], bank[4][:, 0:2 * P].rearrange("p (z v) -> p z v", z=2)).then_inc(r_ready, 1)

        def dve_uc(dve, t, i):
            dve.wait_ge(uu_done, 4 * t + i + 1)
            nc.vector.tensor_copy(UCH[:, :, :], bank[4][:, 0:2 * P].rearrange("p (z v) -> p z v", z=2)).then_inc(uu_ready, 1)

        def dve_yt(dve, t):
            dve.wait_ge(y_done, 4 * t + 4)
            dve.wait_ge(rb_ready, t + 1)
            nc.vector.tensor_scalar(tile_of(R, t).rearrange("p (c t) -> p c t", c=NCH), bank_of(6)[:, :, CH:P], 1.0, None,
                                    ALU.mult).then_inc(yt_ready, 1)

        def bank_of(n):
            return bank[n][:, :].rearrange("p (c s) -> p c s", c=NCH)

        def dve_tile(dve, t, p, chunks, ahead, own):
            tt, q = nc.vector.tensor_tensor, 1 - p
            group = [slice(z * NCH, (z + 1) * NCH) for z in range(2)]
            dve.wait_ge(a_done, 3 * t + 2)
            for z in range(2):
                own(tt(AQ[p][:, group[z], :], bank_of(2 + z), mask("first_incl", z), ALU.mult))
            dve.wait_ge(abd_ready, 2 * t + 2)
            for z in range(2):
                own(tt(blocks(TBD, z), blocks(ABD, z), mask64("first", z), ALU.mult))
            own.settle()
            eye = istack.rearrange("p (o s) -> p o s", o=1).broadcast_to([P, NU, CH])
            halves(lambda r, h: own(tt(QBD[r, :, h, :], AQ[p][r, :, 0:CH], eye[r], ALU.add)))
            for z in range(2):
                tt(TBD[:, group[z], :], TBD[:, group[z], :], ident.rearrange("p (o s) -> p o s", o=1)
                   .broadcast_to([P, NCH, P]), ALU.add).then_inc(t_ready, 1)
            dve.wait_ge(a_done, 3 * t + 3)
            own(tt(BQ[p][:, group[1], :], bank_of(1), mask("strict_incl", 1), ALU.mult))
            tt(BQ[p][:, group[0], :], bank_of(7), mask("strict_incl", 0), ALU.mult).then_inc(a_ready, 1)
            for n in range(len(LEVELS)):
                step = chunks and n < NCH
                if step:
                    dve_rc(dve, t - 1, n)
                for z in range(2):
                    if z == 0 and step:
                        dve_uc(dve, t - 1, n)
                    dve.wait_ge(d_done, 10 * t + 2 * n + z + 1)
                    dve.wait_ge(t_ready, 12 * t + 2 * n + z + 1)
                    if n < len(LEVELS) - 1:
                        own(tt(TBD[:, group[z], :], TBD[:, group[z], :], bank_of(z), ALU.add))
                        q_bd = QBD[:, group[z], :, :].rearrange("p u h s -> p u (h s)")
                        tt(q_bd, q_bd, bank_of(2 + z), ALU.add).then_inc(t_ready, 1)
                    else:
                        q_bd = QBD[:, group[z], :, :].rearrange("p u h s -> p u (h s)")
                        tt(QF[:, group[z], :], q_bd, bank_of(2 + z), ALU.add).then_inc(t_ready, 1)
                if ahead and n == 4:
                    dve_kappa(dve, own, t + 1)
                if ahead and n == 0:
                    dve_prefix(dve, own, t + 1)
                if ahead and n == 1:
                    dve_kb(dve, own, t + 1)
                if ahead and n == 2:
                    dve_rb(dve, t + 1)
                if n == 3:
                    if chunks:
                        dve_yt(dve, t - 1)
                    if ahead:
                        dve_bonus(dve, t + 1)
                        dve_alpha(dve, t + 1, q)

        def pool_operands(pool, t, part):
            g = nc.gpsimd.tensor_tensor
            if part == 0:
                pool.wait_ge(kd_ready, t + 1)
                g(TMPK, KD[:, 0:L], KD[:, L:2 * L], ALU.add).then_inc(tm_ready, 1)
            else:
                pool.wait_ge(e_ready, 4 * t + 2)
                g(BE, BB, E3, ALU.mult).then_inc(be_ready, 1)
                pool.wait_ge(tm_ready, t + 1)
                g(KD, KD, E3, ALU.mult).then_inc(be_ready, 1)

        def pool_tile(pool, t, ahead):
            for n in range(len(LEVELS)):
                for z in range(2):
                    if n:
                        pool.wait_ge(z_done, 10 * t + 2 * (n - 1) + z + 1)
                    elif z == 0:
                        pool.wait_ge(abd_ready, 2 * t + 2)
                    nc.gpsimd.tensor_tensor(blocks(XLV, z), blocks(ABD, z), mask64("level", z * len(LEVELS) + n), ALU.mult)\
                        .then_inc(xl_ready, 1)
                if ahead and n == 1:
                    pool_operands(pool, t + 1, 0)
                if ahead and n == 3:
                    pool_operands(pool, t + 1, 1)

        def act_mix1(act):
            s0 = S_RKV
            A = nc.scalar.activation
            act_root(act, 4, (st_ready, 2))
            for i in range(6):
                for k in range(CT):
                    act.wait_ge(xi_ready, CT * i + k + 1)
                    if i and k == 0:
                        act.wait_ge(blocks_done, 3 * s0 + (CT * i if i < 4 else 24 + i - 3))
                    A(HH[:, k, :], XI[:, k, :], ACT.Copy).then_inc(mx_hh, 1)
                for m in (range(CT) if i < 3 else range(1 if i < 5 else 2)):
                    g = CT * i + m if i < 3 else 24 + i - 3 + m
                    if g % 3 == 0 and s0 + g // 3 + 1 < S_O:
                        next_hi(act, s0 + g // 3 + 1)
                    act.wait_ge(blocks_done, 3 * s0 + g + 1)
                    src = UB[g % 3][:, 0:L]
                    if i < 3:
                        A((R, K, V)[i][:, m * L:(m + 1) * L], src, ACT.Copy).then_inc(rkv_ready, 1)
                    elif i == 3:
                        A(HID[:, 0, :], src, ACT.Tanh).then_inc(rkv_ready, 1)
                        act.wait_ge(rkv_ready, g + 1)
                        A(PH[:, 0, :], HID[:, 0, :], ACT.Copy).then_inc(lr_hi, 1)
                    elif i == 4:
                        A(HID[:, 1, :], src, ACT.Copy).then_inc(rkv_ready, 1)
                        act.wait_ge(rkv_ready, g + 1)
                        A(PH[:, 1, :], HID[:, 1, :], ACT.Copy).then_inc(lr_hi, 1)
                    else:
                        act.wait_ge(lr_lo, m + 1)
                        A(HID[:, m, :], src, ACT.Sigmoid).then_inc(rkv_ready, 1)
                        act.wait_ge(rkv_ready, g + 1)
                        A(GH[:, m, :], HID[:, m, :], ACT.Copy).then_inc(lr_hi, 1)
            q = 0
            for i, dst in enumerate((LW, AG)):
                for m in range(CT):
                    for z in range(2):
                        if m == CT - 1 and z == 1:
                            act.wait_ge(blocks_done, 3 * (S_LORA + 1) + 2 + i)
                        else:
                            act.wait_ge(lr_done, q + 1 - i)
                        A(dst[:, (z * CT + m) * L:(z * CT + m + 1) * L], UB[q % 3][:, 0:L], ACT.Sigmoid,
                          bias=pcol(("w0", "a0")[i], z * CT + m)).then_inc(lr_ready, 1)
                        q += 1
            for j in range(CT):
                A(XSQ[:, j, :], K[:, j * L:(j + 1) * L], ACT.Square, scale=pcol("k_k", j)).then_inc(kk_sq, 1)
            act.wait_ge(kk_max, 1)
            A(RN[:, 0, :], HID[0:16, 0, :], ACT.Sqrt).then_inc(kk_root, 1)
            act.wait_ge(kk_ready, 1)
            for part in range(3):
                act_operands(act, 0, part)
            act_operands_late(act, 0, 0)
            tiles(act, lambda t, p, c, a: act_tile(act, t, p, c, a))
            act.wait_ge(e_ready, 4 * CT)
            for i in range(NCH):
                act_s(act, CT - 1, 1, i)
            act.wait_ge(yt_ready, CT + 1)
            next_hi(act, S_O)
            next_hi(act, S_O + 1)
            act_groupnorm(act)

        def dve_mix1(dve, own):
            V_ = nc.vector
            tt, ts, stt = V_.tensor_tensor, V_.tensor_scalar, V_.scalar_tensor_tensor
            dve_root(dve, 4)
            own(V_.memset(H[:, :, 0:1], 0.0))
            own(V_.memset(H[:, :, L + 1:L + 2], 0.0))
            dve.wait_ge(rstd_ready, 5)
            for k in range(CT):
                own(stt(out=H[:, k, 1:L + 1], in0=X[:, k, :], scalar=pcol("mix_norm", CT + k), in1=rstd[:, :],
                        op0=ALU.mult, op1=ALU.mult))
            own.settle()
            own(tt(XX[:, :, :], H[:, :, 0:L], H[:, :, 2:L + 2], ALU.add))
            own.settle()
            own(stt(out=XX[:, :, :], in0=XX[:, :, :], scalar=0.5, in1=H[:, :, 1:L + 1], op0=ALU.mult, op1=ALU.subtract))
            own.settle()

            def mix(i):
                if i:
                    dve.wait_ge(mx_hl, CT * i)
                for k in range(CT):
                    stt(out=XI[:, k, :], in0=XX[:, k, :], scalar=pcol("mu", MIXES[i] * CT + k), in1=H[:, k, 1:L + 1],
                        op0=ALU.mult, op1=ALU.add).then_inc(xi_ready, 1)
            mix(0)
            for i in range(6):
                for k in range(CT):
                    dve.wait_ge(mx_hh, CT * i + k + 1)
                    tt(HL[:, k, :], XI[:, k, :], HH[:, k, :].bitcast(fp32), ALU.subtract).then_inc(mx_hl, 1)
                if i < 5:
                    mix(i + 1)
                for m in (range(CT) if i < 3 else range(1 if i < 5 else 2)):
                    g = CT * i + m if i < 3 else 24 + i - 3 + m
                    if g % 3 == 0 and S_RKV + g // 3 + 1 < S_O:
                        next_lo(dve, S_RKV + g // 3 + 1)
                    if i >= 3:
                        dve.wait_ge(lr_hi, g - 23)
                        hi, lo, o = (PH, PL, i - 3) if i < 5 else (GH, GL, m)
                        tt(lo[:, o, :], HID[:, o, :], hi[:, o, :].bitcast(fp32), ALU.subtract).then_inc(lr_lo, 1)
            dve.wait_ge(kk_ss, 1)
            ts(HID[0:16, 0, :], ST[0:16, 0:L], 1e-24, None, ALU.max).then_inc(kk_max, 1)
            dve.wait_ge(kk_root, 1)
            V_.reciprocal(RN[:, 1, :], RN[:, 0, :]).then_inc(kk_rec, 1)
            own(ts(omk, par[:, COL["k_a"]:COL["k_a"] + CT], -1.0, 1.0, ALU.mult, ALU.add))
            for a in (*ALB, *BTB, BEB, KAB, QBD):
                own(V_.memset(a[:, :, :, :], 0.0))
            own(V_.memset(VB[:, :, :, :], 0.0))
            dve.wait_ge(kk_bc, 1)
            for j in range(CT):
                own(stt(out=KK[:, j * L:(j + 1) * L], in0=K[:, j * L:(j + 1) * L], scalar=pcol("k_k", j),
                        in1=DN[j // 2][:, (j % 2) * L:(j % 2) * L + L], op0=ALU.mult, op1=ALU.mult))
            own.settle()
            V_.memset(small[:, 36:37], 0.0).then_inc(yt_ready, 1)
            V_.memset(small[:, 37:38], 0.0).then_inc(kk_ready, 1)
            dve_prefix(dve, own, 0)
            dve_kb(dve, own, 0)
            dve_rb(dve, 0)
            dve_bonus(dve, 0)
            dve_alpha(dve, 0, 0)
            dve_kappa(dve, own, 0)
            tiles(dve, lambda t, p, c, a: dve_tile(dve, t, p, c, a, own), own)
            for i in range(NCH):
                dve_rc(dve, CT - 1, i)
                dve_uc(dve, CT - 1, i)
            dve_yt(dve, CT - 1)
            next_lo(dve, S_O)
            next_lo(dve, S_O + 1)
            dve_groupnorm(dve, own)

        def ytile(j):
            return R[:, j * L:(j + 1) * L]

        def half_bank(bs, j):
            return bs[j // 2][:, (j % 2) * L:(j % 2) * L + L]
        MB = [bank[0], bank[1], bank[2], bank[3]]

        def pe_groupnorm(pe):
            for j in range(CT):
                pe.wait_ge(yt_ready, CT + 1)
                nc.tensor.matmul(half_bank(MB, j), blockones, ytile(j), start=True, stop=True).then_inc(gn_mean, 1)
            for j in range(CT):
                pe.wait_ge(lo_ready, S_O + 1)
                for i in range(2):
                    last = three(half_bank(DN, j), i * BLK + j * P, S_O % 2, GH[:, i, :], GL[:, i, :], i == 0, i == 1)
                    if j == CT - 1:
                        last.then_inc(blocks_done, 1)
            for j in range(CT):
                pe.wait_ge(gn_sq, max(j + 1, 2))
                last = nc.tensor.matmul(bank[0][0:16, 0:L], sel[:, j, :], XSQ[:, j, :], start=j == 0, stop=j == CT - 1)
            last.then_inc(gn_ss, 1)
            pe.wait_ge(gn_rec, 1)
            for j in range(CT):
                if j >= 2:
                    pe.wait_ge(gn_n, j - 1)
                nc.tensor.matmul(bank[j % 2][:, L:2 * L], selt[:, j, :], RN[:, 1, :], start=True, stop=True).then_inc(gn_bc, 1)
            for m in range(CT):
                g = m + 2
                s, b = S_O + g // 3, g % 3
                if b == 0:
                    pe.wait_ge(lo_ready, s + 1)
                if m == 0:
                    pe.wait_ge(gn_n, CT)
                for k in range(CT):
                    if m == 0:
                        pe.wait_ge(mix_hl, CT + k + 1)
                    last = three(half_bank(MB, m), b * BLK + k * P, s % 2, HH[:, k, :], HL[:, k, :], k == 0, k == CT - 1)
                    if m == CT - 1 and k in (2, 5):
                        last.then_inc(blocks_done, 1)
                last.then_inc(blocks_done, 1)

        def act_groupnorm(act):
            A = nc.scalar.activation
            for j in range(CT):
                act.wait_ge(gn_c, j + 1)
                A(XSQ[:, j, :], ytile(j), ACT.Square).then_inc(gn_sq, 1)
            act.wait_ge(gn_ss, 1)
            A(RN[:, 0, :], bank[0][0:16, 0:L], ACT.Sqrt, bias=eps6[0:16, 1:2], scale=1.0 / HD).then_inc(gn_root, 1)
            for j in range(CT):
                act.wait_ge(gn_n, j + 1)
                A(ytile(j), ytile(j), ACT.Identity, bias=pcol("ln_b", j), scale=pcol("ln_w", j)).then_inc(gn_af, 1)
                act_mixed(act, j, CT)
            for s in (2, 3, 4):
                next_hi(act, S_O + s)

        def dve_groupnorm(dve, own):
            tt, stt = nc.vector.tensor_tensor, nc.vector.scalar_tensor_tensor
            for j in range(CT):
                dve.wait_ge(gn_mean, 2 * (j // 2) + 2)
                stt(out=ytile(j), in0=half_bank(MB, j), scalar=-1.0 / HD, in1=ytile(j), op0=ALU.mult, op1=ALU.add)\
                    .then_inc(gn_c, 1)
            dve.wait_ge(gn_root, 1)
            nc.vector.reciprocal(RN[:, 1, :], RN[:, 0, :]).then_inc(gn_rec, 1)
            dve.wait_ge(blocks_done, 3 * S_O + 2)
            for j in range(CT):
                dve.wait_ge(gn_bc, j + 1)
                tt(ytile(j), ytile(j), bank[j % 2][:, L:2 * L], ALU.mult).then_inc(gn_n, 1)
                dve.wait_ge(gn_af, j + 1)
                own(tt(ytile(j), ytile(j), K[:, j * L:(j + 1) * L], ALU.add))
                own.settle()
                if j >= 2:
                    dve.wait_ge(mix_hh, CT + j - 1)
                tt(ymix[:, j % 2, :], ytile(j), half_bank(DN, j), ALU.mult).then_inc(ym_ready, 1)
                dve_mixed(dve, j, CT)
            for s in (2, 3, 4):
                next_lo(dve, S_O + s)
            for part, (js, done) in enumerate((((0, 1), 6), ((2,), 8), ((3,), 12))):
                dve.wait_ge(blocks_done, 3 * S_O + done)
                for j in js:
                    last = tt(X[:, 2 * j:2 * j + 2, :], MB[j][:, :].rearrange("p (a n) -> p a n", a=2),
                              X[:, 2 * j:2 * j + 2, :], ALU.add)
                last.then_inc(x_ready, 1)
        @block.sync
        def _(sp):
            for dst, src in ((hcst, hconst_d), (fw, fw_d), (par[:, :], par_d), (cst[:, :], const_d), (X[:, :, :], xT)):
                sp.dma_start(dst, src).then_inc(loaded, 16)
            for s in range(2):
                sp.dma_start(raw[:, s, :], stream[s]).then_inc(raw_full[s], 16)

            def load(s, u):
                sp.dma_start(raw[:, u, :], stream[s]).then_inc(raw_full[u], 16)
            for first, end in ((2, min(S_O, STEPS)), (S_O, STEPS)):
                if first == S_O and end > first:
                    sp.wait_ge(yt_ready, CT + 1)
                n = (end - first) // 2
                if n <= 0:
                    continue
                with sp.Fori(0, n) as i:
                    for u in range(2):
                        sp.wait_ge(lo_ready, 2 * i + (first - 1 + u))
                        load(2 * i + (first + u), (first + u) % 2)
                for s in range(first + 2 * n, end):
                    sp.wait_ge(lo_ready, s - 1)
                    load(s, s % 2)
            sp.wait_ge(x_ready, 3 * len(NORM_TILES))
            sp.dma_start(out, X[:, :, :]).then_inc(stored, 16)
            sp.wait_ge(stored, 16)

        @block.tensor
        def _(pe):
            pe.wait_ge(loaded, LOADS)
            pe_filter(pe)
            pe_ffn(pe, 0, S_FFN[0], 0)
            pe_mix0(pe)
            pe_ffn(pe, 2, S_FFN[1], FT)
            pe_ffn(pe, 3, S_FFN[2], 2 * FT)
            pe_mix1(pe)
            pe_ffn(pe, 5, S_FFN[3], 3 * FT)

        @block.scalar
        def _(act):
            act.wait_ge(loaded, LOADS)
            act_filter(act)
            next_hi(act, 0)
            act_norm_in(act, 0, ("ffn1_norm", 0))
            act_ffn(act, 0, S_FFN[0], 0)
            act_norm_in(act, 1, ("mix_norm", 0))
            act_mix0(act)
            for s in (1, 2, 3):
                next_hi(act, S_OUT + s)
            act_norm_in(act, 2, ("ffn2_norm", 0))
            act_ffn(act, 2, S_FFN[1], FT)
            act_norm_in(act, 3, ("ffn1_norm", CT))
            act_ffn(act, 3, S_FFN[2], 2 * FT)
            act.wait_ge(x_ready, 12)
            act_squares(act)
            act_mix1(act)
            act_norm_in(act, 5, ("ffn2_norm", CT))
            act_ffn(act, 5, S_FFN[3], 3 * FT)

        @block.gpsimd
        def _(pool):
            pool.wait_ge(kk_ready, 1)
            for part in range(2):
                pool_operands(pool, 0, part)
            tiles(pool, lambda t, p, c, a: pool_tile(pool, t, a))

        @block.vector
        def _(dve):
            own = Own(dve, dve_own)
            nc.vector.memset(eps6[:, 0:1], 1e-6)
            nc.vector.memset(eps6[:, 1:2], 64e-5).then_inc(eps_ready, 1)
            dve.wait_ge(loaded, LOADS)
            dve_filter(dve, own)
            next_lo(dve, 0)
            dve_norm_in(dve, 0, ("ffn1_norm", 0))
            dve_ffn(dve, 0, S_FFN[0], 0)
            dve_residual(dve, S_FFN[0] + FT, 0.5)
            dve_norm_in(dve, 1, ("mix_norm", 0))
            dve_mix0(dve, own)
            for s in (1, 2, 3):
                next_lo(dve, S_OUT + s)
            dve_out(dve, S_OUT)
            dve_norm_in(dve, 2, ("ffn2_norm", 0))
            dve_ffn(dve, 2, S_FFN[1], FT)
            dve_residual(dve, S_FFN[1] + FT, 0.5)
            dve_norm_in(dve, 3, ("ffn1_norm", CT))
            dve_ffn(dve, 3, S_FFN[2], 2 * FT)
            dve_residual(dve, S_FFN[2] + FT, 0.5)
            dve_mix1(dve, own)
            dve_norm_in(dve, 5, ("ffn2_norm", CT))
            dve_ffn(dve, 5, S_FFN[3], 3 * FT)
            dve_residual(dve, S_FFN[3] + FT, 0.5)


def _consts():
    c = np.zeros((P, NCONST), np.float32)

    def put(name, a, off=0):
        c[:, CC[name] + off:CC[name] + off + a.shape[1]] = a
    r = np.arange(P)
    put("ident", np.eye(P))
    put("istack", np.tile(np.eye(CH), (2, 1)))
    put("blockones", (r[:, None] // HD == r[None, :] // HD) * 1.0)
    put("ones", np.ones((P, P)))
    for j in range(CT):
        put("sel", (np.arange(16)[None, :] == 2 * j + r[:, None] // HD) * 1.0, 16 * j)
        put("selt", (r[:, None] == 2 * j + r[None, :] // HD) * 1.0, P * j)
    put("perm", (r[:, None] == (r[None, :] + HD) % P) * 1.0)
    t, s = np.arange(CH)[:, None], np.arange(CH)[None, :]
    for z in range(2):
        pair = (t // 2 == s // 2) & ((t > s) if z == 0 else (t < s))
        before = (s < t) if z == 0 else (s > t)
        incl = np.tile((before | (s == t)).T * 1.0, (2, 1))
        put("first", np.tile(pair * 1.0, (2, 1)), z * CH)
        put("first_incl", np.concatenate([np.tile(pair.T * 1.0, (2, 1)), incl], 1), z * P)
        put("strict_incl", np.concatenate([np.tile(before.T * 1.0, (2, 1)), incl], 1), z * P)
        for n, b in enumerate(LEVELS):
            m = (t // (2 * b) == s // (2 * b)) & ((t // b > s // b) if z == 0 else (t // b < s // b))
            put("level", np.tile(m * 1.0, (2, 1)), (z * len(LEVELS) + n) * CH)
    put("reset", np.tile((np.arange(L) % CH != 0) * 1.0, (P, 1)))
    return c


def _hconsts():
    c = np.zeros((P, NHC), np.float32)

    def put(name, a):
        c[:, HC[name]:HC[name] + 2 * a.shape[1]] = a.reshape(2, P, -1).transpose(1, 0, 2).reshape(P, -1)
    t = np.arange(L, dtype=np.float64)
    theta = 2 * np.pi * (t + 0.5) / (2 * L)
    put("cos", np.cos(t[:, None] * theta[None, :]))
    put("sin", np.sin(t[:, None] * theta[None, :]))
    put("icos", np.cos(theta[:, None] * t[None, :]) / L)
    put("isin", np.sin(theta[:, None] * t[None, :]) / L)
    f32 = np.float32
    tt = (t.astype(f32) / f32(L - 1)).astype(f32)
    deltas = np.abs(np.linspace(math.log(1e-2) / 1.5, math.log(1e-2) / 0.3, 512).astype(f32))
    put("window", np.exp((-tt[:, None] * deltas[None, :]).astype(np.float64)))
    d = np.abs(t[:, None] - t[None, :])
    put("dist", np.where(d <= 128, d, 1e30))
    bands = (FILTER_EMB - 1) // 2
    freqs = np.linspace(1e-4, bands - 1, bands).astype(f32)
    ang = (f32(2.0 * math.pi / L) * t.astype(f32)[:, None] * freqs[None, :]).astype(np.float64)
    feat = np.concatenate([tt[:, None], np.cos(ang), -np.sin(ang)], axis=1)
    c[:FILTER_EMB, HC["feat"]:HC["feat"] + L] = feat.T
    return c


def _blocks(i):
    st = np.zeros((STEPS, P, 3, BLK), np.float32)

    def col(w, m, width=P):
        b = np.zeros((P, CT, P), np.float32)
        b[:, :, :width] = w[:, m * P:m * P + width].reshape(CT, P, width).transpose(1, 0, 2)
        return b.reshape(P, BLK)
    for n, (name, layer) in enumerate((("ffn1", 0), ("ffn2", 0), ("ffn1", 1), ("ffn2", 1))):
        g, u, d = (i[f"{name}_{k}"][layer] for k in ("wg", "wu", "wd"))
        for f in range(FT):
            st[S_FFN[n] + f, :, 0] = col(g, f)
            st[S_FFN[n] + f, :, 1] = col(u, f)
            st[S_FFN[n] + f + 1, :, 2 if f < FT - 1 else 0] = d[f * P:(f + 1) * P]

    def lay(s0, blocks):
        for k, b in enumerate(blocks):
            st[s0 + k // 3, :, k % 3] = b
    lay(S_IN, [col(i["ab_w_in"][0], m) for m in range(18)])
    lay(S_OUT, [col(i["ab_w_out"][0], m) for m in range(CT)])
    lay(S_RKV, [col(i[f"rw_w_{k}"][0], m) for k in "rkv" for m in range(CT)])
    both = lambda w: np.concatenate([w[0], w[1]], axis=-1)
    g1, g2 = i["rw_g1"][0], i["rw_g2"][0]
    g2b = np.zeros((P, C), np.float32)
    g2b[:LORA_G - P] = g2[P:]
    lay(S_LORA, [col(both(i["rw_w1"][0]), 0), col(both(i["rw_a1"][0]), 0), col(g1, 0),
                 col(g1, 1, LORA_G - P), i["rw_w2"][0].reshape(P, C), i["rw_a2"][0].reshape(P, C)])
    lay(S_O, [g2[:P], g2b] + [col(i["rw_w_o"][0], m) for m in range(CT)])
    return st.reshape(STEPS, P, 3 * BLK)


def _params(i):
    c = np.zeros((P, NPAR), np.float32)

    def put(name, a, off=0):
        a = a.reshape(-1, P).T
        c[:, COL[name] + off:COL[name] + off + a.shape[1]] = a
    for n in ("ffn1_norm", "mix_norm", "ffn2_norm"):
        put(n, i[n])
    put("conv_w", i["ab_conv_w"][0])
    put("conv_b", i["ab_conv_b"][0])
    put("hy_bias", i["hy_bias"][0])
    for n in ("mu", "w0", "a0", "k_k", "k_a", "r_k", "ln_w", "ln_b"):
        put(n, i["rw_" + n][0])
    c[:, COL["q_gain"]] = np.tile(i["attn_q_norm"][0], 2)
    c[:, COL["k_gain"]] = np.tile(i["attn_k_norm"][0], 2)
    c[:, COL["sink"]:COL["sink"] + NQ] = np.broadcast_to(i["attn_sink"][0], (P, NQ))
    for n in range(3):
        c[:FILTER_ORDER, COL["f_b"] + n] = i[f"hy_f{n + 1}_b"][0]
    c[:FILTER_ORDER, COL["freq"]] = i["hy_sin_freq"][0]
    return c


def _filter_weights(i):
    w = np.zeros((P, NFW), np.float32)
    w[:FILTER_EMB, :FILTER_ORDER] = i["hy_f1_w"][0]
    w[:FILTER_ORDER, FILTER_ORDER:2 * FILTER_ORDER] = i["hy_f2_w"][0]
    w[:FILTER_ORDER, 2 * FILTER_ORDER:3 * FILTER_ORDER] = i["hy_f3_w"][0]
    w[:FILTER_ORDER, 3 * FILTER_ORDER:] = i["hy_f4_w"][0]
    return w


def _channel_major(x):
    return np.ascontiguousarray(x.reshape(L, CT, P).transpose(2, 1, 0))


def _arrays(inputs):
    i = {k: np.asarray(v) for k, v in inputs.items()}
    return {"xT_in": _channel_major(i["x"][0]), "stream_in": _blocks(i), "par_in": _params(i), "const_in": _consts(),
            "hconst_in": _hconsts(), "fw_in": _filter_weights(i)}


def kernel(**inputs):
    import concourse.bacc as bacc
    from concourse.bass_utils import run_bass_kernel_spmd

    nc = bacc.Bacc("TRN2", target_bir_lowering=False, num_devices=1)
    arrays = _arrays(inputs)
    io = [nc.dram_tensor(n, a.shape, mybir.dt.float32, kind="ExternalInput").ap() for n, a in arrays.items()]
    io.append(nc.dram_tensor("out", (P, CT, L), mybir.dt.float32, kind="ExternalOutput").ap())
    build(nc, io)
    r = run_bass_kernel_spmd(nc, [arrays], core_ids=[0])
    y = np.asarray(r.results[0]["out"])
    return np.ascontiguousarray(y.transpose(2, 1, 0)).reshape(1, L, C)
```

```python
import math
from contextlib import ExitStack

import numpy as np
import concourse.bass as bass
from concourse import mybir

P = 128
C = 1024
L = 256
CT = C // P
F = 2816
FT = F // P
HT = 4
NQ, NKV, HD = 8, 2, 64
LORA_G = 160
CH = 64
NCH = L // CH
NU = 2 * NCH
BLK = CT * P
FILTER_EMB, FILTER_ORDER = 33, 64
DECAY = math.exp(-0.5)

FFN_STEPS = FT + 1
IN_STEPS, OUT_STEPS, RKV_STEPS, LORA_STEPS, O_STEPS = 6, 3, 8, 2, 4
SCAN_OWN = 46
S_FFN = [0, 0, 0, 0]
S_FFN[0] = 0
S_IN = FFN_STEPS
S_OUT = S_IN + IN_STEPS
S_FFN[1] = S_OUT + OUT_STEPS
S_FFN[2] = S_FFN[1] + FFN_STEPS
S_RKV = S_FFN[2] + FFN_STEPS
S_LORA = S_RKV + RKV_STEPS
S_O = S_LORA + LORA_STEPS
S_FFN[3] = S_O + O_STEPS
STEPS = S_FFN[3] + FFN_STEPS


def blocks_in(s):
    for s0 in S_FFN:
        if s == s0:
            return 2
        if s == s0 + FT:
            return 1
    return {S_OUT + 2: 2, S_O + 3: 1}.get(s, 3)


_names = [("ffn1_norm", 2 * CT), ("mix_norm", 2 * CT), ("ffn2_norm", 2 * CT), ("conv_w", 3 * 12), ("conv_b", 12),
          ("hy_bias", HT), ("mu", 6 * CT), ("w0", 2 * CT), ("a0", 2 * CT), ("k_k", CT), ("k_a", CT), ("r_k", CT),
          ("ln_w", CT), ("ln_b", CT), ("q_gain", 1), ("k_gain", 1), ("sink", NQ), ("f_b", 3), ("freq", 1)]
COL = {}
_at = 0
for _n, _w in _names:
    COL[_n] = _at
    _at += _w
NPAR = _at
LEVELS = [2, 4, 8, 16, 32]
ARENA = 18390

_cn = [("ident", P), ("istack", CH), ("blockones", P), ("ones", P), ("sel", CT * 16), ("selt", CT * P), ("perm", P),
       ("first", 2 * CH), ("first_incl", 2 * P), ("strict_incl", 2 * P), ("level", len(LEVELS) * 2 * CH), ("reset", L)]
CC = {}
_at = 0
for _n, _w in _cn:
    CC[_n] = _at
    _at += _w
NCONST = _at
_hn = [("cos", 2 * L), ("sin", 2 * L), ("icos", 2 * L), ("isin", 2 * L), ("window", 2 * 512), ("dist", 2 * L),
       ("feat", L)]
HC = {}
_at = 0
for _n, _w in _hn:
    HC[_n] = _at
    _at += _w
NHC = _at
NFW = 3 * FILTER_ORDER + 2 * 512


def build(nc, io):
    fp32 = mybir.dt.float32
    f32r = mybir.dt.float32r
    ALU = mybir.AluOpType
    ACT = mybir.ActivationFunctionType
    AX = mybir.AxisListType
    xT, stream, par_d, const_d, hconst_d, fw_d, out = io
    ctx = ExitStack()
    with ctx:
        def sb(name, shape, dt=fp32):
            return ctx.enter_context(nc.sbuf_tensor(name, shape, dt))

        def sem(name):
            return ctx.enter_context(nc.semaphore(name))

        X = sb("X", [P, CT, L])
        h_offset = nc.sbuf_base
        HH = sb("HH", [P, CT, L], f32r)
        HL = sb("HL", [P, CT, L], f32r)
        XSQ = sb("XSQ", [P, CT, L])
        raw = sb("raw", [P, 2, 3 * BLK])
        w_offset = nc.sbuf_base
        WH = sb("WH", [P, 2, 3 * BLK], f32r)
        WL = sb("WL", [P, 2, 3 * BLK], f32r)
        PH = sb("PH", [P, 2, L], f32r)
        PL = sb("PL", [P, 2, L], f32r)
        work = sb("work", [P, 4, 2, L])
        prod, gs, us, sg = (work[:, n, :, :] for n in range(4))
        std = sb("std", [P, L])
        rstd = sb("rstd", [P, L])
        par = sb("par", [P, NPAR])
        cst = sb("cst", [P, NCONST])

        scan = nc.alloc_sbuf_tensor_at("scan", [P, 4 * 3 * BLK], fp32, offset=w_offset)
        scan2 = nc.alloc_sbuf_tensor_at("scan2", [P, 2 * CT * L], fp32, offset=h_offset)

        bank = [ctx.enter_context(nc.psum_tensor(f"bank{i}", [P, 512], fp32)) for i in range(8)]
        GU = bank[0:2]
        ST = bank[2]
        DN = bank[4:8]

        def pcol(name, i=0):
            return par[:, COL[name] + i:COL[name] + i + 1]

        def ccols(name, n, off=0):
            return cst[:, CC[name] + off:CC[name] + off + n]

        ones = ccols("ones", P)

        raw_full = [sem("raw_full0"), sem("raw_full1")]
        hi_ready = sem("hi_ready")
        lo_ready = sem("lo_ready")
        blocks_done = sem("blocks_done")
        loaded = sem("loaded")
        hh_ready = sem("hh_ready")
        hl_ready = sem("hl_ready")
        sq_ready = sem("sq_ready")
        std_ready = sem("std_ready")
        rstd_ready = sem("rstd_ready")
        gs_ready = sem("gs_ready")
        sg_ready = sem("sg_ready")
        prod_ready = sem("prod_ready")
        ph_ready = sem("ph_ready")
        pl_ready = sem("pl_ready")
        x_ready = sem("x_ready")
        stored = sem("stored")
        block = ctx.enter_context(nc.Block())

        def split_hi(act, s, width=3 * BLK, slot=None, uses=None):
            slot = s % 2 if slot is None else slot
            act.wait_ge(raw_full[slot], 16 * (s // 2 + 1) if uses is None else uses)
            act.wait_ge(blocks_done, 3 * s - 3) if not (isinstance(s, int) and s < 2) else None
            nc.scalar.activation(WH[:, slot, :width], raw[:, slot, :width], ACT.Copy).then_inc(hi_ready, 1)

        def split_lo(dve, s, width=3 * BLK, slot=None):
            slot = s % 2 if slot is None else slot
            dve.wait_ge(hi_ready, s + 1)
            nc.vector.tensor_tensor(WL[:, slot, :width], raw[:, slot, :width],
                                    WH[:, slot, :width].bitcast(fp32), ALU.subtract).then_inc(lo_ready, 1)

        def next_hi(act, s):
            if s < STEPS:
                split_hi(act, s, blocks_in(s) * BLK)

        def next_lo(dve, s):
            if s < STEPS:
                split_lo(dve, s, blocks_in(s) * BLK)

        def three(out_ap, lo_off, slot, xh, xl, start, stop, rows=slice(0, P), m=P, **kw):
            wh = WH[rows, slot, lo_off:lo_off + m]
            wl = WL[rows, slot, lo_off:lo_off + m]
            nc.tensor.matmul(out_ap, wh, xh, start=start, stop=False, **kw)
            nc.tensor.matmul(out_ap, wh, xl, start=False, stop=False, **kw)
            return nc.tensor.matmul(out_ap, wl, xh, start=False, stop=stop, **kw)

        def project(out_ap, slot, b, inp=None, wait=None):
            xh, xl = inp if inp is not None else (HH, HL)
            for k in range(CT):
                if wait is not None:
                    wait(k)
                last = three(out_ap, b * BLK + k * P, slot, xh[:, k, :], xl[:, k, :], k == 0, k == CT - 1)
            return last

        def pe_down(pe, slot, b, par_, first, last=False):
            for m in range(CT):
                dst = DN[m // 2][:, (m % 2) * L:(m % 2) * L + L]
                w = b * BLK + m * P
                a, c_ = PH[:, par_, :], PL[:, par_, :]
                ins = three(dst, w, slot, a, c_, first and m % 2 == 0, last, skip_group_check=True)
                if last and m in (3, 5):
                    ins.then_inc(blocks_done, 1)
            ins.then_inc(blocks_done, 1)

        def pe_ffn(pe, n, s0, q0):
            p0 = s0 % 2
            h0 = NORM_TILES[n]
            pe.wait_ge(lo_ready, s0 + 1)

            def wait_h(k):
                pe.wait_ge(hl_ready, h0 + k + 1)
            project(GU[0][:, 0:L], p0, 0, wait=wait_h).then_inc(blocks_done, 1)
            project(GU[0][:, L:2 * L], p0, 1).then_inc(blocks_done, 1)
            pe_stats(pe, n).then_inc(blocks_done, 1)

            def step(s, f, slot, first=False):
                pe.wait_ge(lo_ready, s + 1)
                if not (isinstance(f, int) and f < 2):
                    pe.wait_ge(gs_ready, 2 * (q0 + f - 1))
                g = GU[(slot - p0) % 2]
                project(g[:, 0:L], slot, 0).then_inc(blocks_done, 1)
                project(g[:, L:2 * L], slot, 1).then_inc(blocks_done, 1)
                pe.wait_ge(pl_ready, q0 + f)
                pe_down(pe, slot, 2, (slot - p0 + 1) % 2, first)
            step(s0 + 1, 1, (p0 + 1) % 2, first=True)
            with pe.Fori(0, (FT - 2) // 2) as i:
                for u in range(2):
                    f = 2 * i + (2 + u)
                    step(s0 + f, f, (p0 + u) % 2)
            pe.wait_ge(lo_ready, s0 + FT + 1)
            pe.wait_ge(pl_ready, q0 + FT)
            pe_down(pe, (s0 + FT) % 2, 0, (FT - 1) % 2, False, last=True)

        def pe_stats(pe, n):
            for k in range(CT):
                if k % (CT // 2) == 0:
                    pe.wait_ge(sq_ready, 2 * n + 1 + k // (CT // 2))
                last = nc.tensor.matmul(ST[:, 0:L], ones, XSQ[:, k, :], start=k == 0, stop=k == CT - 1)
            return last

        def act_norm_in(act, n, gain):
            if n == 0:
                act.wait_ge(loaded, LOADS)
            elif n % 3 == 2:
                act.wait_ge(x_ready, 3 * n)
            for k in range(CT):
                if n % 3 != 2 and n and k in (0, 4, 6):
                    act.wait_ge(x_ready, 3 * n - 2 + (0, 4, 6).index(k))
                nc.scalar.activation(HH[:, k, :], X[:, k, :], ACT.Copy, scale=pcol(gain[0], gain[1] + k))\
                    .then_inc(hh_ready, 1)
            act_squares(act)

        def act_squares(act):
            for k in range(2):
                nc.scalar.activation(XSQ[:, 4 * k:4 * k + 4, :], X[:, 4 * k:4 * k + 4, :], ACT.Square)\
                    .then_inc(sq_ready, 1)

        def dve_norm_in(dve, n, gain):
            for k in range(CT):
                dve.wait_ge(hh_ready, NORM_TILES[n] + k + 1)
                nc.vector.scalar_tensor_tensor(out=HL[:, k, :], in0=X[:, k, :], scalar=pcol(gain[0], gain[1] + k),
                                               in1=HH[:, k, :].bitcast(fp32), op0=ALU.mult, op1=ALU.subtract)\
                    .then_inc(hl_ready, 1)

        def act_root(act, n, st_wait):
            act.wait_ge(*st_wait)
            if n == 0:
                act.wait_ge(eps_ready, 1)
            nc.scalar.activation(std[:, :], ST[:, 0:L], ACT.Sqrt, bias=eps6[:, 0:1], scale=1.0 / C).then_inc(std_ready, 1)

        def dve_root(dve, n):
            dve.wait_ge(std_ready, n + 1)
            nc.vector.reciprocal(rstd[:, :], std[:, :]).then_inc(rstd_ready, 1)

        def act_ffn(act, n, s0, q0):
            p0 = s0 % 2
            next_hi(act, s0 + 1)
            act_root(act, n, (blocks_done, 3 * s0 + 3))

            def glue(f, o):
                act.wait_ge(gs_ready, 2 * (q0 + f) + 1)
                nc.scalar.activation(sg[:, o, :], gs[:, o, :], ACT.Silu).then_inc(sg_ready, 1)
                act.wait_ge(prod_ready, q0 + f + 1)
                nc.scalar.activation(PH[:, o, :], prod[:, o, :], ACT.Copy).then_inc(ph_ready, 1)
            glue(0, 0)
            with act.Fori(0, (FT - 2) // 2) as i:
                for u in range(2):
                    s = s0 + 2 * i + (2 + u)
                    slot = (p0 + u) % 2
                    split_hi(act, s, slot=slot, uses=16 * i + 16 * ((s0 + 2 + u) // 2 + 1))
                    glue(2 * i + (1 + u), (1 + u) % 2)
            next_hi(act, s0 + FT)
            glue(FT - 1, (FT - 1) % 2)
            next_hi(act, s0 + FT + 1)

        def dve_ffn(dve, n, s0, q0):
            p0 = s0 % 2
            next_lo(dve, s0 + 1)
            dve_root(dve, n)

            def glue(f, o):
                dve.wait_ge(blocks_done, 3 * s0 + 3 * f + 2)
                if isinstance(f, int) and f == 0:
                    dve.wait_ge(rstd_ready, n + 1)
                nc.vector.tensor_tensor(gs[:, o, :], GU[o][:, 0:L], rstd[:, :], ALU.mult).then_inc(gs_ready, 1)
                nc.vector.tensor_tensor(us[:, o, :], GU[o][:, L:2 * L], rstd[:, :], ALU.mult).then_inc(gs_ready, 1)
                dve.wait_ge(sg_ready, q0 + f + 1)
                dve.wait_ge(gs_ready, 2 * (q0 + f + 1))
                nc.vector.tensor_tensor(prod[:, o, :], sg[:, o, :], us[:, o, :], ALU.mult).then_inc(prod_ready, 1)
                dve.wait_ge(ph_ready, q0 + f + 1)
                nc.vector.tensor_tensor(PL[:, o, :], prod[:, o, :], PH[:, o, :].bitcast(fp32), ALU.subtract)\
                    .then_inc(pl_ready, 1)
            glue(0, 0)
            with dve.Fori(0, (FT - 2) // 2) as i:
                for u in range(2):
                    split_lo(dve, s0 + 2 * i + (2 + u), slot=(p0 + u) % 2)
                    glue(2 * i + (1 + u), (1 + u) % 2)
            next_lo(dve, s0 + FT)
            glue(FT - 1, (FT - 1) % 2)
            next_lo(dve, s0 + FT + 1)

        def dve_residual(dve, s, scale):
            for part, js in enumerate(((0, 1), (2,), (3,))):
                dve.wait_ge(blocks_done, 3 * s + part + 1)
                for j in js:
                    last = nc.vector.scalar_tensor_tensor(
                        out=X[:, 2 * j:2 * j + 2, :], in0=DN[j][:, :].rearrange("p (a n) -> p a n", a=2), scalar=scale,
                        in1=X[:, 2 * j:2 * j + 2, :], op0=ALU.mult, op1=ALU.add)
                last.then_inc(x_ready, 1)

        eps6 = sb("eps6", [P, 4])
        NORM_TILES = [0, CT, 2 * CT, 3 * CT, None, 4 * CT]
        arena_offset = nc.sbuf_base
        arena = sb("arena", [P, ARENA])
        at = [0]

        def place(n):
            at[0] += n
            assert at[0] <= ARENA
            return arena[:, at[0] - n:at[0]]
        hcst = place(NHC)
        fw = place(NFW)
        HRI = place(4 * 512).rearrange("p (i k c) -> p i k c", i=2, k=2)
        U3 = place(12 * (L + 2)).rearrange("p (m t) -> p m t", t=L + 2)
        UQ = place(6 * L).rearrange("p (m t) -> p m t", t=L)
        after_u = at[0]
        UC = place(12 * L).rearrange("p (m t) -> p m t", t=L)
        ZT = place(2 * 512).rearrange("p (a c) -> p a c", a=2)
        TM = XSQ[:, :, :].rearrange("p k t -> p (k t)").rearrange("p (i c) -> p i c", i=4)
        at[0] = NHC + NFW + 4 * 512
        YRI = place(4 * 512).rearrange("p (i k c) -> p i k c", i=2, k=2)
        at[0] = NHC + NFW + 4 * 512
        HFB = place(4 * 512).rearrange("p (i a c) -> p i a c", i=2, a=2)
        ABS = place(4 * 512).rearrange("p (i a c) -> p i a c", i=2, a=2)
        HSD = place(4 * 512).rearrange("p (i a c) -> p i a c", i=2, a=2)
        FARG = place(3 * L).rearrange("p (i t) -> p i t", i=3)
        FHID = place(3 * L).rearrange("p (i t) -> p i t", i=3)
        at[0] = after_u
        QN = place(4 * L).rearrange("p (m t) -> p m t", t=L)
        KN = place(2 * L).rearrange("p (m t) -> p m t", t=L)
        VT = place(2 * P).rearrange("p (a c) -> p a c", a=2)
        SC = place(2 * 512).rearrange("p (o a k) -> p o a k", o=2, a=2)
        EX = place(2 * 512).rearrange("p (o a k) -> p o a k", o=2, a=2)
        PT = place(2 * 512).rearrange("p (o b q) -> p o b q", o=2, b=2)
        RN = sg[0:16, :, :]
        small = sb("small", [P, 64])
        hy_rnorm = small[:, 0:4]
        amax, anegm, asum, aes, aden, arden = (small[:, 4 + 2 * k:6 + 2 * k] for k in range(6))
        ymix = prod
        sel = ccols("sel", CT * 16).rearrange("p (j h) -> p j h", h=16)
        selt = ccols("selt", CT * P)[0:16, :].rearrange("p (j c) -> p j c", c=P)
        ident = ccols("ident", P)

        def hc(name, n):
            return hcst[:, HC[name]:HC[name] + n]
        dft = [hc(n, 2 * L).rearrange("p (a k) -> p a k", a=2) for n in ("cos", "sin")]
        idft = [hc(n, 2 * L).rearrange("p (k t) -> p k t", k=2) for n in ("icos", "isin")]
        window = hc("window", 1024).rearrange("p (a c) -> p a c", a=2)
        dist = hc("dist", 2 * L).rearrange("p (a k) -> p a k", a=2)
        FO = FILTER_ORDER
        INV2PI = 1.0 / (2.0 * math.pi)
        ROUND = 1.5 * 2.0 ** 23
        PI2 = [6.28125, float(np.float32(2 * math.pi - 6.28125))]
        PI2.append(2 * math.pi - PI2[0] - PI2[1])
        SLOPES = [2.0 ** (-8.0 * (h + 1) / NQ) for h in range(NQ)]

        eps_ready = sem("eps_ready")
        dve_own = sem("dve_own")
        flt_mm = sem("flt_mm")
        flt_arg = sem("flt_arg")
        flt_sin = sem("flt_sin")
        flt_win = sem("flt_win")
        flt_abs = sem("flt_abs")
        flt_sum = sem("flt_sum")
        flt_h = sem("flt_h")
        u_ready = sem("u_ready")
        cv_ready = sem("cv_ready")
        qsq_ready = sem("qsq_ready")
        ss_done = sem("ss_done")
        root_ready = sem("root_ready")
        rec_ready = sem("rec_ready")
        bc_done = sem("bc_done")
        qn_ready = sem("qn_ready")
        z_ready = sem("z_ready")
        zt_done = sem("zt_done")
        zt_ready = sem("zt_ready")
        zf_done = sem("zf_done")
        y_spec = sem("y_spec")
        yi_done = sem("yi_done")
        ym_ready = sem("ym_ready")
        ks_done = sem("ks_done")
        ks_ready = sem("ks_ready")
        mix_hh = sem("mix_hh")
        mix_hl = sem("mix_hl")
        st_ready = sem("st_ready")
        sc_done = sem("sc_done")
        sc_ready = sem("sc_ready")
        ex_ready = sem("ex_ready")
        pr_ready = sem("pr_ready")
        pt_done = sem("pt_done")
        pt_ready = sem("pt_ready")
        pv_done = sem("pv_done")

        class Own:
            def __init__(self, eng, s, before=0):
                self.eng, self.s, self.before, self.n = eng, s, before, 0

            def __call__(self, ins):
                ins.then_inc(self.s, 1)
                self.n = self.n + 1

            def settle(self):
                self.eng.wait_ge(self.s, self.before + self.n)

            def enter(self, per):
                self.start, self.per = self.n, per

            def at(self, i):
                self.before, self.n = self.start + i * self.per, 0

            def leave(self, times):
                assert self.n == self.per, self.n
                self.before, self.n = 0, self.start + times * self.per

        def pe_filter(pe):
            b3 = bank[3]
            nc.tensor.matmul(b3[0:FO, 0:L], fw[0:FILTER_EMB, 0:FO], hc("feat", L)[0:FILTER_EMB, :],
                             start=True, stop=True).then_inc(flt_mm, 1)
            for n in (1, 2):
                pe.wait_ge(flt_sin, n)
                nc.tensor.matmul(b3[0:FO, 0:L], fw[0:FO, n * FO:(n + 1) * FO], FHID[0:FO, n - 1, :],
                                 start=True, stop=True).then_inc(flt_mm, 1)
            pe.wait_ge(flt_sin, 3)
            for a in range(2):
                for i in range(2):
                    last = nc.tensor.matmul(DN[2 * a + i][:, :], FHID[0:FO, 2, a * P:(a + 1) * P],
                                            fw[0:FO, 3 * FO + 512 * i:3 * FO + 512 * (i + 1)], start=True, stop=True)
            last.then_inc(flt_mm, 1)
            pe.wait_ge(flt_abs, 1)
            for c in range(HT):
                for n in range(4):
                    last = nc.tensor.matmul(b3[:, c:c + 1], ABS[:, n // 2, n % 2, c * P:(c + 1) * P], ones[:, 0:1],
                                            start=n == 0, stop=n == 3)
            last.then_inc(flt_mm, 1)
            pe.wait_ge(flt_sum, 1)
            for i in range(2):
                for k in range(2):
                    for a in range(2):
                        last = nc.tensor.matmul(DN[2 * i + k][:, :], dft[i][:, a, k * P:(k + 1) * P], HSD[:, i, a, :],
                                                start=a == 0, stop=a == 1)
            last.then_inc(flt_mm, 1)

        def act_filter(act):
            for n in range(3):
                act.wait_ge(flt_arg, n + 1)
                nc.scalar.activation(FHID[0:FO, n, :], FARG[0:FO, 0, :], ACT.Sin).then_inc(flt_sin, 1)
            act.wait_ge(flt_win, 1)
            nc.scalar.activation(ABS[:, :, :, :], HFB[:, :, :, :], ACT.Abs).then_inc(flt_abs, 1)
            act.wait_ge(flt_mm, 6)
            for n in range(4):
                last = nc.scalar.activation(HRI[:, n // 2, n % 2, :], DN[n][:, :], ACT.Copy)
            last.then_inc(flt_h, 1)

        def dve_filter(dve, own):
            ts, stt = nc.vector.tensor_scalar, nc.vector.scalar_tensor_tensor
            x, k = FARG[0:FO, 0, :], FARG[0:FO, 1, :]
            for n in range(3):
                dve.wait_ge(flt_mm, n + 1)
                if n:
                    dve.wait_ge(flt_sin, n)
                own(ts(x, bank[3][0:FO, 0:L], pcol("f_b", n)[0:FO], pcol("freq")[0:FO], ALU.add, ALU.mult))
                own.settle()
                own(ts(k, x, INV2PI, ROUND, ALU.mult, ALU.add))
                own.settle()
                own(ts(k, k, -ROUND, None, ALU.add))
                for c in PI2:
                    own.settle()
                    own(stt(out=x, in0=k, scalar=-c, in1=x, op0=ALU.mult, op1=ALU.add))
                own.settle()
                ts(x, x, 3.1415925, -3.1415925, ALU.min, ALU.max).then_inc(flt_arg, 1)
            dve.wait_ge(flt_mm, 4)
            for a in range(2):
                for i in range(2):
                    own(nc.vector.tensor_tensor(HFB[:, i, a, :], DN[2 * a + i][:, :], window[:, a, :], ALU.mult))
            own.settle()
            own(nc.vector.tensor_tensor(HFB[0:1, 0, 0, :], HFB[0:1, 0, 0, :], HFB[0:1, 1, 0, :], ALU.add))
            own.settle()
            nc.vector.memset(HFB[0:1, 1, 0, :], 0.0).then_inc(flt_win, 1)
            dve.wait_ge(flt_win, 1)
            nc.vector.tensor_tensor(HSD[:, 0, :, :], HFB[:, 0, :, :], HFB[:, 1, :, :], ALU.add)
            nc.vector.tensor_tensor(HSD[:, 1, :, :], HFB[:, 0, :, :], HFB[:, 1, :, :], ALU.subtract).then_inc(flt_sum, 1)
            dve.wait_ge(flt_mm, 5)
            own(nc.vector.reciprocal(hy_rnorm, bank[3][:, 0:HT]))
            dve.wait_ge(flt_mm, 6)
            own(nc.vector.memset(U3[:, :, 0:1], 0.0))
            own(nc.vector.memset(U3[:, :, L + 1:L + 2], 0.0))

        UB = [GU[0], GU[1], bank[3]]

        def pe_mix0(pe):
            s0, n = S_IN, 1
            for m in range(18):
                s, b = s0 + m // 3, m % 3
                if b == 0:
                    pe.wait_ge(lo_ready, s + 1)
                if m >= 3:
                    pe.wait_ge(u_ready, m - 2)
                wait = (lambda k: pe.wait_ge(hl_ready, NORM_TILES[n] + k + 1)) if m == 0 else None
                project(UB[m % 3][:, 0:L], s % 2, b, wait=wait).then_inc(blocks_done, 1)
                if m == 0:
                    pe_stats(pe, n).then_inc(st_ready, 1)
            pe.wait_ge(qsq_ready, 5)
            pe.wait_ge(u_ready, 16)
            for j in range(5):
                last = nc.tensor.matmul(GU[0][0:16, 0:L], sel[:, j, :], XSQ[:, j, :], start=j == 0, stop=j == 4)
            last.then_inc(ss_done, 1)
            pe.wait_ge(z_ready, 1)
            for a in range(2):
                for c in range(HT):
                    last = nc.tensor.transpose(DN[a][:, c * P:(c + 1) * P], UC[:, 8 + c, a * P:(a + 1) * P], ident)
            last.then_inc(zt_done, 1)
            pe.wait_ge(u_ready, 18)
            pe.wait_ge(rec_ready, 1)
            for j in range(5):
                dst = (bank[3], GU[1], GU[0])[j // 2][:, (j % 2) * L:(j % 2) * L + L]
                last = nc.tensor.matmul(dst, selt[:, j, :], RN[:, 1, :], start=True, stop=True)
            last.then_inc(bc_done, 1)
            pe.wait_ge(zt_ready, 1)
            for i in range(2):
                for k in range(2):
                    for a in range(2):
                        last = nc.tensor.matmul(DN[2 * i + k][:, :], dft[i][:, a, k * P:(k + 1) * P], ZT[:, a, :],
                                                start=a == 0, stop=a == 1)
            last.then_inc(zf_done, 1)
            pe.wait_ge(y_spec, 1)
            for c in range(HT):
                for n in range(4):
                    last = nc.tensor.matmul(DN[c][:, 0:L], YRI[:, n // 2, n % 2, c * P:(c + 1) * P],
                                            idft[n // 2][:, n % 2, :], start=n == 0, stop=n == 3)
                last.then_inc(yi_done, 1)
            pe.wait_ge(qn_ready, 5)
            nc.tensor.matmul(GU[0][:, L:2 * L], ccols("perm", P), KN[:, 0, :], start=True, stop=True).then_inc(ks_done, 1)
            for a in range(2):
                last = nc.tensor.transpose(ST[:, a * P:(a + 1) * P], UQ[:, 5, a * P:(a + 1) * P], ident)
            last.then_inc(zt_done, 1)
            pe.wait_ge(ks_ready, 1)
            pe.wait_ge(zt_ready, 2)
            pe.wait_ge(ym_ready, HT)

            def scores(h):
                if h >= 2:
                    pe.wait_ge(sc_ready, h - 1)
                r = slice(HD * (h % 2), HD * (h % 2) + HD)
                kn = KN[r, 0 if h % 2 == h // 4 else 1, :]
                for a in range(2):
                    last = nc.tensor.matmul(DN[h % 2][:, a * L:(a + 1) * L], QN[r, h // 2, a * P:(a + 1) * P], kn,
                                            start=True, stop=True)
                last.then_inc(sc_done, 1)
            scores(0)
            for h in range(NQ):
                if h + 1 < NQ:
                    scores(h + 1)
                pe.wait_ge(pr_ready, h + 1)
                if h >= 2:
                    pe.wait_ge(pt_ready, h - 1)
                for b in range(2):
                    for a in range(2):
                        last = nc.tensor.transpose(DN[2 + h % 2][:, b * L + a * P:b * L + (a + 1) * P],
                                                   SC[:, h % 2, a, b * P:(b + 1) * P], ident)
                last.then_inc(pt_done, 1)
                pe.wait_ge(pt_ready, h + 1)
                if h >= 4 and h % 2 == 0:
                    pe.wait_ge(ym_ready, HT + (h - 4) // 2 + 1)
                kv, r = h // 4, slice(HD * (h % 2), HD * (h % 2) + HD)
                for b in range(2):
                    last = nc.tensor.matmul(GU[(h // 2) % 2][r, 0:L], VT[:, b, kv * HD:(kv + 1) * HD],
                                            PT[:, h % 2, b, :], start=b == 0, stop=b == 1)
                last.then_inc(pv_done, 1)
            pe_out(pe, S_OUT)

        def pe_out(pe, s0):
            for m in range(CT):
                s, b = s0 + m // 3, m % 3
                if b == 0:
                    pe.wait_ge(lo_ready, s + 1)
                dst = DN[m // 2][:, (m % 2) * L:(m % 2) * L + L]
                for k in range(CT):
                    if m == 0:
                        pe.wait_ge(mix_hl, (CT if s0 == S_O else 0) + k + 1)
                    last = three(dst, b * BLK + k * P, s % 2, HH[:, k, :], HL[:, k, :], k == 0, k == CT - 1)
                    if m == CT - 1 and k == 3:
                        last.then_inc(blocks_done, 1)
                last.then_inc(blocks_done, 1)

        def dve_out(dve, s0):
            for part, (js, done) in enumerate((((0, 1), 4), ((2,), 6), ((3,), 9))):
                dve.wait_ge(blocks_done, 3 * s0 + done)
                for j in js:
                    last = nc.vector.tensor_tensor(X[:, 2 * j:2 * j + 2, :], DN[j][:, :].rearrange("p (a n) -> p a n", a=2),
                                                   X[:, 2 * j:2 * j + 2, :], ALU.add)
                last.then_inc(x_ready, 1)

        def act_mix0(act):
            act_root(act, 1, (st_ready, 1))
            for m in range(18):
                if m % 3 == 0:
                    next_hi(act, S_IN + m // 3 + 1)
                act.wait_ge(u_ready, m + 1)
                if m < 12:
                    nc.scalar.activation(UC[:, m, :], U3[:, m, 1:L + 1], ACT.Identity, bias=pcol("conv_b", m),
                                         scale=pcol("conv_w", 12 + m)).then_inc(cv_ready, 1)
                elif m < 17:
                    nc.scalar.activation(XSQ[:, m - 12, :], UQ[:, m - 12, :], ACT.Square).then_inc(qsq_ready, 1)
            act.wait_ge(ss_done, 1)
            nc.scalar.activation(RN[:, 0, :], GU[0][0:16, 0:L], ACT.Sqrt, bias=eps6[0:16, 0:1], scale=1.0 / HD)\
                .then_inc(root_ready, 1)
            act.wait_ge(zt_done, 1)
            for a in range(2):
                last = nc.scalar.activation(ZT[:, a, :], DN[a][:, :], ACT.Copy)
            last.then_inc(zt_ready, 1)
            for c in range(HT):
                act_mixed(act, c)
            act.wait_ge(ks_done, 1)
            nc.scalar.activation(KN[:, 1, :], GU[0][:, L:2 * L], ACT.Copy).then_inc(ks_ready, 1)
            act.wait_ge(zt_done, 2)
            nc.scalar.activation(VT[:, :, :], ST[:, 0:2 * P].rearrange("p (a c) -> p a c", a=2), ACT.Copy)\
                .then_inc(zt_ready, 1)
            for h in range(NQ):
                act.wait_ge(sc_ready, h + 1)
                for a in range(2):
                    nc.scalar.activation(EX[:, h % 2, a, :], SC[:, h % 2, a, :], ACT.Exp, bias=anegm[:, a:a + 1],
                                         accum_out=asum[:, a:a + 1])
                nc.scalar.activation(aes, anegm, ACT.Exp, bias=pcol("sink", h)).then_inc(ex_ready, 1)
                act.wait_ge(pt_done, h + 1)
                nc.scalar.activation(PT[:, h % 2, :, :], DN[2 + h % 2][:, :].rearrange("p (b q) -> p b q", b=2), ACT.Copy)\
                    .then_inc(pt_ready, 1)
                if h % 2:
                    act_mixed(act, HT + h // 2)

        def act_mixed(act, t, base=0):
            act.wait_ge(ym_ready, base + t + 1)
            nc.scalar.activation(HH[:, t, :], ymix[:, t % 2, :], ACT.Copy).then_inc(mix_hh, 1)

        def dve_mixed(dve, t, base=0):
            dve.wait_ge(mix_hh, base + t + 1)
            nc.vector.tensor_tensor(HL[:, t, :], ymix[:, t % 2, :], HH[:, t, :].bitcast(fp32), ALU.subtract)\
                .then_inc(mix_hl, 1)

        def dve_mix0(dve, own):
            tt, stt = nc.vector.tensor_tensor, nc.vector.scalar_tensor_tensor
            dve_root(dve, 1)
            dve.wait_ge(rstd_ready, 2)
            own.settle()
            dve.wait_ge(flt_h, 1)

            def conv(m):
                dve.wait_ge(cv_ready, m + 1)
                own(stt(out=UC[:, m, :], in0=U3[:, m, 0:L], scalar=pcol("conv_w", m), in1=UC[:, m, :],
                        op0=ALU.mult, op1=ALU.add))
                own.settle()
                own(stt(out=UC[:, m, :], in0=U3[:, m, 2:L + 2], scalar=pcol("conv_w", 24 + m), in1=UC[:, m, :],
                        op0=ALU.mult, op1=ALU.add))
            for m in range(18):
                if m % 3 == 0:
                    next_lo(dve, S_IN + m // 3 + 1)
                dve.wait_ge(blocks_done, 3 * S_IN + m + 1)
                dst = U3[:, m, 1:L + 1] if m < 12 else UQ[:, m - 12, :]
                tt(dst, UB[m % 3][:, 0:L], rstd[:, :], ALU.mult).then_inc(u_ready, 1)
                if 1 <= m <= 12:
                    conv(m - 1)
                if m == 12:
                    own.settle()
                    tt(UC[:, 8:12, :], UC[:, 8:12, :], UC[:, 4:8, :], ALU.mult).then_inc(z_ready, 1)
            dve.wait_ge(root_ready, 1)
            nc.vector.reciprocal(RN[:, 1, :], RN[:, 0, :]).then_inc(rec_ready, 1)
            dve.wait_ge(zf_done, 1)
            for k in range(2):
                for n in range(4):
                    i, o = ((0, 0), (1, 1), (0, 1), (1, 0))[n]
                    own(tt(TM[:, n, :], HRI[:, i, k, :], DN[2 * o + k][:, :], ALU.mult))
                own.settle()
                own(tt(YRI[:, 0, k, :], TM[:, 0, :], TM[:, 1, :], ALU.subtract))
                ins = tt(YRI[:, 1, k, :], TM[:, 2, :], TM[:, 3, :], ALU.add)
                if k:
                    ins.then_inc(y_spec, 1)
                else:
                    own(ins)
                    own.settle()
            for c in range(HT):
                if c >= 2:
                    dve.wait_ge(mix_hh, c - 1)
                y = ymix[:, c % 2, :]
                own(nc.vector.tensor_scalar(y, UC[:, 8 + c, :], pcol("hy_bias", c), None, ALU.mult))
                own.settle()
                dve.wait_ge(yi_done, c + 1)
                own(stt(out=y, in0=DN[c][:, 0:L], scalar=hy_rnorm[:, c:c + 1], in1=y, op0=ALU.mult, op1=ALU.add))
                own.settle()
                tt(y, y, UC[:, c, :], ALU.mult).then_inc(ym_ready, 1)
                dve_mixed(dve, c)
            dve.wait_ge(bc_done, 1)
            dve.wait_ge(zt_ready, 1)
            dve.wait_ge(ym_ready, HT)
            for j in range(5):
                src = (bank[3], GU[1], GU[0])[j // 2][:, (j % 2) * L:(j % 2) * L + L]
                if j < 4:
                    stt(out=QN[:, j, :], in0=UQ[:, j, :], scalar=pcol("q_gain"), in1=src, op0=ALU.mult, op1=ALU.mult)\
                        .then_inc(qn_ready, 1)
                else:
                    own(nc.vector.tensor_scalar(UQ[:, j, :], UQ[:, j, :], pcol("k_gain"), HD ** -0.5, ALU.mult, ALU.mult))
                    own.settle()
                    tt(KN[:, 0, :], UQ[:, j, :], src, ALU.mult).then_inc(qn_ready, 1)
            for h in range(NQ):
                o = h % 2
                dve.wait_ge(sc_done, h + 1)
                if h >= 2:
                    dve.wait_ge(pt_done, h - 1)
                own(stt(out=SC[:, o, :, :], in0=dist[:, :, :], scalar=-SLOPES[h],
                        in1=DN[o][:, :].rearrange("p (a k) -> p a k", a=2), op0=ALU.mult, op1=ALU.add))
                own.settle()
                if h:
                    dve.wait_ge(ex_ready, h)
                own(nc.vector.tensor_reduce(amax, SC[:, o, :, :], AX.X, ALU.max))
                own.settle()
                nc.vector.tensor_scalar(anegm, amax, pcol("sink", h), -1.0, ALU.max, ALU.mult).then_inc(sc_ready, 1)
                dve.wait_ge(ex_ready, h + 1)
                own(tt(aden, asum, aes, ALU.add))
                own.settle()
                own(nc.vector.reciprocal(arden, aden))
                own.settle()
                for a in range(2):
                    last = nc.vector.tensor_scalar(SC[:, o, a, :], EX[:, o, a, :], arden[:, a:a + 1], None, ALU.mult)
                last.then_inc(pr_ready, 1)
                if o:
                    t = HT + h // 2
                    dve.wait_ge(pv_done, h + 1)
                    dve.wait_ge(mix_hh, t - 1)
                    nc.vector.tensor_copy(ymix[:, t % 2, :], GU[(h // 2) % 2][:, 0:L]).then_inc(ym_ready, 1)
                    dve_mixed(dve, t)
        LOADS = 80

        at[0] = 0
        R, K, V = (place(CT * L) for _ in range(3))
        LW = place(2 * CT * L)
        XI4, XI5 = (LW[:, n * CT * L:(n + 1) * CT * L].rearrange("p (k t) -> p k t", t=L) for n in range(2))
        place(-(arena_offset // 4 + at[0]) % 8)
        ag_at = at[0]
        AG = place(2 * CT * L)
        mixparts = nc.alloc_sbuf_tensor_at("mixparts", [P, 2, CT, L], f32r, offset=arena_offset + 4 * ag_at)
        PARTS = [(HH, HL), (mixparts[:, 0], mixparts[:, 1])]
        h_at = at[0]
        H = place(CT * (L + 2)).rearrange("p (k t) -> p k t", t=L + 2)
        XX = XSQ
        xi = work[:, :, :, :].rearrange("p i o t -> p (i o) t")
        XI = [xi] * 4 + [XI4, XI5]
        KSQ = xi
        at[0] = h_at
        KK = place(CT * L + 16)[:, 0:CT * L]
        CI = place(2 * L)
        HID = CI.rearrange("p (i t) -> p i t", i=2)
        fixed = [[scan2, 2 * CT * L, 0], [work[:, :, :, :].rearrange("p i o t -> p (i o t)"), 8 * L, 0],
                 [XSQ[:, :, :].rearrange("p k t -> p (k t)"), CT * L, 0], [arena, ARENA, at[0]]]
        weights = [[scan, 4 * 3 * BLK, 0], [raw[:, :, :].rearrange("p s n -> p (s n)"), 6 * BLK, 0]]

        def splace(n, pools=None):
            for pool in pools or weights + fixed:
                if pool[2] + n <= pool[1]:
                    pool[2] += n
                    return pool[0][:, pool[2] - n:pool[2]]
            raise ValueError((n, [p[1] - p[2] for p in weights + fixed]))

        def bd(n=NU, pools=None):
            return splace(n * P, pools).rearrange("p (u h s) -> p u h s", h=2, s=CH)

        def full(n=NU, pools=None):
            return splace(n * P, pools).rearrange("p (u c) -> p u c", c=P)

        def pair(f, n=NU):
            return [f(n), f(n, fixed)]
        landed = [weights[1]]
        ALB, BTB = ([bd(pools=landed), bd(pools=fixed)] for _ in range(2))
        BEB, KAB, QBD = (bd(pools=landed) for _ in range(3))
        VB = bd(NCH, landed)
        CE = splace(2 * L, landed)
        KTK, BTK = pair(full), pair(full)
        AR = [a.rearrange("p u (i t) -> p u i t", i=2) for a in pair(full)]
        AQ, BQ = pair(full), pair(full)
        QF = full(pools=fixed)
        VTK = pair(full, NCH)
        ABD, TBD, ZBD, XLV = (full() for _ in range(4))
        E2, E3, KD, BB = (splace(2 * L) for _ in range(4))
        E1, KAT, BE = CE, E2, BB
        RCH, UCH, SCH0 = (full(2, fixed) for _ in range(3))
        SCH = (SCH0, std[:, :].rearrange("p (z v) -> p z v", z=2))
        TMPK = splace(L)
        RB = TMPK
        etot = [small[:, 40:48], small[:, 48:56]]
        omk = small[:, 24:24 + CT]
        GH, GL = sb("GH", [P, 2, L], f32r), sb("GL", [P, 2, L], f32r)
        blockones, istack = ccols("blockones", P), ccols("istack", CH)

        def mask64(name, z):
            return ccols(name, CH, z * CH).rearrange("p (o s) -> p o s", o=1).broadcast_to([P, 2 * NCH, CH])

        def blocks(a, z):
            return a[:, z * NCH:(z + 1) * NCH, :].rearrange("p c (h s) -> p (c h) s", h=2)

        def mask(name, z):
            return ccols(name, P, z * P).rearrange("p (o s) -> p o s", o=1).broadcast_to([P, NCH, P])

        mx_hh, mx_hl = sem("mx_hh"), sem("mx_hl")
        xi_ready = sem("xi_ready")
        xp_ready = sem("xp_ready")
        hx_ready = sem("hx_ready")
        pool_own = sem("pool_own")
        zeros_ready = sem("zeros_ready")
        rkv_ready = sem("rkv_ready")
        lr_done = sem("lr_done")
        lr_ready = sem("lr_ready")
        lr_hi, lr_lo = sem("lr_hi"), sem("lr_lo")
        kk_sq, kk_ss, kk_max, kk_root, kk_rec, kk_bc, kk_ready = (sem(f"kk_{n}") for n in
                                                                "sq ss max root rec bc ready".split())
        ka_ready, c_ready, e_ready = sem("ka_ready"), sem("c_ready"), sem("e_ready")
        tm_ready, rb_ready, bo_done, bo_read = sem("tm_ready"), sem("rb_ready"), sem("bo_done"), sem("bo_read")
        kd_ready, al_ready, be_ready, bd_ready = sem("kd_ready"), sem("al_ready"), sem("be_ready"), sem("bd_ready")
        tr_done, tr_ready, a_done, a_ready = sem("tr_done"), sem("tr_ready"), sem("a_done"), sem("a_ready")
        aq_done, bq_done, x0_ready = sem("aq_done"), sem("bq_done"), sem("x0_ready")
        abd_ready, bt_ready, kab_ready = sem("abd_ready"), sem("bt_ready"), sem("kab_ready")
        xl_ready, z_done, zb_ready, d_done, t_ready = (sem(n) for n in "xl_ready z_done zb_ready d_done t_ready".split())
        r_done, r_ready, uu_done, uu_ready, y_done, s_done, s_ready = (
            sem(n) for n in "r_done r_ready uu_done uu_ready y_done s_done s_ready".split())
        yt_ready = sem("yt_ready")
        gn_mean, gn_sq, gn_ss, gn_root, gn_rec, gn_bc, gn_af, gn_c = (sem(f"gn_{n}") for n in
                                                                      "mean sq ss root rec bc af c".split())
        g_done, gn_n = sem("g_done"), sem("gn_n")
        MIXES = [0, 2, 3, 1, 4, 5]

        OUTS = [CT, CT, CT, 1, 1, 2]
        FIRST = [0, CT, 2 * CT, 24, 25, 26]

        def pe_mix1(pe):
            s0, n = S_RKV, 4
            pe_stats(pe, n).then_inc(st_ready, 1)
            q = 0
            for i in range(6):
                for m in range(OUTS[i]):
                    g = FIRST[i] + m
                    s, b = s0 + g // 3, g % 3
                    if b == 0:
                        pe.wait_ge(lo_ready, s + 1)
                    if g >= 3:
                        pe.wait_ge(rkv_ready, g - 2)
                    wait = (lambda k: pe.wait_ge(mx_hl, CT * i + k + 1)) if m == 0 else None
                    project(UB[g % 3][:, 0:L], s % 2, b, inp=PARTS[i % 2], wait=wait).then_inc(blocks_done, 1)
                if i == 4:
                    pe.wait_ge(kk_sq, CT)
                    for j in range(CT):
                        last = nc.tensor.matmul(ST[0:16, 0:L], sel[:, j, :], KSQ[:, j, :], start=j == 0, stop=j == CT - 1)
                    last.then_inc(kk_ss, 1)
            for i in range(2):
                pe.wait_ge(lr_lo, i + 1)
                s, b = S_LORA + 1, 1 + i
                for m in range(CT):
                    for z in range(2):
                        if q >= 3:
                            pe.wait_ge(lr_ready, q - 2)
                        else:
                            pe.wait_ge(rkv_ready, 28)
                        r = slice(64 * z, 64 * z + 64)
                        ins = three(UB[q % 3][:, 0:L], b * BLK + m * P, s % 2, PH[r, i, :], PL[r, i, :], True, True,
                                    rows=r)
                        if m == CT - 1 and z == 1:
                            ins.then_inc(blocks_done, 1)
                        else:
                            ins.then_inc(lr_done, 1)
                        q += 1
                    if i == 0:
                        pe.wait_ge(kk_rec, 1)
                        nc.tensor.matmul(DN[m // 2][:, (m % 2) * L:(m % 2) * L + L], selt[:, m, :], RN[:, 1, :],
                                         start=True, stop=True).then_inc(kk_bc, 1)
            pe.wait_ge(kk_ready, 1)
            tiles(pe, lambda t, p, c, a: pe_tile(pe, t, p, c, a))
            fill = [[lambda: pe_mean(pe, (0, 1)), lambda: pe_mean(pe, (2, 3)), lambda: pe_mean(pe, (4, 5, 6))],
                    [lambda: pe_ss(pe, (0, 1)), lambda: pe_ss(pe, (2, 3)), lambda: None],
                    [lambda: pe_ss(pe, (4, 5)), lambda: pe_ss(pe, (6,)), lambda: None], [lambda: None] * 3]
            for i in range(NCH):
                pe_r(pe, CT - 1, 1, i)
                fill[i][0]()
                pe_u(pe, CT - 1, i)
                fill[i][1]()
                pe_s(pe, CT - 1, 1, i)
                pe_y(pe, CT - 1, 1, i)
                fill[i][2]()
            pe_groupnorm(pe)

        def tiles(eng, body, own=None):
            body(0, 0, False, True)
            if own:
                own.enter(SCAN_OWN)
            with eng.Fori(0, (CT - 2) // 2) as i:
                if own:
                    own.at(i)
                for o in range(2):
                    body(2 * i + (1 + o), (1 + o) % 2, True, True)
            if own:
                own.leave((CT - 2) // 2)
            body(CT - 1, (CT - 1) % 2, True, False)

        def flat(a):
            return a.rearrange("p h s -> p (h s)")

        def units(i):
            return (i, 2 * NCH - 1 - i)

        def pe_bonus(pe, t):
            pe.wait_ge(rb_ready, t + 1)
            nc.tensor.matmul(bank[7][:, 0:L], blockones, RB, start=True, stop=True).then_inc(bo_done, 1)

        def pe_tr(pe, t, n):
            if n:
                pe.wait_ge(tr_ready, 5 * t + n)
            else:
                pe.wait_ge(a_ready, 2 * t + 2)
                pe.wait_ge(bd_ready, 3 * t + 1)
            for c in range(NCH):
                src = VB[:, c] if n == 0 else (KAB, BEB)[(n - 1) // 2][:, (n - 1) % 2 * NCH + c]
                last = nc.tensor.transpose(bank[7][:, c * P:(c + 1) * P], flat(src), ident)
            last.then_inc(tr_done, 1)

        def pe_r(pe, t, p, i):
            for z, u in enumerate(units(i)):
                dst = bank[4][:, z * P:(z + 1) * P]
                if i:
                    pe.wait_ge(s_ready, 6 * t + 2 * i)
                    pe.wait_ge(uu_ready, 4 * t + i)
                    nc.tensor.matmul(dst, flat(ALB[p][:, u]), SCH[i % 2][:, z, :], start=True, stop=False)
                elif z == 0:
                    pe.wait_ge(tr_ready, 5 * t + 5)
                    pe.wait_ge(t_ready, 12 * t + 12)
                    pe.wait_ge(bt_ready, t + 1)
                last = nc.tensor.matmul(dst, flat(BTB[p][:, u]), VTK[p][:, u % NCH, :], start=i == 0, stop=True)
            last.then_inc(r_done, 1)

        def pe_u(pe, t, i):
            pe.wait_ge(r_ready, 4 * t + i + 1)
            for z, u in enumerate(units(i)):
                last = nc.tensor.matmul(bank[4][:, z * P:(z + 1) * P], QF[:, u, :], RCH[:, z, :], start=True, stop=True)
            last.then_inc(uu_done, 1)

        def pe_s(pe, t, p, i):
            if i == NCH - 1:
                return
            pe.wait_ge(uu_ready, 4 * t + i + 1)
            for z, u in enumerate(units(i)):
                dst = bank[5][:, z * P:(z + 1) * P]
                if i:
                    nc.tensor.matmul(dst, ident, SCH[i % 2][:, z, :], start=True, stop=False)
                nc.tensor.matmul(dst, KTK[p][:, u, :], VTK[p][:, u % NCH, :], start=i == 0, stop=False)
                last = nc.tensor.matmul(dst, BTK[p][:, u, :], UCH[:, z, :], start=False, stop=True)
            last.then_inc(s_done, 1)

        def pe_y(pe, t, p, i):
            if i == 0:
                pe.wait_ge(yt_ready, t + 1)
            pe.wait_ge(uu_ready, 4 * t + i + 1)
            for z, u in enumerate(units(i)):
                c = u % NCH
                dst = bank[6][:, c * P:(c + 1) * P]
                nc.tensor.matmul(dst, VTK[p][:, c, :], BQ[p][:, u, :], start=i == 0 and z == 0, stop=False)
                if i:
                    nc.tensor.matmul(dst, SCH[i % 2][:, z, :], flat(AR[p][:, u]), start=False, stop=False)
                last = nc.tensor.matmul(dst, UCH[:, z, :], AQ[p][:, u, :], start=False, stop=i == NCH - 1 and z == 1)
            last.then_inc(y_done, 1)

        def pe_tile(pe, t, p, chunks, ahead):
            mm, B, q = nc.tensor.matmul, bank, 1 - p
            pe.wait_ge(al_ready, 2 * t + 2)
            pe.wait_ge(bd_ready, 3 * t + 2)
            if not (isinstance(t, int) and t == 0):
                pe.wait_ge(t_ready, 12 * t)
            for u in range(NU):
                last = mm(B[2 + u // NCH][:, (u % NCH) * P:(u % NCH + 1) * P], flat(BEB[:, u]), flat(AR[p][:, u]),
                          start=True, stop=True)
            last.then_inc(aq_done, 1)
            pe.wait_ge(bd_ready, 3 * t + 3)
            for u in range(NU):
                last = mm(B[u // NCH][:, (u % NCH) * P:(u % NCH + 1) * P], flat(ALB[p][:, u]), flat(BEB[:, u]),
                          start=True, stop=True)
            last.then_inc(a_done, 1)
            pe.wait_ge(kab_ready, t + 1)
            if not (isinstance(t, int) and t == 0):
                pe.wait_ge(bo_read, t)
            for u in range(NU):
                if u == NCH:
                    pe.wait_ge(abd_ready, 2 * t + 2)
                last = mm(B[(7, 1)[u // NCH]][:, (u % NCH) * P:(u % NCH + 1) * P], flat(KAB[:, u]), flat(AR[p][:, u]),
                          start=True, stop=True)
            last.then_inc(bq_done, 1)
            for n in range(len(LEVELS)):
                step = chunks and n < NCH
                if step:
                    pe_r(pe, t - 1, q, n)
                for z in range(2):
                    if n == 0:
                        pe.wait_ge(x0_ready, 2 * t + z + 1)
                    else:
                        pe.wait_ge(xl_ready, 8 * t + 2 * n + z - 1)
                    if n == 0 and z == 1:
                        pe.wait_ge(a_ready, 2 * t + 1)
                    if n:
                        pe.wait_ge(t_ready, 12 * t + 2 * n + z + 1)
                    for c in range(NCH):
                        u = z * NCH + c
                        last = mm(B[z][:, c * P:(c + 1) * P], XLV[:, u, :], flat(QBD[:, u]), start=True, stop=True)
                    last.then_inc(z_done, 1)
                if n in (1, 2):
                    pe_tr(pe, t, 2 * n)
                if step:
                    pe_u(pe, t - 1, n)
                for z in range(2):
                    pe.wait_ge(zb_ready, 10 * t + 2 * n + z + 1)
                    if n == 0:
                        pe.wait_ge(t_ready, 12 * t + z + 1)
                    for c in range(NCH):
                        u = z * NCH + c
                        last = mm(B[2 + z][:, c * P:(c + 1) * P], TBD[:, u, :], ZBD[:, u, :], start=True, stop=True)
                    if n < len(LEVELS) - 1:
                        for c in range(NCH):
                            u = z * NCH + c
                            last = mm(B[z][:, c * P:(c + 1) * P], ZBD[:, u, :], TBD[:, u, :], start=True, stop=True)
                    last.then_inc(d_done, 1)
                    if z == 0:
                        if n == 0:
                            pe_tr(pe, t, 0)
                        if step:
                            pe_s(pe, t - 1, q, n)
                        if n == 3:
                            if step:
                                pe_y(pe, t - 1, q, n)
                            pe.wait_ge(tr_ready, 5 * t + 5)
                            pe_bonus(pe, t)
                if step and n < 3:
                    pe_y(pe, t - 1, q, n)
                if n < 2:
                    pe_tr(pe, t, 2 * n + 1)

        def halves(fn):
            for h in range(2):
                last = fn(slice(HD * h, HD * h + HD), h)
            return last

        def tile_of(a, j, z=0, n=1):
            return a[:, bass.ds(z * CT * L + j * L, L)]

        def act_operands(act, t, part):
            A, cp, p = nc.scalar.activation, ACT.Copy, None
            if part == 0:
                if not (isinstance(t, int) and t == 0):
                    act.wait_ge(al_ready, 2 * t)
                for z in range(2):
                    last = A(KAT[:, z * L:(z + 1) * L], tile_of(AG, t, z), ACT.Identity,
                             bias=small[:, bass.ds(24 + t, 1)], scale=par[:, bass.ds(COL["k_a"] + t, 1)])
                last.then_inc(ka_ready, 1)
            elif part == 1:
                if not (isinstance(t, int) and t == 0):
                    act.wait_ge(tr_done, 5 * t - 4)
                halves(lambda r, h: A(VB[r, :, h, :], V[r, bass.ds(t * L, L)].rearrange("p (c s) -> p c s", c=NCH), cp))\
                    .then_inc(bd_ready, 1)
                act.wait_ge(c_ready, t + 1)
                if not (isinstance(t, int) and t == 0):
                    act.wait_ge(be_ready, 2 * t)
                A(E1[:, :], CE[:, :], ACT.Exp, scale=-DECAY).then_inc(e_ready, 1)
                A(E3[:, :], CI[:, :], ACT.Exp, scale=DECAY).then_inc(e_ready, 1)
            elif part == 2:
                act.wait_ge(kd_ready, t + 1)
                A(E2[:, :], CI[:, :], ACT.Exp, scale=-DECAY).then_inc(e_ready, 1)

        def act_etot(act, t, p):
            A = nc.scalar.activation
            ci = CI[:, :].rearrange("p (z c t) -> p z c t", z=2, c=NCH)
            for z in range(2):
                last = A(etot[p][:, z * NCH:(z + 1) * NCH], ci[:, z, :, (CH - 1) if z == 0 else 0], ACT.Exp, scale=-DECAY)
            last.then_inc(e_ready, 1)

        def act_beb(act, t):
            A, cp = nc.scalar.activation, ACT.Copy
            act.wait_ge(be_ready, 2 * t + 1)
            if not (isinstance(t, int) and t == 0):
                act.wait_ge(tr_done, 5 * t)
            halves(lambda r, h: A(BEB[r, :, h, :], BE[r, :].rearrange("p (u t) -> p u t", u=NU), cp)).then_inc(bd_ready, 1)

        def act_alb(act, t, p):
            A, cp = nc.scalar.activation, ACT.Copy
            act.wait_ge(al_ready, 2 * t + 1)
            halves(lambda r, h: A(ALB[p][r, :, h, :], AR[p][r, :, 0, :], cp)).then_inc(bd_ready, 1)

        def act_tr(act, t, p, n):
            A, cp = nc.scalar.activation, ACT.Copy
            act.wait_ge(tr_done, 5 * t + n + 1)
            src = bank[7][:, :].rearrange("p (c s) -> p c s", c=NCH)
            dst = VTK[p][:, :, :] if n == 0 else (KTK, BTK)[(n - 1) // 2][p][:, (n - 1) % 2 * NCH:(n - 1) % 2 * NCH + NCH, :]
            A(dst, src, cp).then_inc(tr_ready, 1)

        def act_s(act, t, p, i):
            if i == NCH - 1:
                return
            act.wait_ge(s_done, 3 * t + i + 1)
            for z, u in enumerate(units(i)):
                nc.scalar.activation(SCH[(i + 1) % 2][:, z, :], bank[5][:, z * P:(z + 1) * P], ACT.Copy,
                                     scale=etot[p][:, u:u + 1])\
                    .then_inc(s_ready, 1)

        def act_tile(act, t, p, chunks, ahead):
            A, cp, B, q = nc.scalar.activation, ACT.Copy, bank, 1 - p
            act.wait_ge(a_done, t + 1)
            for z in range(2):
                A(ABD[:, z * NCH:(z + 1) * NCH, :], bank_of(z), cp).then_inc(abd_ready, 1)
            if ahead:
                act_operands(act, t + 1, 0)
            if chunks:
                act.wait_ge(e_ready, 4 * t)
            for n in range(len(LEVELS)):
                step = chunks and n < NCH
                for z in range(2):
                    act.wait_ge(z_done, 10 * t + 2 * n + z + 1)
                    A(ZBD[:, z * NCH:(z + 1) * NCH, :], bank_of(z), cp).then_inc(zb_ready, 1)
                if n < 3:
                    act_tr(act, t, p, 2 * n)
                if n == 0:
                    act.wait_ge(a_ready, 2 * t + 2)
                    halves(lambda r, h: A(BTB[p][r, :, h, :], BQ[p][r, :, 0:CH], cp)).then_inc(bt_ready, 1)
                if step:
                    act_s(act, t - 1, q, n)
                if n < 2:
                    act_tr(act, t, p, 2 * n + 1)
                if ahead and n in (1, 2):
                    act_operands(act, t + 1, n)
                if ahead and n == 3:
                    act_etot(act, t + 1, q)
                    act_beb(act, t + 1)
                if ahead and n == 4:
                    act_alb(act, t + 1, q)

        def dve_prefix(dve, own, t):
            tt, z2 = nc.vector.tensor_tensor, slice(L, 2 * L)
            if not (isinstance(t, int) and t == 0):
                dve.wait_ge(e_ready, 4 * t)
                dve.wait_ge(al_ready, 2 * t)
            for z in range(2):
                own(nc.vector.tensor_tensor_scan(out=(CI if z == 0 else CE)[:, z * L:(z + 1) * L], data0=ccols("reset", L),
                                                 data1=tile_of(LW, t, z), initial=0.0, op0=ALU.mult, op1=ALU.add))
            own.settle()
            own(tt(CE[:, 0:L], CI[:, 0:L], tile_of(LW, t, 0), ALU.subtract))
            p1 = CE[:, z2].rearrange("p (c t) -> p c t", c=NCH)
            own(nc.vector.tensor_copy(small[:, 32:36], p1[:, :, CH - 1]))
            own.settle()
            own(tt(p1, small[:, 32:36].rearrange("p (c o) -> p c o", o=1).broadcast_to([P, NCH, CH]), p1, ALU.subtract))
            own.settle()
            tt(CI[:, z2], CE[:, z2], tile_of(LW, t, 1), ALU.add).then_inc(c_ready, 1)

        def dve_kb(dve, own, t):
            tt = nc.vector.tensor_tensor
            dve.wait_ge(ka_ready, t + 1)
            if not (isinstance(t, int) and t == 0):
                dve.wait_ge(kab_ready, t)
            for z in range(2):
                own(tt(BB[:, z * L:(z + 1) * L], tile_of(AG, t, z), tile_of(KK, t), ALU.mult))
                ins = tt(KD[:, z * L:(z + 1) * L], KAT[:, z * L:(z + 1) * L], tile_of(K, t), ALU.mult)
                if z == 0:
                    own(ins)
            ins.then_inc(kd_ready, 1)

        def dve_rb(dve, t):
            dve.wait_ge(tm_ready, t + 1)
            nc.vector.scalar_tensor_tensor(out=RB, in0=tile_of(R, t), scalar=par[:, bass.ds(COL["r_k"] + t, 1)], in1=TMPK,
                                           op0=ALU.mult, op1=ALU.mult).then_inc(rb_ready, 1)

        def dve_bonus(dve, t):
            dve.wait_ge(bo_done, t + 1)
            dve.wait_ge(kd_ready, t + 1)
            nc.vector.scalar_tensor_tensor(out=tile_of(K, t), in0=bank[7][:, 0:L], scalar=0.5, in1=tile_of(V, t),
                                           op0=ALU.mult, op1=ALU.mult).then_inc(bo_read, 1)

        def dve_alpha(dve, t, p):
            c4 = lambda a: a.rearrange("p (c t) -> p c t", c=NCH)
            dve.wait_ge(e_ready, 4 * t + 1)
            for z in range(2):
                ins = nc.vector.scalar_tensor_tensor(out=AR[p][:, z * NCH:(z + 1) * NCH, 0, :], in0=c4(tile_of(KK, t)),
                                                     scalar=-1.0, in1=c4(E1[:, z * L:(z + 1) * L]), op0=ALU.mult, op1=ALU.mult)
            ins.then_inc(al_ready, 1)
            dve.wait_ge(e_ready, 4 * t + 3)
            for z in range(2):
                ins = nc.vector.tensor_tensor(AR[p][:, z * NCH:(z + 1) * NCH, 1, :], c4(tile_of(R, t)),
                                              c4(E2[:, z * L:(z + 1) * L]), ALU.mult)
            ins.then_inc(al_ready, 1)

        def dve_kappa(dve, own, t):
            dve.wait_ge(be_ready, 2 * t + 2)
            if not (isinstance(t, int) and t == 0):
                dve.wait_ge(tr_done, 5 * t)
            kd = KD.rearrange("p (u t) -> p u t", u=NU)
            own(nc.vector.tensor_copy(KAB[0:HD, :, 0, :], kd[0:HD]))
            nc.vector.tensor_copy(KAB[HD:P, :, 1, :], kd[HD:P]).then_inc(kab_ready, 1)

        def dve_rc(dve, t, i):
            dve.wait_ge(r_done, 4 * t + i + 1)
            nc.vector.tensor_copy(RCH[:, :, :], bank[4][:, 0:2 * P].rearrange("p (z v) -> p z v", z=2)).then_inc(r_ready, 1)

        def dve_uc(dve, t, i):
            dve.wait_ge(uu_done, 4 * t + i + 1)
            nc.vector.tensor_copy(UCH[:, :, :], bank[4][:, 0:2 * P].rearrange("p (z v) -> p z v", z=2)).then_inc(uu_ready, 1)

        def dve_yt(dve, t):
            dve.wait_ge(y_done, 4 * t + 4)
            dve.wait_ge(rb_ready, t + 1)
            nc.vector.tensor_scalar(tile_of(R, t).rearrange("p (c t) -> p c t", c=NCH), bank_of(6)[:, :, CH:P], 1.0, None,
                                    ALU.mult).then_inc(yt_ready, 1)

        def bank_of(n):
            return bank[n][:, :].rearrange("p (c s) -> p c s", c=NCH)

        def dve_tile(dve, t, p, chunks, ahead, own):
            tt, q = nc.vector.tensor_tensor, 1 - p
            group = [slice(z * NCH, (z + 1) * NCH) for z in range(2)]
            dve.wait_ge(aq_done, t + 1)
            for z in range(2):
                own(tt(AQ[p][:, group[z], :], bank_of(2 + z), mask("first_incl", z), ALU.mult))
            own.settle()
            eye = istack.rearrange("p (o s) -> p o s", o=1).broadcast_to([P, NU, CH])
            halves(lambda r, h: own(tt(QBD[r, :, h, :], AQ[p][r, :, 0:CH], eye[r], ALU.add)))
            dve.wait_ge(abd_ready, 2 * t + 2)
            for z in range(2):
                tt(blocks(XLV, z), blocks(ABD, z), mask64("level", z * len(LEVELS)), ALU.mult).then_inc(x0_ready, 1)
            dve.wait_ge(bq_done, t + 1)
            tt(BQ[p][:, group[1], :], bank_of(1), mask("strict_incl", 1), ALU.mult).then_inc(a_ready, 1)
            if chunks:
                dve_rc(dve, t - 1, 0)
            for z in range(2):
                own(tt(blocks(TBD, z), blocks(ABD, z), mask64("first", z), ALU.mult))
                own.settle()
                tt(TBD[:, group[z], :], TBD[:, group[z], :], ident.rearrange("p (o s) -> p o s", o=1)
                   .broadcast_to([P, NCH, P]), ALU.add).then_inc(t_ready, 1)
            tt(BQ[p][:, group[0], :], bank_of(7), mask("strict_incl", 0), ALU.mult).then_inc(a_ready, 1)
            for n in range(len(LEVELS)):
                step = chunks and n < NCH
                if step and n:
                    dve_rc(dve, t - 1, n)
                for z in range(2):
                    if z == 0 and step:
                        dve_uc(dve, t - 1, n)
                    dve.wait_ge(d_done, 10 * t + 2 * n + z + 1)
                    dve.wait_ge(t_ready, 12 * t + 2 * n + z + 1)
                    if n < len(LEVELS) - 1:
                        own(tt(TBD[:, group[z], :], TBD[:, group[z], :], bank_of(z), ALU.add))
                        q_bd = QBD[:, group[z], :, :].rearrange("p u h s -> p u (h s)")
                        tt(q_bd, q_bd, bank_of(2 + z), ALU.add).then_inc(t_ready, 1)
                    else:
                        q_bd = QBD[:, group[z], :, :].rearrange("p u h s -> p u (h s)")
                        tt(QF[:, group[z], :], q_bd, bank_of(2 + z), ALU.add).then_inc(t_ready, 1)
                if ahead and n == 0:
                    dve_prefix(dve, own, t + 1)
                if ahead and n == 1:
                    dve_kb(dve, own, t + 1)
                if n == 3:
                    if chunks:
                        dve_yt(dve, t - 1)
                    if ahead:
                        dve_alpha(dve, t + 1, q)
                    dve_bonus(dve, t)
                    if ahead:
                        dve_kappa(dve, own, t + 1)
                if ahead and n == 4:
                    dve_rb(dve, t + 1)

        def pool_mixes(pool):
            pool.wait_ge(hx_ready, 1)
            for n in range(2):
                for k in range(CT):
                    nc.gpsimd.tensor_scalar(XI[4 + n][:, k, :], XX[:, k, :], pcol("mu", MIXES[4 + n] * CT + k), None, ALU.mult)\
                        .then_inc(pool_own, 1)
                for k in range(CT):
                    pool.wait_ge(pool_own, n * CT + k + 1)
                    nc.gpsimd.tensor_tensor(XI[4 + n][:, k, :], XI[4 + n][:, k, :], H[:, k, 1:L + 1], ALU.add)\
                        .then_inc(xp_ready, 1)

        def pool_zeros(pool):
            pool.wait_ge(lo_ready, S_O)
            pool.wait_ge(xp_ready, 2 * CT)
            for a in (BEB, KAB, QBD, ALB[0], BTB[0]):
                nc.gpsimd.memset(a[:, :, :, :], 0.0)
            nc.gpsimd.memset(VB[:, :, :, :], 0.0).then_inc(zeros_ready, 1)
            pool.wait_ge(blocks_done, 3 * S_RKV + 28)
            nc.gpsimd.memset(ALB[1][:, :, :, :], 0.0)
            nc.gpsimd.memset(BTB[1][:, :, :, :], 0.0).then_inc(zeros_ready, 1)

        def pool_last(pool):
            pool.wait_ge(hi_ready, S_O + 2)
            pool.wait_ge(lo_ready, S_O + 1)
            slot = (S_O + 1) % 2
            nc.gpsimd.tensor_tensor(WL[:, slot, :], raw[:, slot, :], WH[:, slot, :].bitcast(fp32), ALU.subtract)\
                .then_inc(lo_ready, 1)

        def pool_operands(pool, t, part):
            g = nc.gpsimd.tensor_tensor
            if part == 0:
                pool.wait_ge(kd_ready, t + 1)
                pool.wait_ge(e_ready, 4 * t + 2)
                g(BE, BB, E3, ALU.mult).then_inc(be_ready, 1)
            else:
                if not (isinstance(t, int) and t == 0):
                    pool.wait_ge(bo_done, t)
                g(TMPK, KD[:, 0:L], KD[:, L:2 * L], ALU.add).then_inc(tm_ready, 1)
                pool.wait_ge(tm_ready, t + 1)
                g(KD, KD, E3, ALU.mult).then_inc(be_ready, 1)

        def pool_tile(pool, t, ahead):
            for n in range(1, len(LEVELS)):
                for z in range(2):
                    pool.wait_ge(z_done, 10 * t + 2 * (n - 1) + z + 1)
                    nc.gpsimd.tensor_tensor(blocks(XLV, z), blocks(ABD, z), mask64("level", z * len(LEVELS) + n), ALU.mult)\
                        .then_inc(xl_ready, 1)
                if ahead and n == 2:
                    pool_operands(pool, t + 1, 0)
                if ahead and n == 3:
                    pool_operands(pool, t + 1, 1)

        def act_mix1(act):
            s0 = S_RKV
            A = nc.scalar.activation
            act_root(act, 4, (st_ready, 2))

            def hi(i, k):
                if i < 4:
                    act.wait_ge(xi_ready, CT * i + k + 1)
                else:
                    act.wait_ge(xp_ready, CT * (i - 4) + k + 1)
                if i >= 2 and k == 0:
                    act.wait_ge(blocks_done, 3 * s0 + FIRST[i - 2] + OUTS[i - 2])
                A(PARTS[i % 2][0][:, k, :], XI[i][:, k, :], ACT.Copy).then_inc(mx_hh, 1)
            for k in range(CT):
                hi(0, k)
            for i in range(6):
                for m in range(OUTS[i]):
                    g = FIRST[i] + m
                    if g % 3 == 0 and s0 + g // 3 + 1 < S_O:
                        next_hi(act, s0 + g // 3 + 1)
                    act.wait_ge(blocks_done, 3 * s0 + g + 1)
                    src = UB[g % 3][:, 0:L]
                    if i < 3:
                        A((R, K, V)[i][:, m * L:(m + 1) * L], src, ACT.Copy).then_inc(rkv_ready, 1)
                        hi(i + 1, m)
                    elif i == 3:
                        A(HID[:, 0, :], src, ACT.Tanh).then_inc(rkv_ready, 1)
                        act.wait_ge(rkv_ready, g + 1)
                        A(PH[:, 0, :], HID[:, 0, :], ACT.Copy).then_inc(lr_hi, 1)
                    elif i == 4:
                        A(HID[:, 1, :], src, ACT.Copy).then_inc(rkv_ready, 1)
                        act.wait_ge(rkv_ready, g + 1)
                        A(PH[:, 1, :], HID[:, 1, :], ACT.Copy).then_inc(lr_hi, 1)
                    else:
                        act.wait_ge(lr_lo, m + 1)
                        A(HID[:, m, :], src, ACT.Sigmoid).then_inc(rkv_ready, 1)
                        act.wait_ge(rkv_ready, g + 1)
                        A(GH[:, m, :], HID[:, m, :], ACT.Copy).then_inc(lr_hi, 1)
                if i in (2, 3):
                    for k in range(CT):
                        hi(i + 2, k)
                if i == 3:
                    act.wait_ge(mx_hl, 4 * CT)
                    for j in range(CT):
                        A(KSQ[:, j, :], K[:, j * L:(j + 1) * L], ACT.Square, scale=pcol("k_k", j)).then_inc(kk_sq, 1)
                if i == 4:
                    act.wait_ge(kk_max, 1)
                    A(RN[:, 0, :], KSQ[0:16, 0, :], ACT.Sqrt).then_inc(kk_root, 1)
            act.wait_ge(mx_hl, 6 * CT)
            q = 0
            for i, dst in enumerate((LW, AG)):
                for m in range(CT):
                    for z in range(2):
                        if m == CT - 1 and z == 1:
                            act.wait_ge(blocks_done, 3 * (S_LORA + 1) + 2 + i)
                        else:
                            act.wait_ge(lr_done, q + 1 - i)
                        A(dst[:, (z * CT + m) * L:(z * CT + m + 1) * L], UB[q % 3][:, 0:L], ACT.Sigmoid,
                          bias=pcol(("w0", "a0")[i], z * CT + m)).then_inc(lr_ready, 1)
                        q += 1
            act.wait_ge(kk_ready, 1)
            act.wait_ge(zeros_ready, 1)
            for part in range(3):
                act_operands(act, 0, part)
            act_etot(act, 0, 0)
            act_beb(act, 0)
            act_alb(act, 0, 0)
            act.wait_ge(zeros_ready, 2)
            tiles(act, lambda t, p, c, a: act_tile(act, t, p, c, a))
            act.wait_ge(e_ready, 4 * CT)
            for i in range(NCH):
                act_s(act, CT - 1, 1, i)
                if i < 2:
                    act_squares_y(act, ((0, 1, 2, 3), (4, 5, 6))[i])
            next_hi(act, S_O)
            next_hi(act, S_O + 1)
            act_groupnorm(act)

        def dve_mix1(dve, own):
            V_ = nc.vector
            tt, ts, stt = V_.tensor_tensor, V_.tensor_scalar, V_.scalar_tensor_tensor
            dve_root(dve, 4)
            own(V_.memset(H[:, :, 0:1], 0.0))
            own(V_.memset(H[:, :, L + 1:L + 2], 0.0))
            dve.wait_ge(rstd_ready, 5)
            for k in range(CT):
                own(stt(out=H[:, k, 1:L + 1], in0=X[:, k, :], scalar=pcol("mix_norm", CT + k), in1=rstd[:, :],
                        op0=ALU.mult, op1=ALU.mult))
            own.settle()
            own(tt(XX[:, :, :], H[:, :, 0:L], H[:, :, 2:L + 2], ALU.add))
            own.settle()
            stt(out=XX[:, :, :], in0=XX[:, :, :], scalar=0.5, in1=H[:, :, 1:L + 1], op0=ALU.mult, op1=ALU.subtract)\
                .then_inc(hx_ready, 1)
            dve.wait_ge(hx_ready, 1)

            def mix(i):
                if i:
                    dve.wait_ge(mx_hl, CT * i)
                for k in range(CT):
                    stt(out=XI[i][:, k, :], in0=XX[:, k, :], scalar=pcol("mu", MIXES[i] * CT + k), in1=H[:, k, 1:L + 1],
                        op0=ALU.mult, op1=ALU.add).then_inc(xi_ready, 1)

            def lo(i, k):
                dve.wait_ge(mx_hh, CT * i + k + 1)
                tt(PARTS[i % 2][1][:, k, :], XI[i][:, k, :], PARTS[i % 2][0][:, k, :].bitcast(fp32), ALU.subtract)\
                    .then_inc(mx_hl, 1)
            mix(0)
            for k in range(CT):
                lo(0, k)
            mix(1)
            for i in range(6):
                for m in range(OUTS[i]):
                    g = FIRST[i] + m
                    if g % 3 == 0 and S_RKV + g // 3 + 1 < S_O:
                        next_lo(dve, S_RKV + g // 3 + 1)
                    if i >= 3:
                        dve.wait_ge(lr_hi, g - 23)
                        hi, lo_, o = (PH, PL, i - 3) if i < 5 else (GH, GL, m)
                        tt(lo_[:, o, :], HID[:, o, :], hi[:, o, :].bitcast(fp32), ALU.subtract).then_inc(lr_lo, 1)
                    else:
                        lo(i + 1, m)
                if i < 2:
                    mix(i + 2)
                if i in (2, 3):
                    for k in range(CT):
                        lo(i + 2, k)
                if i == 4:
                    dve.wait_ge(kk_ss, 1)
                    ts(KSQ[0:16, 0, :], ST[0:16, 0:L], 1e-24, None, ALU.max).then_inc(kk_max, 1)
                    dve.wait_ge(kk_root, 1)
                    V_.reciprocal(RN[:, 1, :], RN[:, 0, :]).then_inc(kk_rec, 1)
            own(ts(omk, par[:, COL["k_a"]:COL["k_a"] + CT], -1.0, 1.0, ALU.mult, ALU.add))
            for j in range(CT):
                dve.wait_ge(kk_bc, 2 * (j // 2) + 2)
                own(stt(out=KK[:, j * L:(j + 1) * L], in0=K[:, j * L:(j + 1) * L], scalar=pcol("k_k", j),
                        in1=DN[j // 2][:, (j % 2) * L:(j % 2) * L + L], op0=ALU.mult, op1=ALU.mult))
            own.settle()
            V_.memset(small[:, 36:37], 0.0).then_inc(yt_ready, 1)
            V_.memset(small[:, 37:38], 0.0).then_inc(kk_ready, 1)
            dve.wait_ge(lr_ready, 9)
            dve_prefix(dve, own, 0)
            dve.wait_ge(blocks_done, 3 * S_O)
            dve.wait_ge(zeros_ready, 1)
            dve_kb(dve, own, 0)
            dve_alpha(dve, 0, 0)
            dve_kappa(dve, own, 0)
            dve_rb(dve, 0)
            tiles(dve, lambda t, p, c, a: dve_tile(dve, t, p, c, a, own), own)
            for i in range(NCH):
                dve_rc(dve, CT - 1, i)
                if i == 0:
                    dve_center(dve, (0, 1))
                dve_uc(dve, CT - 1, i)
                if i < 2:
                    dve_center(dve, ((2, 3), (4, 5, 6))[i])
            next_lo(dve, S_O)
            dve_yt(dve, CT - 1)
            dve_groupnorm(dve, own)

        def ytile(j):
            return R[:, j * L:(j + 1) * L]

        def half_bank(bs, j):
            return bs[j // 2][:, (j % 2) * L:(j % 2) * L + L]
        MB = [bank[0], bank[1], bank[2], bank[3]]
        OB = [bank[6], bank[7], bank[4], bank[5]]
        YSQ = LW[:, 0:CT * L].rearrange("p (j t) -> p j t", t=L)

        def mean_bank(j):
            return half_bank(MB, j) if j < CT - 1 else bank[5][:, 0:L]

        def pe_mean(pe, js):
            for j in js:
                pe.wait_ge(yt_ready, j + 2)
                nc.tensor.matmul(mean_bank(j), blockones, ytile(j), start=True, stop=True).then_inc(gn_mean, 1)

        def pe_ss(pe, js):
            for j in js:
                pe.wait_ge(gn_sq, j + 1)
                last = nc.tensor.matmul(bank[7][0:16, 0:L], sel[:, j, :], YSQ[:, j, :], start=j == 0, stop=j == CT - 1)
            if js[-1] == CT - 1:
                last.then_inc(gn_ss, 1)

        def act_squares_y(act, js):
            for j in js:
                act.wait_ge(gn_c, j + 1)
                nc.scalar.activation(YSQ[:, j, :], ytile(j), ACT.Square).then_inc(gn_sq, 1)

        def dve_center(dve, js):
            for j in js:
                dve.wait_ge(gn_mean, min(2 * (j // 2) + 2, CT - 1) if j < CT - 1 else CT)
                nc.vector.scalar_tensor_tensor(out=ytile(j), in0=mean_bank(j), scalar=-1.0 / HD, in1=ytile(j),
                                               op0=ALU.mult, op1=ALU.add).then_inc(gn_c, 1)

        def pe_gate(pe, js):
            for j in js:
                pe.wait_ge(gn_c, min(2 * (j // 2) + 2, CT - 1))
                for i in range(2):
                    last = three(half_bank(MB, j), i * BLK + j * P, S_O % 2, GH[:, i, :], GL[:, i, :], i == 0, i == 1)
                    if j == CT - 1:
                        last.then_inc(blocks_done, 1)
                if j < CT - 1:
                    last.then_inc(g_done, 1)

        def pe_groupnorm(pe):
            pe.wait_ge(lo_ready, S_O + 1)
            pe_gate(pe, (0, 1, 2, 3))
            pe_mean(pe, (CT - 1,))
            pe_gate(pe, (4, 5))
            pe_ss(pe, (CT - 1,))
            pe_gate(pe, (6, 7))

            def spread_rstd(j):
                if j >= 2:
                    pe.wait_ge(gn_n, j - 1)
                nc.tensor.matmul(bank[4 + j % 2][:, 0:L], selt[:, j, :], RN[:, 1, :], start=True, stop=True).then_inc(gn_bc, 1)
            pe.wait_ge(gn_rec, 1)
            spread_rstd(0)
            spread_rstd(1)
            pe.wait_ge(lo_ready, S_O + 2)
            pe.wait_ge(gn_root, 1)
            for k in range(CT):
                if k + 2 < CT:
                    spread_rstd(k + 2)
                pe.wait_ge(mix_hl, CT + k + 1)
                for m in range(2):
                    g = m + 2
                    last = three(half_bank(OB, m), g % 3 * BLK + k * P, (S_O + g // 3) % 2, HH[:, k, :], HL[:, k, :],
                                 k == 0 and m == 0, k == CT - 1, skip_group_check=True)
                    if k == CT - 1:
                        last.then_inc(blocks_done, 1)
            for m in range(2, CT):
                g = m + 2
                s, b = S_O + g // 3, g % 3
                if b == 0:
                    pe.wait_ge(lo_ready, s + 1)
                if m == 4:
                    pe.wait_ge(gn_n, CT)
                for k in range(CT):
                    last = three(half_bank(OB, m), b * BLK + k * P, s % 2, HH[:, k, :], HL[:, k, :], k == 0, k == CT - 1)
                    if m == CT - 1 and k in (2, 5):
                        last.then_inc(blocks_done, 1)
                last.then_inc(blocks_done, 1)

        def act_groupnorm(act):
            A = nc.scalar.activation
            act.wait_ge(bo_read, CT)
            for j in range(CT):
                A(K[:, j * L:(j + 1) * L], K[:, j * L:(j + 1) * L], ACT.Identity, bias=pcol("ln_b", j)).then_inc(gn_af, 1)
            act_squares_y(act, (CT - 1,))
            act.wait_ge(gn_ss, 1)
            A(RN[:, 0, :], bank[7][0:16, 0:L], ACT.Sqrt, bias=eps6[0:16, 1:2], scale=1.0 / HD).then_inc(gn_root, 1)
            for j in range(CT):
                act_mixed(act, j, CT)
            for s in (2, 3, 4):
                next_hi(act, S_O + s)

        def dve_groupnorm(dve, own):
            tt, stt = nc.vector.tensor_tensor, nc.vector.scalar_tensor_tensor

            def gated(js):
                for j in js:
                    if j < CT - 2:
                        dve.wait_ge(g_done, 2 * (j // 2) + 2)
                    else:
                        dve.wait_ge(blocks_done, 3 * S_O + 2)
                    dve.wait_ge(gn_sq, j + 1)
                    dve.wait_ge(gn_af, j + 1)
                    k = K[:, j * L:(j + 1) * L]
                    own(tt(k, k, half_bank(MB, j), ALU.mult))
                    own(stt(out=ytile(j), in0=ytile(j), scalar=pcol("ln_w", j), in1=half_bank(MB, j), op0=ALU.mult,
                            op1=ALU.mult))
            dve_center(dve, (CT - 1,))
            gated((0, 1, 2))
            dve.wait_ge(gn_root, 1)
            nc.vector.reciprocal(RN[:, 1, :], RN[:, 0, :]).then_inc(gn_rec, 1)
            gated((3, 4))
            for j in range(CT + 1):
                if j in (1, 2, 3):
                    gated((j + 4,))
                if j < CT:
                    own.settle()
                    dve.wait_ge(gn_bc, j + 1)
                    tt(ytile(j), ytile(j), bank[4 + j % 2][:, 0:L], ALU.mult).then_inc(gn_n, 1)
                    if j >= 2:
                        dve.wait_ge(mix_hh, CT + j - 1)
                    dve.wait_ge(gn_n, j + 1)
                    tt(ymix[:, j % 2, :], ytile(j), K[:, j * L:(j + 1) * L], ALU.add).then_inc(ym_ready, 1)
                if j:
                    dve_mixed(dve, j - 1, CT)
            for s in (2, 3, 4):
                next_lo(dve, S_O + s)
            for part, (js, done) in enumerate((((0, 1), 6), ((2,), 8), ((3,), 12))):
                dve.wait_ge(blocks_done, 3 * S_O + done)
                for j in js:
                    last = tt(X[:, 2 * j:2 * j + 2, :], OB[j][:, :].rearrange("p (a n) -> p a n", a=2),
                              X[:, 2 * j:2 * j + 2, :], ALU.add)
                last.then_inc(x_ready, 1)
        @block.sync
        def _(sp):
            for dst, src in ((hcst, hconst_d), (fw, fw_d), (par[:, :], par_d), (cst[:, :], const_d), (X[:, :, :], xT)):
                sp.dma_start(dst, src).then_inc(loaded, 16)
            for s in range(2):
                sp.dma_start(raw[:, s, :], stream[s]).then_inc(raw_full[s], 16)

            def load(s, u):
                sp.dma_start(raw[:, u, :], stream[s]).then_inc(raw_full[u], 16)
            for first, end in ((2, min(S_O, STEPS)), (S_O, STEPS)):
                if first == S_O and end > first:
                    sp.wait_ge(t_ready, 12 * CT)
                n = (end - first) // 2
                if n <= 0:
                    continue
                with sp.Fori(0, n) as i:
                    for u in range(2):
                        sp.wait_ge(lo_ready, 2 * i + (first - 1 + u))
                        load(2 * i + (first + u), (first + u) % 2)
                for s in range(first + 2 * n, end):
                    sp.wait_ge(lo_ready, s - 1)
                    load(s, s % 2)
            sp.wait_ge(x_ready, 3 * len(NORM_TILES))
            sp.dma_start(out, X[:, :, :]).then_inc(stored, 16)
            sp.wait_ge(stored, 16)

        @block.tensor
        def _(pe):
            pe.wait_ge(loaded, LOADS)
            pe_filter(pe)
            pe_ffn(pe, 0, S_FFN[0], 0)
            pe_mix0(pe)
            pe_ffn(pe, 2, S_FFN[1], FT)
            pe_ffn(pe, 3, S_FFN[2], 2 * FT)
            pe_mix1(pe)
            pe_ffn(pe, 5, S_FFN[3], 3 * FT)

        @block.scalar
        def _(act):
            act.wait_ge(loaded, LOADS)
            act_filter(act)
            next_hi(act, 0)
            act_norm_in(act, 0, ("ffn1_norm", 0))
            act_ffn(act, 0, S_FFN[0], 0)
            act_norm_in(act, 1, ("mix_norm", 0))
            act_mix0(act)
            for s in (1, 2, 3):
                next_hi(act, S_OUT + s)
            act_norm_in(act, 2, ("ffn2_norm", 0))
            act_ffn(act, 2, S_FFN[1], FT)
            act_norm_in(act, 3, ("ffn1_norm", CT))
            act_ffn(act, 3, S_FFN[2], 2 * FT)
            act.wait_ge(x_ready, 12)
            act_squares(act)
            act_mix1(act)
            act_norm_in(act, 5, ("ffn2_norm", CT))
            act_ffn(act, 5, S_FFN[3], 3 * FT)

        @block.gpsimd
        def _(pool):
            pool_mixes(pool)
            pool_zeros(pool)
            pool.wait_ge(kk_ready, 1)
            for part in range(2):
                pool_operands(pool, 0, part)
            tiles(pool, lambda t, p, c, a: pool_tile(pool, t, a))
            pool_last(pool)

        @block.vector
        def _(dve):
            own = Own(dve, dve_own)
            nc.vector.memset(eps6[:, 0:1], 1e-6)
            nc.vector.memset(eps6[:, 1:2], 64e-5).then_inc(eps_ready, 1)
            dve.wait_ge(loaded, LOADS)
            dve_filter(dve, own)
            next_lo(dve, 0)
            dve_norm_in(dve, 0, ("ffn1_norm", 0))
            dve_ffn(dve, 0, S_FFN[0], 0)
            dve_residual(dve, S_FFN[0] + FT, 0.5)
            dve_norm_in(dve, 1, ("mix_norm", 0))
            dve_mix0(dve, own)
            for s in (1, 2, 3):
                next_lo(dve, S_OUT + s)
            dve_out(dve, S_OUT)
            dve_norm_in(dve, 2, ("ffn2_norm", 0))
            dve_ffn(dve, 2, S_FFN[1], FT)
            dve_residual(dve, S_FFN[1] + FT, 0.5)
            dve_norm_in(dve, 3, ("ffn1_norm", CT))
            dve_ffn(dve, 3, S_FFN[2], 2 * FT)
            dve_residual(dve, S_FFN[2] + FT, 0.5)
            dve_mix1(dve, own)
            dve_norm_in(dve, 5, ("ffn2_norm", CT))
            dve_ffn(dve, 5, S_FFN[3], 3 * FT)
            dve_residual(dve, S_FFN[3] + FT, 0.5)


def _consts():
    c = np.zeros((P, NCONST), np.float32)

    def put(name, a, off=0):
        c[:, CC[name] + off:CC[name] + off + a.shape[1]] = a
    r = np.arange(P)
    put("ident", np.eye(P))
    put("istack", np.tile(np.eye(CH), (2, 1)))
    put("blockones", (r[:, None] // HD == r[None, :] // HD) * 1.0)
    put("ones", np.ones((P, P)))
    for j in range(CT):
        put("sel", (np.arange(16)[None, :] == 2 * j + r[:, None] // HD) * 1.0, 16 * j)
        put("selt", (r[:, None] == 2 * j + r[None, :] // HD) * 1.0, P * j)
    put("perm", (r[:, None] == (r[None, :] + HD) % P) * 1.0)
    t, s = np.arange(CH)[:, None], np.arange(CH)[None, :]
    for z in range(2):
        pair = (t // 2 == s // 2) & ((t > s) if z == 0 else (t < s))
        before = (s < t) if z == 0 else (s > t)
        incl = np.tile((before | (s == t)).T * 1.0, (2, 1))
        put("first", np.tile(pair * 1.0, (2, 1)), z * CH)
        put("first_incl", np.concatenate([np.tile(pair.T * 1.0, (2, 1)), incl], 1), z * P)
        put("strict_incl", np.concatenate([np.tile(before.T * 1.0, (2, 1)), incl], 1), z * P)
        for n, b in enumerate(LEVELS):
            m = (t // (2 * b) == s // (2 * b)) & ((t // b > s // b) if z == 0 else (t // b < s // b))
            put("level", np.tile(m * 1.0, (2, 1)), (z * len(LEVELS) + n) * CH)
    put("reset", np.tile((np.arange(L) % CH != 0) * 1.0, (P, 1)))
    return c


def _hconsts():
    c = np.zeros((P, NHC), np.float32)

    def put(name, a):
        c[:, HC[name]:HC[name] + 2 * a.shape[1]] = a.reshape(2, P, -1).transpose(1, 0, 2).reshape(P, -1)
    t = np.arange(L, dtype=np.float64)
    theta = 2 * np.pi * (t + 0.5) / (2 * L)
    put("cos", np.cos(t[:, None] * theta[None, :]))
    put("sin", np.sin(t[:, None] * theta[None, :]))
    put("icos", np.cos(theta[:, None] * t[None, :]) / L)
    put("isin", np.sin(theta[:, None] * t[None, :]) / L)
    f32 = np.float32
    tt = (t.astype(f32) / f32(L - 1)).astype(f32)
    deltas = np.abs(np.linspace(math.log(1e-2) / 1.5, math.log(1e-2) / 0.3, 512).astype(f32))
    put("window", np.exp((-tt[:, None] * deltas[None, :]).astype(np.float64)))
    d = np.abs(t[:, None] - t[None, :])
    put("dist", np.where(d <= 128, d, 1e30))
    bands = (FILTER_EMB - 1) // 2
    freqs = np.linspace(1e-4, bands - 1, bands).astype(f32)
    ang = (f32(2.0 * math.pi / L) * t.astype(f32)[:, None] * freqs[None, :]).astype(np.float64)
    feat = np.concatenate([tt[:, None], np.cos(ang), -np.sin(ang)], axis=1)
    c[:FILTER_EMB, HC["feat"]:HC["feat"] + L] = feat.T
    return c


def _blocks(i):
    st = np.zeros((STEPS, P, 3, BLK), np.float32)

    def col(w, m, width=P):
        b = np.zeros((P, CT, P), np.float32)
        b[:, :, :width] = w[:, m * P:m * P + width].reshape(CT, P, width).transpose(1, 0, 2)
        return b.reshape(P, BLK)
    for n, (name, layer) in enumerate((("ffn1", 0), ("ffn2", 0), ("ffn1", 1), ("ffn2", 1))):
        g, u, d = (i[f"{name}_{k}"][layer] for k in ("wg", "wu", "wd"))
        for f in range(FT):
            st[S_FFN[n] + f, :, 0] = col(g, f)
            st[S_FFN[n] + f, :, 1] = col(u, f)
            st[S_FFN[n] + f + 1, :, 2 if f < FT - 1 else 0] = d[f * P:(f + 1) * P]

    def lay(s0, blocks):
        for k, b in enumerate(blocks):
            st[s0 + k // 3, :, k % 3] = b
    lay(S_IN, [col(i["ab_w_in"][0], m) for m in range(18)])
    lay(S_OUT, [col(i["ab_w_out"][0], m) for m in range(CT)])
    lay(S_RKV, [col(i[f"rw_w_{k}"][0], m) for k in "rkv" for m in range(CT)])
    both = lambda w: np.concatenate([w[0], w[1]], axis=-1)
    g1, g2 = i["rw_g1"][0], i["rw_g2"][0]
    g2b = np.zeros((P, C), np.float32)
    g2b[:LORA_G - P] = g2[P:]
    lay(S_LORA, [col(both(i["rw_w1"][0]), 0), col(both(i["rw_a1"][0]), 0), col(g1, 0),
                 col(g1, 1, LORA_G - P), i["rw_w2"][0].reshape(P, C), i["rw_a2"][0].reshape(P, C)])
    lay(S_O, [g2[:P], g2b] + [col(i["rw_w_o"][0], m) for m in range(CT)])
    return st.reshape(STEPS, P, 3 * BLK)


def _params(i):
    c = np.zeros((P, NPAR), np.float32)

    def put(name, a, off=0):
        a = a.reshape(-1, P).T
        c[:, COL[name] + off:COL[name] + off + a.shape[1]] = a
    for n in ("ffn1_norm", "mix_norm", "ffn2_norm"):
        put(n, i[n])
    put("conv_w", i["ab_conv_w"][0])
    put("conv_b", i["ab_conv_b"][0])
    put("hy_bias", i["hy_bias"][0])
    for n in ("mu", "w0", "a0", "k_k", "k_a", "r_k", "ln_w", "ln_b"):
        put(n, i["rw_" + n][0])
    c[:, COL["q_gain"]] = np.tile(i["attn_q_norm"][0], 2)
    c[:, COL["k_gain"]] = np.tile(i["attn_k_norm"][0], 2)
    c[:, COL["sink"]:COL["sink"] + NQ] = np.broadcast_to(i["attn_sink"][0], (P, NQ))
    for n in range(3):
        c[:FILTER_ORDER, COL["f_b"] + n] = i[f"hy_f{n + 1}_b"][0]
    c[:FILTER_ORDER, COL["freq"]] = i["hy_sin_freq"][0]
    return c


def _filter_weights(i):
    w = np.zeros((P, NFW), np.float32)
    w[:FILTER_EMB, :FILTER_ORDER] = i["hy_f1_w"][0]
    w[:FILTER_ORDER, FILTER_ORDER:2 * FILTER_ORDER] = i["hy_f2_w"][0]
    w[:FILTER_ORDER, 2 * FILTER_ORDER:3 * FILTER_ORDER] = i["hy_f3_w"][0]
    w[:FILTER_ORDER, 3 * FILTER_ORDER:] = i["hy_f4_w"][0]
    return w


def _channel_major(x):
    return np.ascontiguousarray(x.reshape(L, CT, P).transpose(2, 1, 0))


def _arrays(inputs):
    i = {k: np.asarray(v) for k, v in inputs.items()}
    return {"xT_in": _channel_major(i["x"][0]), "stream_in": _blocks(i), "par_in": _params(i), "const_in": _consts(),
            "hconst_in": _hconsts(), "fw_in": _filter_weights(i)}


def kernel(**inputs):
    import concourse.bacc as bacc
    from concourse.bass_utils import run_bass_kernel_spmd

    nc = bacc.Bacc("TRN2", target_bir_lowering=False, num_devices=1)
    arrays = _arrays(inputs)
    io = [nc.dram_tensor(n, a.shape, mybir.dt.float32, kind="ExternalInput").ap() for n, a in arrays.items()]
    io.append(nc.dram_tensor("out", (P, CT, L), mybir.dt.float32, kind="ExternalOutput").ap())
    build(nc, io)
    r = run_bass_kernel_spmd(nc, [arrays], core_ids=[0])
    y = np.asarray(r.results[0]["out"])
    return np.ascontiguousarray(y.transpose(2, 1, 0)).reshape(1, L, C)
```
